# Optimizing a Trainium2 kernel written in Bass

```python
import jax, jax.numpy as jnp
from jax import lax
import numpy as np

D_MODEL = 2048
BATCH = 1
SEQ = 256
DEPTH = 1

MIX_WIDTH = D_MODEL
POOL_WIDTH = MIX_WIDTH // 2
RWKV_WIDTH = MIX_WIDTH - POOL_WIDTH
POOL_WINDOWS = (2, 4, 8, 16)
N_POOL_GROUPS = len(POOL_WINDOWS)
POOL_GROUP = POOL_WIDTH // N_POOL_GROUPS
HEAD_SIZE = 64
N_RWKV_HEADS = RWKV_WIDTH // HEAD_SIZE
D_DECAY_LORA = 64
D_AAA_LORA = 64
D_MV_LORA = 32
D_GATE_LORA = 160
D_FF = 4 * D_MODEL
D_PLE = 256
NORM_EPS = 1e-6
GN_EPS = 64e-5
SHIFT_WIDTH = 3 * RWKV_WIDTH + D_DECAY_LORA + D_AAA_LORA + D_GATE_LORA
IN_WIDTH = POOL_WIDTH + SHIFT_WIDTH


def rms_norm(x, g):
    xf = x.astype(jnp.float32)
    y = xf * lax.rsqrt(jnp.mean(xf * xf, axis=-1, keepdims=True) + NORM_EPS)
    return (y * g.astype(jnp.float32)).astype(x.dtype)

def token_shift(z, mu):
    zf = z.astype(jnp.float32)
    z_prev = jnp.pad(zf, ((0, 0), (1, 0), (0, 0)))[:, :-1]
    return zf + (z_prev - zf) * mu.astype(jnp.float32)

def causal_multiscale_pool(u):
    B, T, _ = u.shape
    uf = u.astype(jnp.float32).reshape(B, T, N_POOL_GROUPS, POOL_GROUP)
    cs = jnp.cumsum(uf, axis=1)
    t = jnp.arange(T)
    outs = []
    for gi, win in enumerate(POOL_WINDOWS):
        c = cs[:, :, gi]
        lagged = jnp.pad(c, ((0, 0), (win, 0), (0, 0)))[:, :T]
        cnt = jnp.minimum(t + 1, win).astype(jnp.float32)[None, :, None]
        outs.append((c - lagged) / cnt - uf[:, :, gi])
    return jnp.stack(outs, axis=2)

def wkv7_scan(r, decay, k, v, a_vec, b_vec):
    B, T, H, N = r.shape
    xs = tuple(jnp.swapaxes(z, 0, 1) for z in (r, decay, k, v, a_vec, b_vec))

    def step(S, inp):
        r_t, w_t, k_t, v_t, a_t, b_t = inp
        sa = jnp.einsum('bhij,bhj->bhi', S, a_t)
        S = S * w_t[:, :, None, :] + sa[..., None] * b_t[:, :, None, :] + v_t[..., None] * k_t[:, :, None, :]
        y = jnp.einsum('bhij,bhj->bhi', S, r_t)
        return S, y

    S0 = jnp.zeros((B, H, N, N), jnp.float32)
    _, y = lax.scan(step, S0, xs)
    return jnp.swapaxes(y, 0, 1)

def rwkv7_time_mix(zr, zk, zv, zw, za, zg, zvr, v_first, w0, w_up, a0, a_up, g_up,
                   v0, v_up, k_k, k_a, r_k, gn_g, gn_b):
    f32 = jnp.float32
    B, T, _ = zr.shape
    H, N = N_RWKV_HEADS, HEAD_SIZE
    r = zr
    k = zk
    v = zv
    w = -jax.nn.softplus(-(w0.astype(f32) + jnp.tanh(zw) @ w_up.astype(f32))) - 0.5
    decay = jnp.exp(-jnp.exp(w))
    a = jax.nn.sigmoid(a0.astype(f32) + za @ a_up.astype(f32))
    g = jax.nn.sigmoid(zg) @ g_up.astype(f32)
    if zvr is None:
        v_first = v
    else:
        v = v + (v_first - v) * jax.nn.sigmoid(v0.astype(f32) + zvr @ v_up.astype(f32))
    hs = lambda z: z.reshape(B, T, H, N)
    kk = hs(k * k_k.astype(f32))
    kk = kk / jnp.maximum(jnp.linalg.norm(kk, axis=-1, keepdims=True), 1e-12)
    k = k * (1.0 + (a - 1.0) * k_a.astype(f32))
    r_h, k_h, v_h, a_h = hs(r), hs(k), hs(v), hs(a)
    y = wkv7_scan(r_h, hs(decay), k_h, v_h, -kk, kk * a_h)
    mu = jnp.mean(y, axis=-1, keepdims=True)
    var = jnp.mean(jnp.square(y - mu), axis=-1, keepdims=True)
    y = (y - mu) * lax.rsqrt(var + GN_EPS) * gn_g.astype(f32).reshape(H, N) + gn_b.astype(f32).reshape(H, N)
    y = y + jnp.sum(r_h * k_h * r_k.astype(f32), axis=-1, keepdims=True) * v_h
    return y.reshape(B, T, RWKV_WIDTH) * g, v_first

def first_inputs(seed: int = 0) -> dict:
    key = jax.random.key(seed)
    ks = iter(jax.random.split(key, 40))
    f32 = jnp.float32

    def nrm(shape, scale):
        return jax.random.normal(next(ks), shape, f32) * scale

    def unif(shape, lo, hi):
        return jax.random.uniform(next(ks), shape, f32, minval=lo, maxval=hi)

    L, Lm1, D, R = DEPTH, DEPTH - 1, D_MODEL, RWKV_WIDTH
    return {
        "x": nrm((BATCH, SEQ, D), 1.0),
        "p": nrm((DEPTH, BATCH, SEQ, D_PLE), 1.0),
        "attn_norm": 1.0 + nrm((L, D), 0.02),
        "w_in": nrm((L, D, IN_WIDTH), D ** -0.5),
        "mu_shift": unif((L, SHIFT_WIDTH), 0.0, 1.0),
        "w_vres_dn": nrm((Lm1, D, D_MV_LORA), D ** -0.5),
        "mu_vres": unif((Lm1, D_MV_LORA), 0.0, 1.0),
        "v0": nrm((Lm1, R), 0.5),
        "v_up": nrm((Lm1, D_MV_LORA, R), D_MV_LORA ** -0.5),
        "pool_w": nrm((L, N_POOL_GROUPS, POOL_GROUP, POOL_GROUP), POOL_GROUP ** -0.5),
        "pool_scale": 0.5 + nrm((L, POOL_WIDTH), 0.1),
        "w0": unif((L, R), -4.0, 1.0),
        "w_up": nrm((L, D_DECAY_LORA, R), D_DECAY_LORA ** -0.5),
        "a0": nrm((L, R), 0.3),
        "a_up": nrm((L, D_AAA_LORA, R), D_AAA_LORA ** -0.5),
        "g_up": nrm((L, D_GATE_LORA, R), D_GATE_LORA ** -0.5),
        "k_k": 0.85 + nrm((L, R), 0.05),
        "k_a": 1.0 + nrm((L, R), 0.05),
        "r_k": nrm((L, N_RWKV_HEADS, HEAD_SIZE), 0.1),
        "gn_g": 1.0 + nrm((L, R), 0.02),
        "gn_b": nrm((L, R), 0.02),
        "w_out": nrm((L, MIX_WIDTH, D), MIX_WIDTH ** -0.5),
        "mlp_norm": 1.0 + nrm((L, D), 0.02),
        "w_ffn_up": nrm((L, D, D_FF), D ** -0.5),
        "w_ffn_down": nrm((L, D_FF, D), D_FF ** -0.5),
        "ple_norm": 1.0 + nrm((L, D), 0.02),
        "w_ple_gate": nrm((L, D, D), D ** -0.5),
        "w_ple_proj": nrm((L, D_PLE, D), D_PLE ** -0.5),
        "final_norm": 1.0 + nrm((D,), 0.02),
    }

def first_block(x, p, attn_norm, w_in, mu_shift, w_vres_dn, mu_vres, v0, v_up, pool_w, pool_scale,
              w0, w_up, a0, a_up, g_up, k_k, k_a, r_k, gn_g, gn_b, w_out, mlp_norm, w_ffn_up,
              w_ffn_down, ple_norm, w_ple_gate, w_ple_proj, final_norm):
    B, T, _ = x.shape
    R = RWKV_WIDTH
    o_w = 3 * R
    o_a = o_w + D_DECAY_LORA
    o_g = o_a + D_AAA_LORA
    v_first = None
    for i in range(DEPTH):
        h = rms_norm(x, attn_norm[i])
        if i == 0:
            z = h @ w_in[0]
        else:
            z = h @ jnp.concatenate([w_in[i], w_vres_dn[i - 1]], axis=1)
        z_pool = z[..., :POOL_WIDTH]
        zs = token_shift(z[..., POOL_WIDTH:IN_WIDTH], mu_shift[i])
        zvr = None if i == 0 else token_shift(z[..., IN_WIDTH:], mu_vres[i - 1])

        d = causal_multiscale_pool(z_pool)
        pool_out = jnp.einsum('btgc,gcd->btgd', d, pool_w[i].astype(jnp.float32)).reshape(B, T, POOL_WIDTH)
        pool_out = pool_out * pool_scale[i].astype(jnp.float32)

        rwkv_out, v_first = rwkv7_time_mix(
            zs[..., :R], zs[..., R:2 * R], zs[..., 2 * R:o_w], zs[..., o_w:o_a], zs[..., o_a:o_g], zs[..., o_g:],
            zvr, v_first, w0[i], w_up[i], a0[i], a_up[i], g_up[i],
            None if i == 0 else v0[i - 1], None if i == 0 else v_up[i - 1],
            k_k[i], k_a[i], r_k[i], gn_g[i], gn_b[i])

        mix = jnp.concatenate([pool_out, rwkv_out], axis=-1).astype(x.dtype)
        x = x + mix @ w_out[i]

        h2 = rms_norm(x, mlp_norm[i])
        x = x + jnp.square(jax.nn.relu(h2 @ w_ffn_up[i])) @ w_ffn_down[i]

        gate = jax.nn.sigmoid(rms_norm(x, ple_norm[i]) @ w_ple_gate[i])
        x = x + gate * (p[i] @ w_ple_proj[i])
    return rms_norm(x, final_norm)


GLA_HEADS = 4
GLA_DK = D_MODEL // 16
GLA_DV = D_MODEL // 8
GLA_GATE_RANK = 16
GLA_GATE_TAU = 16.0
GLA_CHUNK = 64
CONV_WIDTH = 4

NSA_HEADS = 8
NSA_KV_HEADS = 2
NSA_GROUP = NSA_HEADS // NSA_KV_HEADS
NSA_HEAD_DIM = 128
CMP_BLOCK = 32
CMP_STRIDE = 16
CMP_HIDDEN = 128
SEL_BLOCK = 64
SEL_TOPK = 16
WINDOW = 512
Q_BLOCK = 128

D_FF_2 = -(-8 * D_MODEL // (3 * 256)) * 256
EPS = 1e-6
NEG = -1e30

GLA_QK = GLA_HEADS * GLA_DK
GLA_VW = GLA_HEADS * GLA_DV
GLA_QKV = 2 * GLA_QK + GLA_VW
NSA_QW = NSA_HEADS * NSA_HEAD_DIM
NSA_KVW = NSA_KV_HEADS * NSA_HEAD_DIM
MIX_WIDTH_2 = GLA_VW + NSA_QW
PROJ_SIZES = (GLA_QKV, GLA_GATE_RANK, GLA_VW, NSA_QW, NSA_KVW, NSA_KVW, NSA_KVW, NSA_KVW, NSA_KVW, NSA_KVW, 3 * NSA_HEADS)
PROJ_WIDTH = sum(PROJ_SIZES)


def rms_norm_2(u, g):
    uf = u.astype(jnp.float32)
    y = uf * lax.rsqrt(jnp.mean(uf * uf, axis=-1, keepdims=True) + EPS)
    return (y * g.astype(jnp.float32)).astype(u.dtype)

def causal_short_conv(u, w):
    s = u.shape[1]
    up = jnp.pad(u, ((0, 0), (CONV_WIDTH - 1, 0), (0, 0)))
    return sum(up[:, i:i + s] * w[i] for i in range(CONV_WIDTH))

def gla_mixer(q, k, v, gate_lr, out_gate, gate_w2, gate_b, norm_g):
    b_, s, _ = q.shape
    h, c = GLA_HEADS, GLA_CHUNK
    n_chunks = s // c
    log_a = jax.nn.log_sigmoid((gate_lr @ gate_w2 + gate_b).astype(jnp.float32)) / GLA_GATE_TAU

    def chunks(u, d):
        return u.reshape(b_, n_chunks, c, h, d).transpose(1, 0, 3, 2, 4)

    qc = chunks(q.astype(jnp.float32) * GLA_DK ** -0.5, GLA_DK)
    kc = chunks(k.astype(jnp.float32), GLA_DK)
    vc = chunks(v.astype(jnp.float32), GLA_DV)
    gc = chunks(log_a, GLA_DK)
    causal = jnp.tril(jnp.ones((c, c), dtype=bool))[:, :, None]

    def step(state, inp):
        qi, ki, vi, gi = inp
        b = jnp.cumsum(gi, axis=2)
        o_inter = jnp.einsum('bhtd,bhde->bhte', qi * jnp.exp(b), state)
        decay = jnp.exp(jnp.where(causal, b[:, :, :, None, :] - b[:, :, None, :, :], -jnp.inf))
        scores = jnp.einsum('bhtd,bhsd,bhtsd->bhts', qi, ki, decay)
        o_intra = jnp.einsum('bhts,bhse->bhte', scores, vi)
        b_last = b[:, :, -1:, :]
        state = (jnp.exp(b_last[:, :, 0, :])[..., None] * state
                 + jnp.einsum('bhsd,bhse->bhde', ki * jnp.exp(b_last - b), vi))
        return state, o_inter + o_intra

    state0 = jnp.zeros((b_, h, GLA_DK, GLA_DV), jnp.float32)
    _, o = lax.scan(step, state0, (qc, kc, vc, gc))
    o = o.transpose(1, 0, 3, 2, 4).reshape(b_, s, h, GLA_DV)
    o = rms_norm_2(o, norm_g) * jax.nn.silu(out_gate.astype(jnp.float32)).reshape(b_, s, h, GLA_DV)
    return o.reshape(b_, s, GLA_VW).astype(q.dtype)

def nsa_mixer(q, kc_raw, vc_raw, ks_raw, vs_raw, kw_raw, vw_raw, gate_logits,
              q_g, kc_g, ks_g, kw_g, k_pos, k_w1, k_w2, v_pos, v_w1, v_w2):
    b_, s, _ = q.shape
    hk, g, dh = NSA_KV_HEADS, NSA_GROUP, NSA_HEAD_DIM
    n_cmp = (s - CMP_BLOCK) // CMP_STRIDE + 1
    n_sel_blocks = s // SEL_BLOCK
    n_sel = min(SEL_TOPK, n_sel_blocks)
    scale = dh ** -0.5

    def heads(u, n):
        return u.reshape(b_, s, n, dh).transpose(0, 2, 1, 3)

    qh = rms_norm_2(heads(q, NSA_HEADS), q_g).reshape(b_, hk, g, s, dh)

    cmp_idx = jnp.arange(n_cmp)[:, None] * CMP_STRIDE + jnp.arange(CMP_BLOCK)[None, :]

    def compress(u, pos, w1, w2):
        blocks = u[:, :, cmp_idx] + pos
        flat = blocks.reshape(b_, hk, n_cmp, CMP_BLOCK * dh)
        return jax.nn.silu(flat @ w1) @ w2

    k_cmp = rms_norm_2(compress(heads(kc_raw, hk), k_pos, k_w1, k_w2), kc_g)
    v_cmp = compress(heads(vc_raw, hk), v_pos, v_w1, v_w2)
    cmp_end = jnp.arange(n_cmp) * CMP_STRIDE + CMP_BLOCK - 1

    c_start = jnp.arange(n_cmp)[:, None] * CMP_STRIDE
    s_start = jnp.arange(n_sel_blocks)[None, :] * SEL_BLOCK
    overlap = jnp.clip(jnp.minimum(c_start + CMP_BLOCK, s_start + SEL_BLOCK)
                       - jnp.maximum(c_start, s_start), 0, None).astype(jnp.float32) / CMP_STRIDE

    k_sel = rms_norm_2(heads(ks_raw, hk), ks_g).reshape(b_, hk, n_sel_blocks, SEL_BLOCK, dh)
    v_sel = heads(vs_raw, hk).reshape(b_, hk, n_sel_blocks, SEL_BLOCK, dh)
    win_pad = ((0, 0), (0, 0), (WINDOW, 0), (0, 0))
    k_win = jnp.pad(rms_norm_2(heads(kw_raw, hk), kw_g), win_pad)
    v_win = jnp.pad(heads(vw_raw, hk), win_pad)
    gates = jax.nn.sigmoid(gate_logits.astype(jnp.float32)).reshape(b_, s, hk, g, 3).transpose(0, 2, 3, 1, 4)

    gather_blocks = jax.vmap(jax.vmap(lambda blk, ix: blk[ix]))
    sel_offsets = jnp.arange(SEL_BLOCK)
    win_offsets = jnp.arange(WINDOW + Q_BLOCK)
    sel_ids = jnp.arange(n_sel_blocks)

    def query_block(s0):
        t = s0 + jnp.arange(Q_BLOCK)
        qb = lax.dynamic_slice_in_dim(qh, s0, Q_BLOCK, axis=3)

        sc = jnp.einsum('bhgqd,bhnd->bhgqn', qb, k_cmp).astype(jnp.float32) * scale
        mc = cmp_end[None, :] <= t[:, None]
        pc = jax.nn.softmax(jnp.where(mc, sc, NEG), axis=-1) * mc
        o_cmp = jnp.einsum('bhgqn,bhnd->bhgqd', pc.astype(v_cmp.dtype), v_cmp)

        imp = jnp.einsum('bhgqn,nj->bhqj', pc, overlap)
        jt = (t // SEL_BLOCK)[:, None]
        forced = (sel_ids == 0) | (sel_ids == jt) | (sel_ids == jt - 1)
        imp = jnp.where(sel_ids > jt, -jnp.inf, jnp.where(forced, jnp.inf, imp))
        _, idx = lax.top_k(imp, n_sel)
        ks = gather_blocks(k_sel, idx).reshape(b_, hk, Q_BLOCK, n_sel * SEL_BLOCK, dh)
        vs = gather_blocks(v_sel, idx).reshape(b_, hk, Q_BLOCK, n_sel * SEL_BLOCK, dh)
        kpos = (idx[..., None] * SEL_BLOCK + sel_offsets).reshape(b_, hk, Q_BLOCK, n_sel * SEL_BLOCK)
        ms = (kpos <= t[:, None])[:, :, None]
        ss = jnp.einsum('bhgqd,bhqkd->bhgqk', qb, ks).astype(jnp.float32) * scale
        ps = jax.nn.softmax(jnp.where(ms, ss, NEG), axis=-1)
        o_sel = jnp.einsum('bhgqk,bhqkd->bhgqd', ps.astype(vs.dtype), vs)

        kwb = lax.dynamic_slice_in_dim(k_win, s0, WINDOW + Q_BLOCK, axis=2)
        vwb = lax.dynamic_slice_in_dim(v_win, s0, WINDOW + Q_BLOCK, axis=2)
        wpos = s0 - WINDOW + win_offsets
        dist = t[:, None] - wpos[None, :]
        mw = (wpos[None, :] >= 0) & (dist >= 0) & (dist < WINDOW)
        sw = jnp.einsum('bhgqd,bhkd->bhgqk', qb, kwb).astype(jnp.float32) * scale
        pw = jax.nn.softmax(jnp.where(mw, sw, NEG), axis=-1)
        o_win = jnp.einsum('bhgqk,bhkd->bhgqd', pw.astype(vwb.dtype), vwb)

        gb = lax.dynamic_slice_in_dim(gates, s0, Q_BLOCK, axis=3)
        return gb[..., 0:1] * o_cmp + gb[..., 1:2] * o_sel + gb[..., 2:3] * o_win

    n_blocks = s // Q_BLOCK
    out = lax.map(query_block, jnp.arange(n_blocks) * Q_BLOCK)
    out = out.transpose(1, 0, 4, 2, 3, 5).reshape(b_, s, NSA_QW)
    return out.astype(q.dtype)

def hybrid_layer(x, attn_norm_g, w_in, gla_conv_w, gla_gate_w2, gla_gate_b, gla_norm_g,
                 nsa_q_norm_g, nsa_kc_norm_g, nsa_ks_norm_g, nsa_kw_norm_g,
                 cmp_k_pos, cmp_k_w1, cmp_k_w2, cmp_v_pos, cmp_v_w1, cmp_v_w2,
                 w_out, ffn_norm_g, w_gate, w_up, w_down):
    n = rms_norm_2(x, attn_norm_g)
    proj = n @ w_in
    offsets = np.cumsum(PROJ_SIZES)[:-1].tolist()
    (g_qkv, g_lr, g_out, nq, kc, vc, ks, vs, kw, vw, ng) = jnp.split(proj, offsets, axis=-1)
    g_qkv = jax.nn.silu(causal_short_conv(g_qkv, gla_conv_w))
    gq, gk, gv = jnp.split(g_qkv, [GLA_QK, 2 * GLA_QK], axis=-1)
    gla_out = gla_mixer(gq, gk, gv, g_lr, g_out, gla_gate_w2, gla_gate_b, gla_norm_g)
    nsa_out = nsa_mixer(nq, kc, vc, ks, vs, kw, vw, ng,
                        nsa_q_norm_g, nsa_kc_norm_g, nsa_ks_norm_g, nsa_kw_norm_g,
                        cmp_k_pos, cmp_k_w1, cmp_k_w2, cmp_v_pos, cmp_v_w1, cmp_v_w2)
    h = x + jnp.concatenate([gla_out, nsa_out], axis=-1) @ w_out
    m = rms_norm_2(h, ffn_norm_g)
    return h + (jax.nn.silu(m @ w_gate) * (m @ w_up)) @ w_down

def second_inputs(seed: int = 0) -> dict:
    key = jax.random.key(seed)
    ks = jax.random.split(key, 22)

    def dense(k, shape, fan_in):
        return jax.random.normal(k, shape, jnp.float32) * fan_in ** -0.5

    def gain(k, d):
        return 1.0 + 0.02 * jax.random.normal(k, (DEPTH, d), jnp.float32)

    dh = NSA_HEAD_DIM
    return {
        'x': jax.random.normal(ks[0], (BATCH, SEQ, D_MODEL), jnp.float32),
        'attn_norm_g': gain(ks[1], D_MODEL),
        'w_in': dense(ks[2], (DEPTH, D_MODEL, PROJ_WIDTH), D_MODEL),
        'gla_conv_w': dense(ks[3], (DEPTH, CONV_WIDTH, GLA_QKV), CONV_WIDTH),
        'gla_gate_w2': dense(ks[4], (DEPTH, GLA_GATE_RANK, GLA_QK), GLA_GATE_RANK),
        'gla_gate_b': 0.02 * jax.random.normal(ks[5], (DEPTH, GLA_QK), jnp.float32),
        'gla_norm_g': gain(ks[6], GLA_DV),
        'nsa_q_norm_g': gain(ks[7], dh),
        'nsa_kc_norm_g': gain(ks[8], dh),
        'nsa_ks_norm_g': gain(ks[9], dh),
        'nsa_kw_norm_g': gain(ks[10], dh),
        'cmp_k_pos': 0.1 * jax.random.normal(ks[11], (DEPTH, CMP_BLOCK, dh), jnp.float32),
        'cmp_k_w1': dense(ks[12], (DEPTH, CMP_BLOCK * dh, CMP_HIDDEN), CMP_BLOCK * dh),
        'cmp_k_w2': dense(ks[13], (DEPTH, CMP_HIDDEN, dh), CMP_HIDDEN),
        'cmp_v_pos': 0.1 * jax.random.normal(ks[14], (DEPTH, CMP_BLOCK, dh), jnp.float32),
        'cmp_v_w1': dense(ks[15], (DEPTH, CMP_BLOCK * dh, CMP_HIDDEN), CMP_BLOCK * dh),
        'cmp_v_w2': dense(ks[16], (DEPTH, CMP_HIDDEN, dh), CMP_HIDDEN),
        'w_out': dense(ks[17], (DEPTH, MIX_WIDTH_2, D_MODEL), MIX_WIDTH_2),
        'ffn_norm_g': gain(ks[18], D_MODEL),
        'w_gate': dense(ks[19], (DEPTH, D_MODEL, D_FF_2), D_MODEL),
        'w_up': dense(ks[20], (DEPTH, D_MODEL, D_FF_2), D_MODEL),
        'w_down': dense(ks[21], (DEPTH, D_FF_2, D_MODEL), D_FF_2),
    }

def second_block(x, attn_norm_g, w_in, gla_conv_w, gla_gate_w2, gla_gate_b, gla_norm_g,
              nsa_q_norm_g, nsa_kc_norm_g, nsa_ks_norm_g, nsa_kw_norm_g,
              cmp_k_pos, cmp_k_w1, cmp_k_w2, cmp_v_pos, cmp_v_w1, cmp_v_w2,
              w_out, ffn_norm_g, w_gate, w_up, w_down):
    for l in range(DEPTH):
        x = hybrid_layer(x, attn_norm_g[l], w_in[l], gla_conv_w[l], gla_gate_w2[l], gla_gate_b[l],
                         gla_norm_g[l], nsa_q_norm_g[l], nsa_kc_norm_g[l], nsa_ks_norm_g[l],
                         nsa_kw_norm_g[l], cmp_k_pos[l], cmp_k_w1[l], cmp_k_w2[l], cmp_v_pos[l],
                         cmp_v_w1[l], cmp_v_w2[l], w_out[l], ffn_norm_g[l], w_gate[l], w_up[l],
                         w_down[l])
    return x


def setup_inputs(seed=0):
    out = dict(first_inputs(seed))
    for name, value in second_inputs(seed + 1).items():
        if name != "x":
            out[name + "_2"] = value
    return out


def reference(
    x, p, attn_norm, w_in, mu_shift, w_vres_dn, mu_vres, v0, v_up, pool_w, pool_scale, w0, w_up,
    a0, a_up, g_up, k_k, k_a, r_k, gn_g, gn_b, w_out, mlp_norm, w_ffn_up, w_ffn_down, ple_norm,
    w_ple_gate, w_ple_proj, final_norm, attn_norm_g_2, w_in_2, gla_conv_w_2, gla_gate_w2_2,
    gla_gate_b_2, gla_norm_g_2, nsa_q_norm_g_2, nsa_kc_norm_g_2, nsa_ks_norm_g_2,
    nsa_kw_norm_g_2, cmp_k_pos_2, cmp_k_w1_2, cmp_k_w2_2, cmp_v_pos_2, cmp_v_w1_2, cmp_v_w2_2,
    w_out_2, ffn_norm_g_2, w_gate_2, w_up_2, w_down_2,
):
    x = first_block(
        x, p, attn_norm, w_in, mu_shift, w_vres_dn, mu_vres, v0, v_up, pool_w, pool_scale, w0,
        w_up, a0, a_up, g_up, k_k, k_a, r_k, gn_g, gn_b, w_out, mlp_norm, w_ffn_up, w_ffn_down,
        ple_norm, w_ple_gate, w_ple_proj, final_norm,
    )
    return second_block(
        x, attn_norm_g_2, w_in_2, gla_conv_w_2, gla_gate_w2_2, gla_gate_b_2, gla_norm_g_2,
        nsa_q_norm_g_2, nsa_kc_norm_g_2, nsa_ks_norm_g_2, nsa_kw_norm_g_2, cmp_k_pos_2,
        cmp_k_w1_2, cmp_k_w2_2, cmp_v_pos_2, cmp_v_w1_2, cmp_v_w2_2, w_out_2, ffn_norm_g_2,
        w_gate_2, w_up_2, w_down_2,
    )


_drawn_inputs = setup_inputs


def setup_inputs(seed=0):
    import zlib

    import numpy as np

    out = dict(_drawn_inputs(seed))
    spreads = {}
    factors = {'attn_norm': 3.089,
     'k_k': 6.054,
     'gn_g': 6.863,
     'gn_b': 6.575,
     'mlp_norm': 2.685,
     'ple_norm': 174.383,
     'attn_norm_g_2': 4.241,
     'gla_gate_w2_2': 3.24,
     'gla_gate_b_2': 64.0,
     'gla_norm_g_2': 6.719,
     'nsa_q_norm_g_2': 8.0,
     'nsa_kc_norm_g_2': 200.0,
     'nsa_ks_norm_g_2': 26.646,
     'nsa_kw_norm_g_2': 23.585,
     'cmp_k_pos_2': 8.0,
     'cmp_v_pos_2': 22.983,
     'ffn_norm_g_2': 12.669}
    for name, (base, spread) in spreads.items():
        noise = np.random.default_rng([zlib.crc32(name.encode()), seed]).standard_normal(out[name].shape)
        drawn = base * np.exp(spread * noise) if base else spread * noise
        out[name] = __import__('jax').numpy.asarray(drawn.astype(out[name].dtype))
    for name, factor in factors.items():
        out[name] = (out[name] * factor).astype(out[name].dtype)
    return out
```

```python
from contextlib import ExitStack

import numpy as np

import concourse.bass as bass
from concourse import mybir

F32 = mybir.dt.float32
ALU = mybir.AluOpType
ACT = mybir.ActivationFunctionType
AX = mybir.AxisListType.X

P = 128
T = 256
TT = T // P
D = 2048
KT = D // P
CW = 512
FF1 = 8192
FF2 = 5632
EPS = 1e-6
RW = 1024
HM = RW // P
C = 64
NCH = T // C
KAPPA = float(np.exp(-0.5))
GN_EPS = 64e-5
LEVELS = (2, 4, 8, 16, 32)
GH, GDK, GDV = 4, 128, 256
GTAU = 16.0
GLA_HALF = (32, 16, 8, 4, 2, 1)
NH, KVH, DH = 8, 2, 128
GRP = NH // KVH
CB, CST = 32, 16
NB = (T - CB) // CST + 1
NEG = -1e30


def constants():
    p = np.arange(P)[:, None]
    q = p % C
    j = np.arange(C)[None, :]
    c = {}
    c["ident"] = np.eye(P)
    c["tri"] = np.concatenate([q < j, q <= j], 1)
    c["levels"] = np.concatenate([((q // b) % 2 == 1) & (j // b == q // b - 1) for b in LEVELS], 1)
    c["level1"] = (j % 2 == 1) & (q == j - 1)
    c["eye64"] = q == j
    c["headones"] = (p // C) == (np.arange(P)[None, :] // C)
    c["ones"] = np.ones((P, P))
    c["keep"] = np.broadcast_to(np.arange(T)[None, :] % C != 0, (P, T))
    t16 = np.arange(16)
    c["invcnt"] = np.broadcast_to(
        np.concatenate([1.0 / np.minimum(t16 + 1, w) for w in (2, 4, 8, 16)])[None, :], (P, 64))
    s = np.arange(P)[None, :]
    c["causal"] = np.concatenate([np.zeros((P, P)), np.where(s > p, NEG, 0.0)], 1)
    end = np.arange(NB)[None, :] * CST + CB - 1
    seen = np.concatenate([end <= p + P * t for t in range(TT)], 1)
    c["cmpseen"] = seen
    c["cmpbias"] = np.where(seen, 0.0, NEG)
    c["glamask"] = GDK ** -0.5 * np.concatenate(
        [((q // w) % 2 == 0) & (j // w == q // w + 1) for w in GLA_HALF] + [q == j], 1)
    return {k: np.asarray(v, np.float32) for k, v in c.items()}


CONST_AT = {}


def pack_constants():
    parts, at = constants(), 0
    for k, v in parts.items():
        CONST_AT[k] = (at, v.shape[1])
        at += v.shape[1]
    return np.ascontiguousarray(np.concatenate(list(parts.values()), 1))


ROWS = [[("attn_norm", 16), ("mlp_norm", 16), ("ple_norm", 16), ("attn_norm_g_2", 16), ("ffn_norm_g_2", 16),
         ("mu_shift", 26), ("mu_tail", 1), ("pool_scale", 8), ("w0", 8)],
        [("a0", 8), ("k_k", 8), ("k_a", 8), ("r_k", 8), ("gla_conv_w_2", 64), ("gla_gate_b_2", 4),
         ("gla_norm_g_2", 2), ("nsa_q_norm_g_2", 1), ("nsa_kc_norm_g_2", 1), ("nsa_ks_norm_g_2", 1),
         ("nsa_kw_norm_g_2", 1), ("gn_g", 8), ("gn_b", 8)]]
COL = {}
for _t, _rows in enumerate(ROWS):
    _at = P * _t
    for _n, _r in _rows:
        COL[_n] = _at
        _at += _r
    assert _at <= P * (_t + 1)


SIGNALS = """
    w_used const_loaded zeroed rows_loaded norm_xn waup_loaded gup_loaded y_ready x_loaded cmpv_loaded n5_dve
    out_stored norm_turned rows_turned z_copied wa_ready head_sums kk_squared lw_ready ga_ready rkr_ready
    kk_root bk_ready bonus_ready bk_copied bk_turned score_masked score_ready pool_ready pool_sums dt_ready
    d_turned d_ready d_added dt_added f_ready pool_out f_masked df_ready dft_ready v_ready v_turned v_placed
    at_placed s_placed0 s_placed1 zc_ready zc_copied u_ready u_placed0 u_placed1 s_ready y_copied yn_ready
    yn_turned mix_step n2_act ffn1_step ptok_loaded p_turned p_copied pproj_loaded n3_act n3_dve proj_ready
    sw_loaded low_rank n4_act lr_copied gw2_loaded silu_qk lb_in ng_copied level_ready gsc_masked gsc_ready
    gqk_ready gk_turned gv_ready gv_turned gsc_summed gkv_copied gs_step go_ready gs_ready on_ready on_turned
    pos_loaded pos_turned xc_ready pos_copied nsq_ready k_sums hid_ready cmp_ready kc_squared nk_ready on_read
    cs_read cs_ready sc_read sc_ready vcmp_copied att_out pt_copied prob_ready pt_ready pt_used n5_act act_step
    norm_sum0 norm_mean norm_root x0_loaded x1_loaded wag_shifted lc_ready exp_ready sd_ready bonus_done gn_var
    gn_root fin_done la_soft conv_qk conv_v gd_ready gexp_ready level_diff level_exp gout_ready o_copied k_var
    k_root max_ready exp_done dve_step ar_ready ple_mul fing_loaded glamask_loaded pool_step n1_dve n1_act
    n2_dve n4_dve w_loaded0 w_loaded1
"""


def build(nc, inp, consts, out):
    ctx = ExitStack()

    def sbuf(name, shape):
        return ctx.enter_context(nc.sbuf_tensor(name, shape, F32))

    xs = sbuf("xs", [P, TT, D])
    actT = sbuf("actT", [P, KT, T])
    ring = sbuf("ring", [P, 2, KT * CW])
    GLAMASK_AT = CONST_AT["glamask"][0]
    cst = sbuf("cst", [P, GLAMASK_AT])
    pcol = sbuf("pcol", [P, 2 * P])
    small = sbuf("small", [P, 64])
    NA = 26560
    arena = sbuf("arena", [P, NA])
    PS = ctx.enter_context(nc.psum_tensor("PS", [P, 8, 512], F32))

    S = {n: ctx.enter_context(nc.semaphore(n)) for n in SIGNALS.split()}

    def con(name):
        at, n = CONST_AT[name]
        return cst[:, at:at + n]

    def col(name, i=0):
        return pcol[:, COL[name] + i:COL[name] + i + 1]

    def split(v, dims):
        if len(dims) == 2:
            return v.rearrange("p (a b) -> p a b", a=dims[0])
        if len(dims) == 3:
            return v.rearrange("p (a b c) -> p a b c", a=dims[0], b=dims[1])
        if len(dims) == 4:
            return v.rearrange("p (a b c d) -> p a b c d", a=dims[0], b=dims[1], c=dims[2])
        return v

    def area(at, *dims):
        n = int(np.prod(dims))
        assert at + n <= NA, (at, dims)
        return split(arena[:, at:at + n], dims)

    def over(ap, n):
        return ap.unsqueeze(1).broadcast_to([ap.shape[0], n, ap.shape[1]])

    def along(ap, n):
        return ap.unsqueeze(len(ap.shape)).broadcast_to(list(ap.shape) + [n])

    ident, tri, eye64 = con("ident"), con("tri"), con("eye64")
    pair = [PS[:, 0:2, :], PS[:, 2:4, :]]

    def half(g):
        return pair[g].rearrange("p b (f t) -> p (b f) t", f=2)

    def slot(s):
        return ring[:, s, :].rearrange("p (k n) -> p k n", k=KT)

    LO, HI = slice(0, C), slice(C, P)
    HALF = [LO, HI]

    ss, ms, sq, rs = (small[:, 2 * i:2 * i + 2] for i in range(4))
    gnm, gnv, gns = (small[:, 8 + 16 * i:24 + 16 * i] for i in range(3))

    ZW = T + 1
    Z = area(0, 27, ZW)
    zr, zk, zv = (Z[:, 8 * i:8 * i + 8, 1:ZW] for i in range(3))
    B = 27 * ZW
    tmp1, tmp2, lw, ga, kk = (area(B + 2048 * i, HM, T) for i in range(5))
    AR_AT = B + 5 * 2048
    AR = area(AR_AT, HM, NCH, P)
    BK = area(AR_AT + 4096, HM, NCH, P)
    SD_AT = AR_AT + 8192
    PEND = area(SD_AT + 512, HM, NCH)
    ZSB = area(SD_AT + 544, HM, C)
    prow = area(AR_AT + 4096, 2, P)
    G = area(B, HM, 2, NCH, P)
    DTi = area(AR_AT + 4096, HM, NCH, C)
    Di = area(AR_AT + 6144, HM, NCH, C)
    Fi = area(B + 4 * 2048, HM, NCH, C)
    UVa = [area(AR_AT + 6144, 2, HM, 2, C), area(B + 4 * 2048, 2, HM, 2, C)]

    def UV(c):
        return UVa[c // 2][:, c % 2]

    def BKtok(c):
        if c < 2:
            v = actT[:, 8 + 4 * c:12 + 4 * c, :].rearrange("p a b -> p (a b)")
        else:
            v = area(8 * ZW + (c - 2) * 1024, 1024)
        return v.rearrange("p (m j) -> p m j", m=HM)

    bonus = zr
    Ytok = area(16 * ZW, TT, RW)
    xflat = xs[:, :, :].rearrange("p a b -> p (a b)")
    waup = xflat[:, 0:RW]
    PW = T + 16
    ZP = xflat[:, RW:RW + HM * PW].rearrange("p (m t) -> p m t", m=HM)
    PB = [xflat[:, RW + HM * PW + i * PW:RW + HM * PW + (i + 1) * PW] for i in range(2)]
    SD = [xflat[:, 3072 + 512 * i:3584 + 512 * i].rearrange("p (m i) -> p m i", m=HM) for i in range(2)]
    xn = area(AR_AT, TT, D)
    poolw = ring[:, 1, 0:2048].rearrange("p (q n) -> p q n", q=8)
    gup, gup2 = ring[:, 1, 2048:3072], ring[0:32, 1, 3072:4096]

    HT1 = area(0, FF1 // P, T)
    pproj = area(4096, 2, D)
    ptok = area(AR_AT + 4096, TT, 256)
    pT = area(16384, 2, T)
    gate_sb = area(0, TT, CW)
    fing = area(2048, D)

    GC = 16 * (T + 3)
    ZG = area(0, 16, T + 3)
    CV = area(GC, 16, T)
    LB = area(GC + 4096, GH, T)
    Q1, K4 = area(GC + 5120, GH, T), area(GC + 8192, GH, T)
    WD = [area(GC + 6144 + 1024 * i, GH, T) for i in range(2)]
    KTOK = area(GC + 9216, TT, GH, GDK)
    SCT = area(GC + 10240, GH, TT, C)
    GS = area(GC + 10752, GH, GDV)
    OT = area(GC + 11776, TT, RW)
    GN_AT = GC + 13824
    GOQ = area(GN_AT, 16, T)
    NK = area(GN_AT + 4096, 8, T)
    VSW = area(GN_AT + 6144, 2, TT, 256)
    SW = area(GN_AT + 7168, KT, 40)
    LR = area(GN_AT + 7808, T)[0:16]
    GW2 = area(GN_AT + 8064, 512)[0:16]
    GE = [area(1024 * i, GH, T) for i in range(2)]
    glamask, SCTMP = area(2048, len(GLA_HALF) + 1, C), area(3072, 512)
    GDEC = small[:, 8:8 + GH * NCH].rearrange("p (h c) -> p h c", h=GH)
    VTOK = area(GC + 2048, TT, RW)
    gates = area(GN_AT + 7168, TT, 24)
    XC = [area(992 * i, CB, 31) for i in range(2)]
    CW2 = [area(1984 + 128 * i, P) for i in range(2)]
    PTAB = [area(2240 + 128 * i, P)[0:CB] for i in range(2)]
    HB = [area(2496 + 2 * i, 2) for i in range(2)]
    HID = [area(2500 + 30 * i, 2 * NB) for i in range(2)]
    KCMP = area(2560, 2 * NB)
    KCSQ = area(2590, 2 * NB)
    QKG = area(2620, 3)
    QRS, RSP = area(2623, TT, NH), area(2639, TT, NH)
    VCMP = area(2656, KVH, DH)[0:NB]
    SQ = area(2912, 12, T)
    PCM = area(5984, TT, NH, NB)
    PSW = [area(6224, 2, NH, P), area(8272, 2, NH, T)]
    PTR = [area(12368 + 512 * i, 512) for i in range(4)]
    PTC = [area(14416 + 512 * i, 512)[0:NB] for i in range(4)]
    MX, SM, WT = (area(16464 + 48 * i, TT, 3, NH) for i in range(3))
    HT2 = area(0, FF2 // P, T)
    up_gate = area(FF2 // P * T, 4, T)

    W = {n: a[0] if n not in ("final_norm", "x", "p") else a for n, a in inp.items()}
    xin, xout = (a.rearrange("o (t p) d -> p (o t) d", p=P) for a in (inp["x"], out))

    def wcols(name, c0, n=CW, k0=0, nk=KT):
        return W[name].rearrange("(k p) n -> p k n", p=P)[:, k0:k0 + nk, c0:c0 + n]

    N_WAG, N_RKV, N_POOL, N_SMALL, N_OUT, N_UP, N_DOWN, N_GATE = 0, 1, 7, 9, 10, 14, 30, 46
    N_GLA, N_GOQ, N_KCVC, N_KSVS, N_KWVW, N_CMP, N_OUT2, N_GU, N_DOWN2 = 50, 54, 58, 59, 60, 61, 62, 66, 88
    KD2 = FF2 // P // 4

    NORMS = {"n1": 0, "n2": 1, "n3": 2, "n4": 3, "n5": 4}
    RMS = {"n1": 1, "n2": 2, "n3": 3, "fin": 4, "n4": 5, "n5": 6}

    block = ctx.enter_context(nc.Block())

    @block.sync
    def _(sp):
        def load(n, dst, src, rest=()):
            if n >= 2:
                sp.wait_ge(S["w_used"], n - 1)
            sp.dma_start(dst, src).then_inc(S[f"w_loaded{n % 2}"], 16)

        def load_loop(first, count, name, c0, step_i, step_j=CW):
            with sp.Fori(0, count // 2) as i:
                for j in range(2):
                    n = first + j
                    sp.wait_ge(S["w_used"], i * 2 + (n - 1))
                    src = W[name].rearrange("(k p) n -> p k n", p=P)[:, :, bass.ds(i * step_i + (c0 + j * step_j), CW)]
                    sp.dma_start(slot(n % 2), src).then_inc(S[f"w_loaded{n % 2}"], 16)

        sp.dma_start(cst[:], consts[:, 0:GLAMASK_AT]).then_inc(S["const_loaded"], 16)
        sp.wait_ge(S["zeroed"], 1)
        for t, rows in enumerate(ROWS):
            at = 0
            for name, n in rows:
                dst = prow[at:at + n, t, :]
                if name == "mu_shift":
                    src = W["mu_shift"][0:26 * P].rearrange("(r c) -> r c", c=P)
                elif name == "mu_tail":
                    dst, src = prow[at:at + 1, t, 0:32], W["mu_shift"][26 * P:].unsqueeze(0)
                elif name == "r_k":
                    src = W["r_k"].rearrange("(r e) c -> r (e c)", e=2)
                elif name == "gla_conv_w_2":
                    src = W[name].rearrange("w (r c) -> (w r) c", c=P)
                else:
                    src = W[name].rearrange("(r c) -> r c", c=P)
                sp.dma_start(dst, src).then_inc(S["rows_loaded"], 16)
                at += n
        load(0, slot(0)[:, :, 0:288], wcols("w_in", 4096, 288))
        load(1, slot(1), wcols("w_in", 1024))
        load(2, slot(0), wcols("w_in", 1536))
        sp.wait_ge(S["norm_xn"], 2)
        sp.dma_start(waup[LO], W["w_up"]).then_inc(S["waup_loaded"], 16)
        sp.dma_start(waup[HI], W["a_up"]).then_inc(S["waup_loaded"], 16)
        for n in range(3, 7):
            load(n, slot(n % 2), wcols("w_in", 512 + 512 * n))
        for n in range(7, 9):
            load(n, slot(n % 2), wcols("w_in", 512 * (n - 7)))
        load(9, poolw, W["pool_w"].rearrange("g (k p) n -> p (g k) n", p=P))
        sp.dma_start(gup, W["g_up"][0:P]).then_inc(S["gup_loaded"], 16)
        sp.dma_start(gup2, W["g_up"][P:]).then_inc(S["gup_loaded"], 16)
        load(10, slot(0), wcols("w_out", 0))
        sp.wait_ge(S["y_ready"], NCH)
        sp.dma_start(xs[:], xin).then_inc(S["x_loaded"], 16)
        for n in range(11, 14):
            load(n, slot(n % 2), wcols("w_out", 512 * (n - 10)))
        load_loop(N_UP, 16, "w_ffn_up", 0, 2 * CW)
        with sp.Fori(0, 4) as i:
            for q in range(4):
                n = N_DOWN + q
                sp.wait_ge(S["w_used"], i * 4 + (n - 1))
                src = wcols("w_ffn_down", 0, D, 16 * q, 16)[:, :, bass.ds(i * CW, CW)]
                sp.dma_start(slot(n % 2), src).then_inc(S[f"w_loaded{n % 2}"], 16)
        load_loop(N_GATE, 4, "w_ple_gate", 0, 2 * CW)
        load_loop(N_GLA, 4, "w_in_2", 0, 2 * CW)
        load_loop(N_GOQ, 4, "w_in_2", 2064, 2 * CW)
        for n in range(N_KCVC, N_CMP):
            load(n, slot(n % 2), wcols("w_in_2", 4112 + CW * (n - N_KCVC)))
        cw = slot(N_CMP % 2).rearrange("p k n -> p (k n)").rearrange("p (s l h) -> p s l h", s=2, l=CB)
        load(N_CMP, cw[:, 0], W["cmp_k_w1_2"].rearrange("(l d) h -> d l h", d=DH))
        sp.dma_start(cw[:, 1], W["cmp_v_w1_2"].rearrange("(l d) h -> d l h", d=DH)).then_inc(S["cmpv_loaded"], 16)
        load_loop(N_OUT2, 4, "w_out_2", 0, 2 * CW)
        with sp.Fori(0, FF2 // CW) as i:
            for j, name in enumerate(("w_gate_2", "w_up_2")):
                n = N_GU + j
                sp.wait_ge(S["w_used"], i * 2 + (n - 1))
                src = W[name].rearrange("(k p) n -> p k n", p=P)[:, :, bass.ds(i * CW, CW)]
                sp.dma_start(slot(n % 2), src).then_inc(S[f"w_loaded{n % 2}"], 16)
        with sp.Fori(0, 4) as i:
            for q in range(4):
                n = N_DOWN2 + q
                sp.wait_ge(S["w_used"], i * 4 + (n - 1))
                src = wcols("w_down_2", 0, D, KD2 * q, KD2)[:, :, bass.ds(i * CW, CW)]
                sp.dma_start(slot(n % 2)[:, 0:KD2], src).then_inc(S[f"w_loaded{n % 2}"], 16)
        sp.wait_ge(S["n5_dve"], 4 + FF2 // CW + 4)
        sp.dma_start(xout, xs[:]).then_inc(S["out_stored"], 16)
        sp.wait_ge(S["out_stored"], 16)

    @block.tensor
    def _(pe):
        def loaded(n, i=None, per=1):
            v = 16 * (n // 2 + 1)
            pe.wait_ge(S[f"w_loaded{n % 2}"], v if i is None else i * (16 * per) + v)

        def rows_out(n, dst, m, k_tiles=KT, f0=0):
            for k in range(k_tiles):
                mm = pe.matmul(dst, slot(n % 2)[:, k, f0:f0 + m], actT[:, k, :], start=(k == 0), stop=(k == k_tiles - 1))
            return mm

        def chunk_rows(n, g, tiles=4):
            for f in range(tiles):
                mm = rows_out(n, half(g)[:, f, :], P, f0=f * P)
            return mm

        def chunk_tokens(n, g):
            for t in range(TT):
                for k in range(KT):
                    mm = pe.matmul(pair[g][:, t, :], actT[:, k, t * P:(t + 1) * P], slot(n % 2)[:, k, :],
                                   start=(k == 0), stop=(k == KT - 1))
            return mm

        def norm(p):
            pe.wait_ge(S["norm_xn"], TT * (NORMS[p] + 1))
            for j in range(KT // 2):
                if j >= 4:
                    pe.wait_ge(S[f"{p}_dve" if j % 2 == 0 else f"{p}_act"], (j - 4) // 2 + 1)
                for q in range(2):
                    for t in range(TT):
                        k = 2 * j + q
                        mm = pe.transpose(PS[:, 4 + j % 4, q * T + t * P:q * T + (t + 1) * P],
                                          xn[:, t, k * P:(k + 1) * P], ident)
                mm.then_inc(S["norm_turned"], 1)
            pe.wait_ge(S[f"{p}_dve"], 4)
            pe.wait_ge(S[f"{p}_act"], 4)

        pe.wait_ge(S["const_loaded"], 16)
        pe.wait_ge(S["rows_loaded"], 16 * sum(len(r) for r in ROWS))
        for t in range(2):
            mm = pe.transpose(PS[:, 0, t * P:(t + 1) * P], prow[:, t, :], ident)
        mm.then_inc(S["rows_turned"], 1)

        norm("n1")
        pe.wait_ge(S["z_copied"], 1)
        loaded(0)
        for f in range(2):
            rows_out(0, half(0)[:, f, :], P, f0=f * P)
        rows_out(0, half(0)[0:32, 2, :], 32, f0=2 * P).then_inc(S["w_used"], 1)
        with pe.Fori(0, 3) as i:
            for j in range(2):
                n = N_RKV + j
                loaded(n, i)
                pe.wait_ge(S["z_copied"], i * 2 + n)
                chunk_rows(n, n % 2).then_inc(S["w_used"], 1)
        pe.wait_ge(S["waup_loaded"], 32)
        pe.wait_ge(S["wa_ready"], 2)
        for m in range(HM):
            mm = pe.matmul(PS[:, 4 + m // 2, m % 2 * T:(m % 2 + 1) * T], waup[LO, m * P:(m + 1) * P],
                           Z[LO, 24, 1:ZW], start=True, stop=True)
        mm.then_inc(S["head_sums"], 1)
        pe.wait_ge(S["z_copied"], 8)
        for m in range(HM):
            mm = pe.matmul(PS[:, m // 2, m % 2 * T:(m % 2 + 1) * T], waup[HI, m * P:(m + 1) * P],
                           Z[HI, 24, 1:ZW], start=True, stop=True)
        mm.then_inc(S["head_sums"], 1)
        pe.wait_ge(S["kk_squared"], 1)
        pe.wait_ge(S["lw_ready"], 1)
        for m in range(HM):
            mm = pe.matmul(PS[:, 4 + m // 2, m % 2 * T:(m % 2 + 1) * T], con("headones"), tmp2[:, m, :],
                           start=True, stop=True)
        mm.then_inc(S["head_sums"], 1)
        pe.wait_ge(S["ga_ready"], 1)
        for n in range(N_POOL, N_POOL + 2):
            loaded(n)
            chunk_rows(n, n % 2).then_inc(S["w_used"], 1)
        pe.wait_ge(S["rkr_ready"], 1)
        pe.wait_ge(S["kk_root"], 1)
        for m in range(HM):
            mm = pe.matmul(PS[:, 4 + m // 2, m % 2 * T:(m % 2 + 1) * T], con("headones"), tmp1[:, m, :],
                           start=True, stop=True)
        mm.then_inc(S["head_sums"], 1)
        pe.wait_ge(S["bk_ready"], 1)
        pe.wait_ge(S["bonus_ready"], 1)
        for g in range(2 * NCH):
            c, m0 = g // 2, g % 2 * 4
            if g >= 4:
                pe.wait_ge(S["bk_copied"], g - 3)
            for m in range(4):
                mm = pe.transpose(PS[:, 4 + g % 4, m * P:(m + 1) * P], BK[:, m0 + m, c, :], ident)
            mm.then_inc(S["bk_turned"], 1)
        pe.wait_ge(S["z_copied"], 10)
        for g in range(2 * HM):
            m, e = g // 2, g % 2
            if g >= 4:
                pe.wait_ge(S["score_masked"], g - 3)
            for c in range(NCH):
                mm = pe.matmul(PS[:, g % 4, c * P:(c + 1) * P], BK[HALF[e], m, c, :], AR[HALF[e], m, c, :],
                               start=True, stop=True)
            mm.then_inc(S["score_ready"], 1)
        loaded(N_SMALL)
        pe.wait_ge(S["pool_ready"], 1)
        pe.wait_ge(S["bk_copied"], 8)
        for m in range(HM):
            for k in range(2):
                g = m // 2
                mm = pe.matmul(PS[:, 4 + m // 2, m % 2 * T:(m % 2 + 1) * T],
                               poolw[:, 2 * g + k, m % 2 * P:(m % 2 + 1) * P], ZP[:, 2 * g + k, 16:PW],
                               start=(k == 0), stop=(k == 1))
        mm.then_inc(S["pool_sums"], 1)
        pe.wait_ge(S["dt_ready"], 1)

        def inverse_group(g, bank, lhs, rhs):
            for m in range(2 * g, 2 * g + 2):
                for c in range(NCH):
                    for e in range(2):
                        h = HALF[e]
                        at = (m % 2 * NCH + c) * C
                        mm = pe.matmul(PS[h, bank, at:at + C], lhs(h, m, c, e), rhs(h, m, c, e), start=True, stop=True)
            return mm

        for g in range(4):
            inverse_group(g, g, lambda h, m, c, e: DTi[h, m, c, :], lambda h, m, c, e: eye64[h]).then_inc(S["d_turned"], 1)
        for lv in range(len(LEVELS)):
            last = lv == len(LEVELS) - 1
            for g in range(4):
                if lv == 0:
                    pe.wait_ge(S["d_ready"], g + 1)
                else:
                    pe.wait_ge(S["d_added"], 4 * (lv - 1) + g + 1)
                    pe.wait_ge(S["dt_added"], 4 * (lv - 1) + g + 1)
                inverse_group(g, g, lambda h, m, c, e: G[h, m, e, c, 0:C], lambda h, m, c, e: Di[h, m, c, :])\
                    .then_inc(S["f_ready"], 1)
            if lv == 0:
                pe.wait_ge(S["pool_out"], 1)
            for g in range(4):
                pe.wait_ge(S["f_masked"], 4 * lv + g + 1)
                if not last:
                    inverse_group(g, 4 + g, lambda h, m, c, e: DTi[h, m, c, :], lambda h, m, c, e: Fi[h, m, c, :])\
                        .then_inc(S["df_ready"], 1)
                inverse_group(g, g, lambda h, m, c, e: Fi[h, m, c, :], lambda h, m, c, e: DTi[h, m, c, :])\
                    .then_inc(S["dft_ready"], 1)
        pe.wait_ge(S["dt_added"], 4 * len(LEVELS))
        pe.wait_ge(S["v_ready"], 1)
        for c in range(NCH):
            for m in range(HM):
                for e in range(2):
                    mm = pe.matmul(PS[HALF[1 - e], 4 + c, m * C:(m + 1) * C], zv[HALF[e], m, c * C:(c + 1) * C],
                                   eye64[HALF[e]], start=True, stop=True)
            mm.then_inc(S["v_turned"], 1)
        pe.wait_ge(S["v_placed"], NCH)
        pe.wait_ge(S["at_placed"], 2)
        for c in range(NCH):
            pe.wait_ge(S["s_placed0"], c + 1)
            pe.wait_ge(S["s_placed1"], c + 1)
            for m in range(HM):
                for e in range(2):
                    mm = pe.matmul(PS[HALF[e], 0, m * C:(m + 1) * C], G[:, m, e, c, 0:C], UV(c)[:, m, e, :],
                                   start=True, stop=True)
            mm.then_inc(S["zc_ready"], 1)
            pe.wait_ge(S["zc_copied"], c + 1)
            for m in range(HM):
                for e in range(2):
                    mm = pe.matmul(PS[HALF[e], 1, m * C:(m + 1) * C], DTi[HALF[e], m, c, :], ZSB[HALF[e], m, :],
                                   start=True, stop=True)
            mm.then_inc(S["u_ready"], 1)
            pe.wait_ge(S["u_placed0"], c + 1)
            pe.wait_ge(S["u_placed1"], c + 1)
            if c < NCH - 1:
                for m in range(HM):
                    for e in range(2):
                        mm = pe.matmul(PS[HALF[e], 2, m * C:(m + 1) * C], BKtok(c)[:, m, e * C:(e + 1) * C],
                                       UV(c)[:, m, e, :], start=True, stop=True)
                mm.then_inc(S["s_ready"], 1)
            for m in range(HM):
                for e in range(2):
                    y = PS[HALF[c % 2], 4 + 2 * (c // 2) + e, m * C:(m + 1) * C]
                    pe.matmul(y, AR[HALF[e], m, c, C:P], SD[c % 2][HALF[e], m, :], start=True, stop=False)
                    mm = pe.matmul(y, G[:, m, e, c, C:P], UV(c)[:, m, e, :], start=False, stop=True)
            mm.then_inc(S["y_ready"], 1)
        pe.wait_ge(S["gup_loaded"], 32)
        for m in range(HM):
            dst = PS[:, m // 2, m % 2 * T:(m % 2 + 1) * T]
            pe.matmul(dst, gup[:, m * P:(m + 1) * P], Z[:, 25, 1:ZW], start=True, stop=False)
            mm = pe.matmul(dst, gup2[:, m * P:(m + 1) * P], Z[0:32, 26, 1:ZW], start=False, stop=True)
        mm.then_inc(S["w_used"], 1)
        pe.wait_ge(S["y_copied"], 2)
        for t in range(TT):
            pe.wait_ge(S["yn_ready"], t + 1)
            for m in range(HM):
                at = m % 2 * T + t * P
                mm = pe.transpose(PS[:, 4 + m // 2, at:at + P], Ytok[:, t, m * P:(m + 1) * P], ident)
        mm.then_inc(S["yn_turned"], 1)

        pe.wait_ge(S["mix_step"], 2)
        with pe.Fori(0, 2) as i:
            for j in range(2):
                n = N_OUT + j
                loaded(n, i)
                pe.wait_ge(S["mix_step"], i * 2 + (j + 1))
                chunk_tokens(n, j).then_inc(S["w_used"], 1)
        norm("n2")
        with pe.Fori(0, 8) as i:
            for j in range(2):
                n = N_UP + j
                loaded(n, i)
                pe.wait_ge(S["n2_act"], i * 2 + (j + 3))
                chunk_rows(n, j).then_inc(S["w_used"], 1)
        pe.wait_ge(S["ffn1_step"], 16)
        with pe.Fori(0, 2) as i:
            for g in range(2):
                pe.wait_ge(S["ffn1_step"], i * 2 + (g + 15))
                for q in range(4):
                    n = N_DOWN + 4 * g + q
                    loaded(n, i, 4)
                    for t in range(TT):
                        for k in range(KT):
                            mm = pe.matmul(pair[g][:, t, :], HT1[:, KT * q + k, t * P:(t + 1) * P], slot(n % 2)[:, k, :],
                                           start=(q == 0 and k == 0), stop=(q == 3 and k == KT - 1))
                    mm.then_inc(S["w_used"], 1)
        pe.wait_ge(S["ptok_loaded"], 16)
        for t in range(TT):
            for k in range(2):
                mm = pe.transpose(PS[:, 4, k * T + t * P:k * T + (t + 1) * P], ptok[:, t, k * P:(k + 1) * P], ident)
        mm.then_inc(S["p_turned"], 1)
        pe.wait_ge(S["p_copied"], 1)
        norm("n3")
        pe.wait_ge(S["pproj_loaded"], 16)
        with pe.Fori(0, 2) as i:
            for j in range(2):
                n = N_GATE + j
                loaded(n, i)
                pe.wait_ge(S["n3_act"], i * 2 + (j + 4))
                chunk_tokens(n, 0).then_inc(S["w_used"], 1)
                pe.wait_ge(S["n3_dve"], i * 2 + (j + 4))
                for t in range(TT):
                    for k in range(2):
                        mm = pe.matmul(pair[1][:, t, :], pT[:, k, t * P:(t + 1) * P],
                                       pproj[:, k, bass.ds(i * (2 * CW) + j * CW, CW)], start=(k == 0), stop=(k == 1))
                mm.then_inc(S["proj_ready"], 1)

        norm("n4")
        pe.wait_ge(S["sw_loaded"], 32)
        for k in range(KT):
            mm = pe.matmul(PS[0:16, 4, 0:T], SW[:, k, 0:16], actT[:, k, :], start=(k == 0), stop=(k == KT - 1))
        mm.then_inc(S["low_rank"], 1)
        for t in range(TT):
            for k in range(KT):
                mm = pe.matmul(PS[:, 5, t * 24:t * 24 + 24], actT[:, k, t * P:(t + 1) * P], SW[:, k, 16:40],
                               start=(k == 0), stop=(k == KT - 1))
        mm.then_inc(S["low_rank"], 1)
        with pe.Fori(0, 2) as i:
            for j in range(2):
                n = N_GLA + j
                loaded(n, i)
                pe.wait_ge(S["n4_act"], i * 2 + (j + 3))
                chunk_rows(n, j).then_inc(S["w_used"], 1)
        pe.wait_ge(S["lr_copied"], 1)
        pe.wait_ge(S["gw2_loaded"], 16)
        for h in range(GH):
            mm = pe.matmul(PS[:, 6 + h // 2, h % 2 * T:(h % 2 + 1) * T], GW2[:, h * P:(h + 1) * P], LR, start=True, stop=True)
        mm.then_inc(S["low_rank"], 1)
        with pe.Fori(0, 2) as i:
            for j in range(2):
                n = N_GOQ + j
                loaded(n, i)
                pe.wait_ge(S["n4_act"], i * 2 + (j + 7))
                chunk_rows(n, j).then_inc(S["w_used"], 1)
        def gla_scores(n):
            lhs, rhs = (CV[:, 4:8, :], CV[:, 0:4, :]) if n == 0 else (WD[(n - 1) % 2],) * 2
            if n == 0:
                pe.wait_ge(S["silu_qk"], 1)
                pe.wait_ge(S["lb_in"], 1)
                pe.wait_ge(S["ng_copied"], 1)
            else:
                pe.wait_ge(S["level_ready"], n)
            if n >= 4:
                pe.wait_ge(S["gsc_masked"], n - 3)
            for c in range(NCH):
                for h in range(GH):
                    at = (h * TT + c // 2) * C
                    mm = pe.matmul(PS[HALF[c % 2], 4 + n % 4, at:at + C], lhs[:, h, c * C:(c + 1) * C],
                                   rhs[:, h, c * C:(c + 1) * C], start=True, stop=True)
            mm.then_inc(S["gsc_ready"], 1)

        for n in range(3):
            gla_scores(n)
        loaded(N_KCVC)
        pe.wait_ge(S["n4_act"], 11)
        chunk_rows(N_KCVC, 0).then_inc(S["w_used"], 1)
        for n in (N_KSVS, N_KWVW):
            g = n % 2
            gla_scores(3 + 2 * (n - N_KSVS))
            gla_scores(4 + 2 * (n - N_KSVS))
            loaded(n)
            pe.wait_ge(S["n4_act"], 12 + n - N_KSVS)
            chunk_rows(n, g, 2)
            for t in range(TT):
                for k in range(KT):
                    mm = pe.matmul(pair[g][:, 1, t * T:(t + 1) * T], actT[:, k, t * P:(t + 1) * P],
                                   slot(n % 2)[:, k, 256:512], start=(k == 0), stop=(k == KT - 1))
            mm.then_inc(S["w_used"], 1)
        pe.wait_ge(S["gqk_ready"], 1)
        pe.wait_ge(S["gsc_masked"], len(GLA_HALF) + 1)
        for t in range(TT):
            for h in range(GH):
                mm = pe.transpose(PS[:, 6 + t, h * P:(h + 1) * P], K4[:, h, t * P:(t + 1) * P], ident)
        mm.then_inc(S["gk_turned"], 1)
        pe.wait_ge(S["gv_ready"], 1)
        pe.wait_ge(S["n4_act"], 15)
        for t in range(TT):
            for m in range(8):
                mm = pe.transpose(PS[:, 2 * t + m // 4, m % 4 * P:(m % 4 + 1) * P], CV[:, 8 + m, t * P:(t + 1) * P], ident)
        mm.then_inc(S["gv_turned"], 1)
        pe.wait_ge(S["gsc_summed"], len(GLA_HALF))
        pe.wait_ge(S["gkv_copied"], 3)
        for c in range(NCH):
            t, hf = c // 2, HALF[c % 2]
            if c:
                pe.wait_ge(S["gs_step"], GH * c)
            for h in range(GH):
                o = PS[hf, 2 * t + h // 2, h % 2 * GDV:(h % 2 + 1) * GDV]
                if c:
                    pe.matmul(o, Q1[:, h, c * C:(c + 1) * C], GS[:, h, :], start=True, stop=False)
                mm = pe.matmul(o, SCT[hf, h, t, :], VTOK[hf, t, h * GDV:(h + 1) * GDV], start=(c == 0), stop=True)
            mm.then_inc(S["go_ready"], 1)
            if c < NCH - 1:
                for h in range(GH):
                    mm = pe.matmul(PS[:, 6 + h // 2, h % 2 * GDV:(h % 2 + 1) * GDV], KTOK[hf, t, h, :],
                                   VTOK[hf, t, h * GDV:(h + 1) * GDV], start=True, stop=True)
                mm.then_inc(S["gs_ready"], 1)
        pe.wait_ge(S["gs_step"], GH * (NCH - 1))
        for t in range(TT):
            pe.wait_ge(S["on_ready"], t + 1)
            for m in range(8):
                at = m % 2 * T + t * P
                mm = pe.transpose(PS[:, 4 + m // 2, at:at + P], OT[:, t, m * P:(m + 1) * P], ident)
        mm.then_inc(S["on_turned"], 1)
        pe.wait_ge(S["pos_loaded"], 64)
        for i in range(2):
            mm = pe.transpose(PS[:, 0, i * CB:(i + 1) * CB], PTAB[i], ident[0:CB, 0:CB])
        mm.then_inc(S["pos_turned"], 1)
        loaded(N_CMP)
        pe.wait_ge(S["cmpv_loaded"], 16)
        cw = slot(N_CMP % 2).rearrange("p k n -> p (k n)").rearrange("p (s l h) -> p s l h", s=2, l=CB)
        pe.wait_ge(S["xc_ready"], 1)
        pe.wait_ge(S["pos_copied"], 2)
        for i in range(2):
            for l in range(CB):
                mm = pe.matmul(PS[:, 1, i * 31:(i + 1) * 31], cw[:, i, l, :], XC[i][:, l, :], start=(l == 0), stop=(l == CB - 1))
        mm.then_inc(S["w_used"], 1)
        pe.wait_ge(S["nsq_ready"], 1)
        for t in range(TT):
            for h in range(NH):
                mm = pe.matmul(PS[:, 2, t * NH + h:t * NH + h + 1], SQ[:, h, t * P:(t + 1) * P], con("ones")[:, 0:1],
                               start=True, stop=True)
        for i in range(2):
            mm = pe.matmul(PS[:, 3, :] if i else PS[:, 0, :], con("ones"), SQ[:, 8 + 2 * i:10 + 2 * i, :].rearrange("p a b -> p (a b)"),
                           start=True, stop=True)
        mm.then_inc(S["k_sums"], 1)
        pe.wait_ge(S["hid_ready"], 2)
        pe.matmul(PS[:, 1, 0:2 * NB], CW2[0], HID[0], start=True, stop=True)
        for kv in range(KVH):
            mm = pe.matmul(PS[0:NB, 1, P + kv * DH:P + (kv + 1) * DH], HID[1][:, kv * NB:(kv + 1) * NB], CW2[1], start=True, stop=True)
        mm.then_inc(S["cmp_ready"], 1)
        pe.wait_ge(S["kc_squared"], 1)
        pe.matmul(PS[:, 2, 0:2 * NB], con("ones"), KCSQ, start=True, stop=True).then_inc(S["k_sums"], 1)
        pe.wait_ge(S["nk_ready"], 3)
        pe.wait_ge(S["on_read"], 2)
        for t in range(TT):
            if t:
                pe.wait_ge(S["cs_read"], 1)
            for h in range(NH):
                mm = pe.matmul(PS[:, 2, h * NB:(h + 1) * NB], GOQ[:, 8 + h, t * P:(t + 1) * P],
                               KCMP[:, h // GRP * NB:(h // GRP + 1) * NB], start=True, stop=True)
            mm.then_inc(S["cs_ready"], 1)
            nk = (t + 1) * P
            for s in range(2):
                for h in range(NH):
                    u = (t * 2 + s) * NH + h
                    if u >= 4:
                        pe.wait_ge(S["sc_read"], u - 3)
                    pe.matmul(PS[:, 4 + u % 4, 0:nk], GOQ[:, 8 + h, t * P:(t + 1) * P], NK[:, 4 + 2 * s + h // GRP, 0:nk],
                              start=True, stop=True).then_inc(S["sc_ready"], 1)
        pe.wait_ge(S["sc_read"], 32)
        pe.wait_ge(S["vcmp_copied"], 1)
        g = 0
        for t in range(TT):
            for kv in range(KVH):
                o = PS[:, kv, :]
                if t:
                    pe.wait_ge(S["att_out"], kv + 1)
                parts = [(2, 0)] + [(s, kt) for s in range(2) for kt in range(t + 1)]
                for q, (s, kt) in enumerate(parts):
                    if g >= 4:
                        pe.wait_ge(S["pt_copied"], g - 3)
                    pe.wait_ge(S["prob_ready"], t * 3 + s + 1)
                    for j in range(GRP):
                        h = kv * GRP + j
                        if s == 2:
                            mm = pe.transpose(PS[0:NB, 4 + g % 4, j * P:(j + 1) * P], PCM[:, t, h, :], ident)
                        else:
                            mm = pe.transpose(PS[:, 4 + g % 4, j * P:(j + 1) * P], PSW[t][:, s, h, kt * P:(kt + 1) * P], ident)
                    mm.then_inc(S["pt_ready"], 1)
                    g += 1
                g -= len(parts)
                for q, (s, kt) in enumerate(parts):
                    pe.wait_ge(S["pt_copied"], g + 1)
                    if s == 2:
                        mm = pe.matmul(o, VCMP[:, kv, :], PTC[g % 4], start=True, stop=False)
                    else:
                        mm = pe.matmul(o, VSW[:, s, kt, kv * DH:(kv + 1) * DH], PTR[g % 4], start=False, stop=(q == len(parts) - 1))
                    mm.then_inc(S["pt_used"], 1)
                    g += 1

        pe.wait_ge(S["att_out"], TT * KVH)
        with pe.Fori(0, 2) as i:
            for j in range(2):
                n = N_OUT2 + j
                loaded(n, i)
                pe.wait_ge(S["on_read"], i * 2 + (j + 1))
                chunk_tokens(n, j).then_inc(S["w_used"], 1)
        norm("n5")
        with pe.Fori(0, FF2 // CW) as i:
            loaded(N_GU, i)
            pe.wait_ge(S["n5_act"], i + 4)
            chunk_rows(N_GU, 0).then_inc(S["w_used"], 1)
            loaded(N_GU + 1, i)
            pe.wait_ge(S["n5_dve"], i + 4)
            chunk_rows(N_GU + 1, 1).then_inc(S["w_used"], 1)
        done = 4 + FF2 // CW
        pe.wait_ge(S["n5_dve"], done)
        with pe.Fori(0, 2) as i:
            for g in range(2):
                pe.wait_ge(S["n5_dve"], i * 2 + (done + g - 1))
                for q in range(4):
                    n = N_DOWN2 + 4 * g + q
                    loaded(n, i, 4)
                    for t in range(TT):
                        for k in range(KD2):
                            mm = pe.matmul(pair[g][:, t, :], HT2[:, KD2 * q + k, t * P:(t + 1) * P], slot(n % 2)[:, k, :],
                                           start=(q == 0 and k == 0), stop=(q == 3 and k == KD2 - 1))
                    mm.then_inc(S["w_used"], 1)

    @block.scalar
    def _(act):
        steps = [0]

        def link(ins):
            steps[0] += 1
            ins.then_inc(S["act_step"], 1)
            act.wait_ge(S["act_step"], steps[0])

        def copy(dst, src, scale=1.0):
            return act.activation(dst, src, ACT.Copy, scale=scale)

        def square_sum(p):
            act.activation(xn[:, 0, :], xs[:, 0, :], ACT.Square, accum_out=ss[:, 0:1]).then_inc(S["norm_sum0"], 1)

        def root(p):
            act.wait_ge(S["norm_mean"], RMS[p])
            act.activation(sq, ms, ACT.Sqrt).then_inc(S["norm_root"], 1)

        def norm(p, gain):
            square_sum(p)
            root(p)
            for j in range(1, KT // 2, 2):
                act.wait_ge(S["norm_turned"], KT // 2 * NORMS[p] + j + 1)
                for q in range(2):
                    k = 2 * j + q
                    ins = copy(actT[:, k, :], PS[:, 4 + j % 4, q * T:(q + 1) * T], col(gain, k))
                ins.then_inc(S[f"{p}_act"], 1)

        act.dma_start(xs[:, 0, :], xin[:, 0, :]).then_inc(S["x0_loaded"], 16)
        act.dma_start(xs[:, 1, :], xin[:, 1, :]).then_inc(S["x1_loaded"], 16)
        act.wait_ge(S["rows_turned"], 1)
        copy(pcol[:], PS[:, 0, 0:2 * P]).then_inc(S["z_copied"], 1)
        act.wait_ge(S["z_copied"], 1)
        act.wait_ge(S["x0_loaded"], 16)
        norm("n1", "attn_norm")
        act.wait_ge(S["w_used"], 1)
        copy(Z[:, 24:26, 1:ZW], half(0)[:, 0:2, :])
        copy(Z[0:32, 26, 1:ZW], half(0)[0:32, 2, :]).then_inc(S["z_copied"], 1)
        act.wait_ge(S["wag_shifted"], 1)
        act.activation(Z[LO, 24, 1:ZW], Z[LO, 24, 1:ZW], ACT.Tanh).then_inc(S["wa_ready"], 1)
        act.activation(Z[:, 25, 1:ZW], Z[:, 25, 1:ZW], ACT.Sigmoid)
        act.activation(Z[0:32, 26, 1:ZW], Z[0:32, 26, 1:ZW], ACT.Sigmoid).then_inc(S["wa_ready"], 1)
        with act.Fori(0, 3) as i:
            for j in range(2):
                n = N_RKV + j
                act.wait_ge(S["w_used"], i * 2 + (n + 1))
                copy(Z[:, bass.ds(i * 8 + 4 * j, 4), 1:ZW], half(n % 2)).then_inc(S["z_copied"], 1)
        act.wait_ge(S["head_sums"], 1)
        for m in range(HM):
            ins = act.activation(lw[:, m, :], PS[:, 4 + m // 2, m % 2 * T:(m % 2 + 1) * T], ACT.Sigmoid, bias=col("w0", m))
        ins.then_inc(S["lw_ready"], 1)
        act.wait_ge(S["head_sums"], 2)
        for m in range(HM):
            ins = act.activation(ga[:, m, :], PS[:, m // 2, m % 2 * T:(m % 2 + 1) * T], ACT.Sigmoid, bias=col("a0", m))
        ins.then_inc(S["ga_ready"], 1)
        act.wait_ge(S["head_sums"], 3)
        act.wait_ge(S["v_ready"], 1)
        act.activation(tmp1.rearrange("p m t -> p (m t)"), PS[:, 4:8, :].rearrange("p b n -> p (b n)"), ACT.Sqrt)\
            .then_inc(S["kk_root"], 1)
        act.wait_ge(S["lc_ready"], 1)
        link(act.activation(tmp2, lw, ACT.Exp, scale=KAPPA))
        act.activation(lw, lw, ACT.Exp, scale=-KAPPA).then_inc(S["exp_ready"], 1)
        for n in range(N_POOL, N_POOL + 2):
            act.wait_ge(S["w_used"], n + 1)
            copy(ZP[:, 4 * (n - N_POOL):4 * (n - N_POOL) + 4, 16:PW], half(n % 2)).then_inc(S["z_copied"], 1)
        for g in range(2 * NCH):
            c, m0 = g // 2, g % 2 * 4
            act.wait_ge(S["bk_turned"], g + 1)
            copy(BKtok(c)[:, m0:m0 + 4, :], PS[:, 4 + g % 4, :].rearrange("p (m j) -> p m j", m=4)).then_inc(S["bk_copied"], 1)
        act.wait_ge(S["pool_sums"], 1)
        for m in range(HM):
            ins = copy(actT[:, m, :], PS[:, 4 + m // 2, m % 2 * T:(m % 2 + 1) * T], col("pool_scale", m))
        ins.then_inc(S["pool_out"], 1)
        for g in range(4):
            act.wait_ge(S["d_turned"], g + 1)
            copy(Di[:, 2 * g:2 * g + 2].rearrange("p m c j -> p (m c j)"), PS[:, g, :]).then_inc(S["d_ready"], 1)
        for c in range(NCH):
            act.wait_ge(S["v_turned"], c + 1)
            for e in range(2):
                h = HALF[1 - e]
                ins = copy(UV(c)[h, :, e, :], PS[h, 4 + c, :].rearrange("p (m i) -> p m i", m=HM))
            ins.then_inc(S["v_placed"], 1)
        for c in range(NCH):
            act.wait_ge(S["u_ready"], c + 1)
            copy(UV(c)[LO, :, 0, :], PS[LO, 1, :].rearrange("p (m i) -> p m i", m=HM)).then_inc(S["u_placed0"], 1)
            if c < NCH - 1:
                act.wait_ge(S["sd_ready"], c + 1)
                copy(UV(c + 1)[LO, :, 0, :], SD[(c + 1) % 2][LO]).then_inc(S["s_placed0"], 1)
            if c % 2:
                t = c // 2
                act.wait_ge(S["y_ready"], c + 1)
                act.wait_ge(S["bonus_done"], 1)
                copy(Ytok[:, t, :].rearrange("p (m e i) -> p e m i", m=HM, e=2),
                     PS[:, 4 + 2 * t:6 + 2 * t, :].rearrange("p e (m i) -> p e m i", m=HM)).then_inc(S["y_copied"], 1)
        for t in range(TT):
            act.wait_ge(S["gn_var"], t + 1)
            act.activation(gns, gnv, ACT.Sqrt).then_inc(S["gn_root"], 1)
        act.wait_ge(S["mix_step"], 6)
        norm("n2", "mlp_norm")
        with act.Fori(0, 8) as i:
            for j in range(2):
                act.wait_ge(S["w_used"], i * 2 + (N_UP + j + 1))
                act.activation(HT1[:, bass.ds(i * 8 + 4 * j, 4), :], half(j), ACT.Relu).then_inc(S["n2_act"], 1)
        act.wait_ge(S["p_turned"], 1)
        copy(pT.rearrange("p k t -> p (k t)"), PS[:, 4, :]).then_inc(S["p_copied"], 1)
        act.wait_ge(S["ffn1_step"], 20)
        norm("n3", "ple_norm")
        with act.Fori(0, 2) as i:
            for j in range(2):
                act.wait_ge(S["w_used"], i * 2 + (N_GATE + j + 1))
                act.wait_ge(S["n3_dve"], i * 2 + (j + 4))
                act.activation(gate_sb, pair[0], ACT.Sigmoid).then_inc(S["n3_act"], 1)
        act.wait_ge(S["n3_dve"], 8)
        square_sum("fin")
        root("fin")

        act.wait_ge(S["fin_done"], 2)
        norm("n4", "attn_norm_g_2")
        act.wait_ge(S["low_rank"], 1)
        copy(LR, PS[0:16, 4, 0:T]).then_inc(S["lr_copied"], 1)
        act.wait_ge(S["low_rank"], 2)
        act.activation(gates.rearrange("p t n -> p (t n)"), PS[:, 5, 0:48], ACT.Sigmoid).then_inc(S["ng_copied"], 1)
        with act.Fori(0, 2) as i:
            for j in range(2):
                act.wait_ge(S["w_used"], i * 2 + (N_GLA + j + 1))
                copy(ZG[:, bass.ds(i * 8 + 4 * j, 4), 3:T + 3], half(j)).then_inc(S["n4_act"], 1)
        act.wait_ge(S["lb_in"], 1)
        link(act.activation(Q1, LB, ACT.Abs))
        link(act.activation(Q1, Q1, ACT.Exp, scale=-1.0))
        act.activation(Q1, Q1, ACT.Ln, bias=1.0).then_inc(S["la_soft"], 1)
        act.wait_ge(S["conv_qk"], 1)
        act.activation(CV[:, 0:8, :], CV[:, 0:8, :], ACT.Silu).then_inc(S["silu_qk"], 1)
        act.wait_ge(S["conv_v"], 1)
        act.activation(CV[:, 8:16, :], CV[:, 8:16, :], ACT.Silu).then_inc(S["gv_ready"], 1)
        act.wait_ge(S["gd_ready"], 1)
        lbc = LB.rearrange("p h (c j) -> p h c j", c=NCH)
        act.activation(GE[0], LB, ACT.Exp, scale=1 / GTAU)
        act.activation(GE[1], GE[1], ACT.Exp, scale=1 / GTAU)
        act.activation(GDEC, lbc[:, :, :, C - 1], ACT.Exp, scale=1 / GTAU).then_inc(S["gexp_ready"], 1)

        def level_exps(*levels):
            for n in levels:
                act.wait_ge(S["level_diff"], n + 1)
                act.activation(WD[n % 2], WD[n % 2], ACT.Exp, scale=1 / GTAU).then_inc(S["level_exp"], 1)

        level_exps(0, 1)
        with act.Fori(0, 2) as i:
            for j in range(2):
                act.wait_ge(S["w_used"], i * 2 + (N_GOQ + j + 1))
                copy(GOQ[:, bass.ds(i * 8 + 4 * j, 4), :], half(j)).then_inc(S["n4_act"], 1)
        act.wait_ge(S["n4_act"], 12)
        act.activation(GOQ[:, 0:8, :], GOQ[:, 0:8, :], ACT.Silu).then_inc(S["gout_ready"], 1)
        level_exps(2, 3)
        act.wait_ge(S["w_used"], N_KCVC + 1)
        copy(NK[:, 0:4, :], half(0)).then_inc(S["n4_act"], 1)
        level_exps(4, 5)
        for n in (N_KSVS, N_KWVW):
            s = n - N_KSVS
            act.wait_ge(S["w_used"], n + 1)
            copy(NK[:, 4 + 2 * s:6 + 2 * s, :], half(n % 2)[:, 0:2, :])
            copy(VSW[:, s], half(n % 2)[:, 2:4, :]).then_inc(S["n4_act"], 1)
        act.wait_ge(S["gk_turned"], 1)
        copy(KTOK.rearrange("p t h d -> p (t h d)"), PS[:, 6:8, :].rearrange("p b n -> p (b n)")).then_inc(S["gkv_copied"], 1)
        act.wait_ge(S["gv_turned"], 1)
        for t in range(TT):
            copy(VTOK[:, t, :], PS[:, 2 * t:2 * t + 2, :].rearrange("p b n -> p (b n)")).then_inc(S["gkv_copied"], 1)
        for t in range(TT):
            act.wait_ge(S["go_ready"], 2 * t + 2)
            copy(OT[:, t, :], PS[:, 2 * t:2 * t + 2, :].rearrange("p b n -> p (b n)")).then_inc(S["o_copied"], 1)
        for t in range(TT):
            act.wait_ge(S["gn_var"], TT + t + 1)
            act.activation(small[:, 32:36], small[:, 28:32], ACT.Sqrt).then_inc(S["gn_root"], 1)
        act.wait_ge(S["pos_turned"], 1)
        for i in range(2):
            copy(XC[i][:, :, 30:31], PS[:, 0, i * CB:(i + 1) * CB].unsqueeze(2)).then_inc(S["pos_copied"], 1)
        act.wait_ge(S["w_used"], N_CMP + 1)
        for i in range(2):
            link(copy(HB[i][:, 0:1], PS[:, 1, i * 31 + 30:i * 31 + 31]))
            act.activation(HID[i], PS[:, 1, i * 31:i * 31 + 30], ACT.Silu, bias=HB[i][:, 0:1]).then_inc(S["hid_ready"], 1)
        act.wait_ge(S["k_var"], 1)
        act.activation(QRS, QRS, ACT.Sqrt)
        act.activation(SQ[:, 0:4, :], SQ[:, 0:4, :], ACT.Sqrt).then_inc(S["k_root"], 1)
        act.wait_ge(S["cmp_ready"], 1)
        copy(VCMP.rearrange("p v d -> p (v d)"), PS[0:NB, 1, P:P + KVH * DH]).then_inc(S["vcmp_copied"], 1)
        act.wait_ge(S["k_var"], 2)
        act.activation(KCSQ, KCSQ, ACT.Sqrt).then_inc(S["k_root"], 1)
        for t in range(TT):
            for s in range(3):
                act.wait_ge(S["max_ready"], t * 3 + s + 1)
                for h in range(NH):
                    a = PCM[:, t, h, :] if s == 2 else PSW[t][:, s, h, :]
                    ins = act.activation(a, a, ACT.Exp, bias=MX[:, t, s, h:h + 1], accum_out=SM[:, t, s, h:h + 1])
                ins.then_inc(S["exp_done"], 1)
        g = 0
        for t in range(TT):
            for kv in range(KVH):
                for s, kt in [(2, 0)] + [(s, kt) for s in range(2) for kt in range(t + 1)]:
                    act.wait_ge(S["pt_ready"], g + 1)
                    if g >= 4:
                        act.wait_ge(S["pt_used"], g - 3)
                    if s == 2:
                        ins = copy(PTC[g % 4], PS[0:NB, 4 + g % 4, :])
                    else:
                        ins = copy(PTR[g % 4], PS[:, 4 + g % 4, :])
                    ins.then_inc(S["pt_copied"], 1)
                    g += 1
                act.wait_ge(S["pt_used"], g)
                copy(actT[:, 8 + kv * GRP:8 + (kv + 1) * GRP, t * P:(t + 1) * P],
                     PS[:, kv, :].rearrange("p (h t) -> p h t", h=GRP)).then_inc(S["att_out"], 1)
        act.wait_ge(S["on_read"], 6)
        norm("n5", "ffn_norm_g_2")
        with act.Fori(0, FF2 // CW) as i:
            act.wait_ge(S["w_used"], i * 2 + (N_GU + 1))
            act.wait_ge(S["n5_dve"], i + 4)
            act.activation(up_gate, half(0), ACT.Silu).then_inc(S["n5_act"], 1)

    @block.vector
    def _(v):
        steps = [0]

        def link(ins):
            steps[0] += 1
            ins.then_inc(S["dve_step"], 1)
            v.wait_ge(S["dve_step"], steps[0])

        def rms(p):
            link(v.tensor_tensor_reduce(out=xn[:, 1, :], in0=xs[:, 1, :], in1=xs[:, 1, :], scale=1.0, scalar=0.0,
                                        op0=ALU.mult, op1=ALU.add, accum_out=ss[:, 1:2]))
            v.wait_ge(S["norm_sum0"], RMS[p])
            v.tensor_scalar(ms, ss, 1.0 / D, EPS, ALU.mult, ALU.add).then_inc(S["norm_mean"], 1)
            v.wait_ge(S["norm_root"], RMS[p])
            link(v.reciprocal(rs, sq))

        def norm(p, gain):
            rms(p)
            for t in range(TT):
                v.tensor_scalar(xn[:, t, :], xs[:, t, :], rs[:, t:t + 1], None, ALU.mult).then_inc(S["norm_xn"], 1)
            for j in range(0, KT // 2, 2):
                v.wait_ge(S["norm_turned"], KT // 2 * NORMS[p] + j + 1)
                for q in range(2):
                    k = 2 * j + q
                    ins = v.tensor_scalar(actT[:, k, :], PS[:, 4 + j % 4, q * T:(q + 1) * T], col(gain, k), None, ALU.mult)
                ins.then_inc(S[f"{p}_dve"], 1)

        v.wait_ge(S["x1_loaded"], 16)
        v.wait_ge(S["x0_loaded"], 16)
        v.wait_ge(S["z_copied"], 1)
        norm("n1", "attn_norm")
        mu = COL["mu_shift"]
        v.wait_ge(S["zeroed"], 2)
        v.wait_ge(S["z_copied"], 2)
        v.tensor_tensor(tmp1[:, 0:2, :], Z[:, 24:26, 0:T], Z[:, 24:26, 1:ZW], ALU.subtract)
        link(v.tensor_tensor(tmp1[0:32, 2, :], Z[0:32, 26, 0:T], Z[0:32, 26, 1:ZW], ALU.subtract))
        for q, n in ((0, P), (1, P), (2, 32)):
            z = Z[0:n, 24 + q, 1:ZW]
            ins = v.scalar_tensor_tensor(z, tmp1[0:n, q, :], pcol[0:n, mu + 24 + q:mu + 25 + q], z, ALU.mult, ALU.add)
        ins.then_inc(S["wag_shifted"], 1)
        v.wait_ge(S["wag_shifted"], 1)
        for q in range(3):
            v.wait_ge(S["z_copied"], 4 + 2 * q)
            link(v.tensor_tensor(tmp1, Z[:, 8 * q:8 * q + 8, 0:T], Z[:, 8 * q:8 * q + 8, 1:ZW], ALU.subtract))
            for m in range(HM):
                z = Z[:, 8 * q + m, 1:ZW]
                ins = v.scalar_tensor_tensor(z, tmp1[:, m, :], pcol[:, mu + 8 * q + m:mu + 8 * q + m + 1], z, ALU.mult, ALU.add)
            if q < 2:
                link(ins)
            else:
                ins.then_inc(S["v_ready"], 1)
            if q == 1:
                for m in range(HM):
                    ins = v.tensor_scalar(kk[:, m, :], zk[:, m, :], col("k_k", m), None, ALU.mult)
                link(ins)
                v.tensor_tensor(tmp2, kk, kk, ALU.mult).then_inc(S["kk_squared"], 1)
        v.wait_ge(S["lw_ready"], 1)
        for m in range(HM):
            ins = v.tensor_tensor_scan(lw[:, m, :], con("keep"), lw[:, m, :], 0.0, ALU.mult, ALU.add)
        ins.then_inc(S["lc_ready"], 1)
        v.wait_ge(S["kk_root"], 1)
        link(v.tensor_scalar(tmp1, tmp1, 1e-12, None, ALU.max))
        link(v.reciprocal(tmp1, tmp1))
        link(v.tensor_tensor(kk, kk, tmp1, ALU.mult))
        v.wait_ge(S["ga_ready"], 1)
        for m in range(HM):
            ins = v.tensor_scalar(tmp1[:, m, :], ga[:, m, :], 1.0, col("k_a", m), ALU.subtract, ALU.mult)
        link(ins)
        link(v.scalar_tensor_tensor(zk, tmp1, 1.0, zk, ALU.add, ALU.mult))
        v.tensor_tensor(ga, kk, ga, ALU.mult)
        for m in range(HM):
            ins = v.scalar_tensor_tensor(tmp1[:, m, :], zr[:, m, :], col("r_k", m), zk[:, m, :], ALU.mult, ALU.mult)
        ins.then_inc(S["rkr_ready"], 1)
        v.wait_ge(S["rkr_ready"], 1)
        v.wait_ge(S["exp_ready"], 1)
        lwc, kkc = (a.rearrange("p m (c j) -> p (m c) j", c=NCH) for a in (lw, kk))
        arf = AR.rearrange("p m c j -> p (m c) j")
        v.tensor_copy(PEND.rearrange("p m c -> p (m c)"), lwc[:, :, C - 1])
        v.tensor_scalar(arf[:, :, 0:1], kkc[:, :, 0:1], -1.0, None, ALU.mult)
        v.scalar_tensor_tensor(arf[:, :, 1:C], lwc[:, :, 0:C - 1], -1.0, kkc[:, :, 1:C], ALU.mult, ALU.mult)

        def chunks(a):
            return a.rearrange("p m (c j) -> p m c j", c=NCH)

        for e in range(2):
            h = HALF[e]
            v.tensor_tensor(BK[h, :, :, e * C:(e + 1) * C], chunks(ga)[h], chunks(tmp2)[h], ALU.mult)
            ins = v.tensor_tensor(BK[h, :, :, (1 - e) * C:(2 - e) * C], chunks(zk)[h], chunks(tmp2)[h], ALU.mult)
        ins.then_inc(S["bk_ready"], 1)
        v.tensor_tensor(AR[:, :, :, C:P], chunks(zr), chunks(lw), ALU.mult).then_inc(S["ar_ready"], 1)
        v.wait_ge(S["ar_ready"], 1)
        v.wait_ge(S["head_sums"], 4)
        v.tensor_tensor(bonus, PS[:, 4:8, :].rearrange("p b (q t) -> p (b q) t", q=2), zv, ALU.mult).then_inc(S["bonus_ready"], 1)
        v.wait_ge(S["bonus_ready"], 1)
        for m in range(HM):
            ins = v.tensor_scalar(bonus[:, m, :], bonus[:, m, :], col("gn_b", m), None, ALU.add)
        ins.then_inc(S["bonus_done"], 1)
        for g in range(2 * HM):
            m, e = g // 2, g % 2
            v.wait_ge(S["score_ready"], g + 1)
            v.tensor_tensor(G[:, m, e], PS[:, g % 4, :].rearrange("p (c j) -> p c j", c=NCH), over(tri, NCH), ALU.mult)\
                .then_inc(S["score_masked"], 1)
        v.wait_ge(S["score_masked"], 2 * HM)
        for e in range(2):
            h = HALF[e]
            l1 = con("level1")[h].unsqueeze(1).unsqueeze(1).broadcast_to([C, HM, NCH, C])
            ins = v.tensor_tensor(DTi[h], G[h, :, e, :, 0:C], l1, ALU.mult)
        link(ins)
        dtf = DTi.rearrange("p m c j -> p (m c) j")
        v.tensor_tensor(dtf, dtf, over(eye64, HM * NCH), ALU.add).then_inc(S["dt_ready"], 1)
        v.wait_ge(S["dt_ready"], 1)

        def eight(a, g):
            return a[:, 2 * g:2 * g + 2].rearrange("p m c j -> p (m c) j")

        def bank8(b):
            return PS[:, b, :].rearrange("p (q j) -> p q j", q=8)

        for lv in range(len(LEVELS)):
            mask = con("levels")[:, lv * C:(lv + 1) * C]
            for g in range(4):
                v.wait_ge(S["f_ready"], 4 * lv + g + 1)
                v.tensor_tensor(eight(Fi, g), bank8(g), over(mask, 8), ALU.mult).then_inc(S["f_masked"], 1)
            for g in range(4):
                if lv < len(LEVELS) - 1:
                    v.wait_ge(S["df_ready"], 4 * lv + g + 1)
                    v.tensor_tensor(eight(Di, g), bank8(4 + g), eight(Di, g), ALU.add).then_inc(S["d_added"], 1)
                v.wait_ge(S["dft_ready"], 4 * lv + g + 1)
                v.tensor_tensor(eight(DTi, g), bank8(g), eight(DTi, g), ALU.add).then_inc(S["dt_added"], 1)
        v.wait_ge(S["pool_sums"], 1)
        v.memset(SD[0], 0.0)
        for e in range(2):
            v.memset(UV(0)[HALF[e], :, e, :], 0.0).then_inc(S[f"s_placed{e}"], 1)
        for e in range(2):
            h = HALF[e]
            v.tensor_copy(G[h, :, e, :, 0:C], AR[h, :, :, 0:C]).then_inc(S["at_placed"], 1)
        for c in range(NCH):
            v.wait_ge(S["zc_ready"], c + 1)
            v.tensor_copy(ZSB.rearrange("p m i -> p (m i)"), PS[:, 0, :]).then_inc(S["zc_copied"], 1)
            v.wait_ge(S["u_ready"], c + 1)
            v.tensor_copy(UV(c)[HI, :, 1, :], PS[HI, 1, :].rearrange("p (m i) -> p m i", m=HM)).then_inc(S["u_placed1"], 1)
            if c < NCH - 1:
                v.wait_ge(S["s_ready"], c + 1)
                now, then = SD[c % 2], SD[(c + 1) % 2]
                link(v.tensor_tensor(then, PS[:, 2, :].rearrange("p (m i) -> p m i", m=HM), now, ALU.add))
                v.tensor_tensor(then, then, along(PEND[:, :, c], C), ALU.mult).then_inc(S["sd_ready"], 1)
                v.wait_ge(S["sd_ready"], c + 1)
                v.tensor_copy(UV(c + 1)[HI, :, 1, :], then[HI]).then_inc(S["s_placed1"], 1)
        gsq = area(B, 16, C)
        v.wait_ge(S["y_copied"], TT)
        for t in range(TT):
            y = Ytok[:, t, :].rearrange("p (h i) -> p h i", h=16)
            link(v.tensor_reduce(gnm, y, AX, ALU.add))
            link(v.tensor_scalar(gnm, gnm, 1.0 / C, None, ALU.mult))
            link(v.tensor_tensor(y, y, along(gnm, C), ALU.subtract))
            link(v.tensor_tensor(gsq, y, y, ALU.mult))
            link(v.tensor_reduce(gnv, gsq, AX, ALU.add))
            v.tensor_scalar(gnv, gnv, 1.0 / C, GN_EPS, ALU.mult, ALU.add).then_inc(S["gn_var"], 1)
            v.wait_ge(S["gn_root"], t + 1)
            link(v.reciprocal(gns, gns))
            v.tensor_tensor(y, y, along(gns, C), ALU.mult).then_inc(S["yn_ready"], 1)
        v.wait_ge(S["yn_turned"], 1)
        for m in range(HM):
            ins = v.scalar_tensor_tensor(actT[:, 8 + m, :], PS[:, 4 + m // 2, m % 2 * T:(m % 2 + 1) * T], col("gn_g", m),
                                         bonus[:, m, :], ALU.mult, ALU.add)
        link(ins)
        v.wait_ge(S["w_used"], N_SMALL + 1)
        for m in range(HM):
            ins = v.tensor_tensor(actT[:, 8 + m, :], PS[:, m // 2, m % 2 * T:(m % 2 + 1) * T], actT[:, 8 + m, :], ALU.mult)
        ins.then_inc(S["mix_step"], 2)

        def add_out(w, g, at, done):
            v.wait_ge(S["w_used"], w)
            r = xs[:, :, bass.ds(at, CW)]
            v.tensor_tensor(r, pair[g], r, ALU.add).then_inc(S[done], 1)

        v.wait_ge(S["x_loaded"], 16)
        with v.Fori(0, 2) as i:
            for j in range(2):
                add_out(i * 2 + (N_OUT + j + 1), j, i * (2 * CW) + j * CW, "mix_step")
        v.wait_ge(S["mix_step"], 6)
        norm("n2", "mlp_norm")
        with v.Fori(0, 8) as i:
            for j in range(2):
                v.wait_ge(S["n2_act"], i * 2 + (j + 5))
                h = HT1[:, bass.ds(i * 8 + 4 * j, 4), :]
                v.tensor_tensor(h, h, h, ALU.mult).then_inc(S["ffn1_step"], 1)
        with v.Fori(0, 2) as i:
            for g in range(2):
                add_out(i * 8 + (N_DOWN + 4 * g + 4), g, i * (2 * CW) + g * CW, "ffn1_step")
        v.wait_ge(S["ffn1_step"], 20)
        norm("n3", "ple_norm")
        with v.Fori(0, 2) as i:
            for j in range(2):
                v.wait_ge(S["n3_act"], i * 2 + (j + 5))
                v.wait_ge(S["proj_ready"], i * 2 + (j + 1))
                v.tensor_tensor(gate_sb, pair[1], gate_sb, ALU.mult).then_inc(S["ple_mul"], 1)
                v.wait_ge(S["ple_mul"], i * 2 + (j + 1))
                r = xs[:, :, bass.ds(i * (2 * CW) + j * CW, CW)]
                v.tensor_tensor(r, r, gate_sb, ALU.add).then_inc(S["n3_dve"], 1)
        v.wait_ge(S["n3_dve"], 8)
        rms("fin")
        v.wait_ge(S["fing_loaded"], 16)
        for t in range(TT):
            v.scalar_tensor_tensor(xs[:, t, :], xs[:, t, :], rs[:, t:t + 1], fing, ALU.mult, ALU.mult).then_inc(S["fin_done"], 1)

        v.wait_ge(S["fin_done"], 2)
        norm("n4", "attn_norm_g_2")
        v.wait_ge(S["low_rank"], 3)
        for h in range(GH):
            ins = v.tensor_scalar(LB[:, h, :], PS[:, 6 + h // 2, h % 2 * T:(h % 2 + 1) * T], col("gla_gate_b_2", h), None, ALU.add)
        ins.then_inc(S["lb_in"], 1)
        v.wait_ge(S["zeroed"], 3)
        v.wait_ge(S["n4_act"], 8)

        def conv(m0):
            for w in range(4):
                for m in range(m0, m0 + 8):
                    tap, x = col("gla_conv_w_2", 16 * w + m), ZG[:, m, w:w + T]
                    if w == 0:
                        ins = v.tensor_scalar(CV[:, m, :], x, tap, None, ALU.mult)
                    else:
                        ins = v.scalar_tensor_tensor(CV[:, m, :], x, tap, CV[:, m, :], ALU.mult, ALU.add)
                if w < 3:
                    link(ins)
            return ins

        conv(0).then_inc(S["conv_qk"], 1)
        v.wait_ge(S["la_soft"], 1)
        link(v.scalar_tensor_tensor(LB, LB, 0.0, Q1, ALU.min, ALU.subtract))
        for h in range(GH):
            ins = v.tensor_tensor_scan(LB[:, h, :], con("keep"), LB[:, h, :], 0.0, ALU.mult, ALU.add)
        link(ins)
        conv(8).then_inc(S["conv_v"], 1)
        v.wait_ge(S["conv_v"], 1)
        lbf = LB.rearrange("p h (c j) -> p (h c) j", c=NCH)
        v.tensor_tensor(GE[1].rearrange("p h (c j) -> p (h c) j", c=NCH), along(lbf[:, :, C - 1], C), lbf, ALU.subtract)\
            .then_inc(S["gd_ready"], 1)

        def halves(a, w, e):
            return a.rearrange("p h (n e w) -> p (h n) e w", e=2, w=w)[:, :, e, :]

        def level_diff(n):
            w = GLA_HALF[n]
            first = halves(LB, w, 0)
            ref = along(first[:, :, w - 1], w)
            v.tensor_tensor(halves(WD[n % 2], w, 0), ref, first, ALU.subtract)
            v.tensor_tensor(halves(WD[n % 2], w, 1), halves(LB, w, 1), ref, ALU.subtract).then_inc(S["level_diff"], 1)

        def level_product(n):
            w, d = GLA_HALF[n], WD[n % 2]
            v.wait_ge(S["level_exp"], n + 1)
            v.tensor_tensor(halves(d, w, 0), halves(d, w, 0), halves(CV[:, 4:8, :], w, 0), ALU.mult)
            v.tensor_tensor(halves(d, w, 1), halves(d, w, 1), halves(CV[:, 0:4, :], w, 1), ALU.mult)\
                .then_inc(S["level_ready"], 1)

        def add_scores(n):
            v.wait_ge(S["gsc_ready"], n + 1)
            sc = SCT.rearrange("p h t j -> p (h t) j")
            tmp = SCTMP.rearrange("p (q j) -> p q j", q=8)
            mask = over(glamask[:, (n - 1) % (len(GLA_HALF) + 1), :], 8)
            v.tensor_tensor(tmp if n else sc, bank8(4 + n % 4), mask, ALU.mult).then_inc(S["gsc_masked"], 1)
            v.wait_ge(S["gsc_masked"], n + 1)
            if n:
                v.tensor_tensor(sc, sc, tmp, ALU.add).then_inc(S["gsc_summed"], 1)
                v.wait_ge(S["gsc_summed"], n)

        level_diff(0)
        level_diff(1)
        v.wait_ge(S["silu_qk"], 1)
        level_product(0)
        level_product(1)
        v.wait_ge(S["gexp_ready"], 1)
        v.scalar_tensor_tensor(Q1, CV[:, 0:4, :], GDK ** -0.5, GE[0], ALU.mult, ALU.mult)
        v.tensor_tensor(K4, CV[:, 4:8, :], GE[1], ALU.mult).then_inc(S["gqk_ready"], 1)
        v.wait_ge(S["glamask_loaded"], 16)
        add_scores(0)
        for n in range(0, len(GLA_HALF), 2):
            add_scores(n + 1)
            add_scores(n + 2)
            if n + 2 < len(GLA_HALF):
                for q in (n + 2, n + 3):
                    level_diff(q)
                for q in (n + 2, n + 3):
                    level_product(q)
        for c in range(NCH - 1):
            v.wait_ge(S["go_ready"], c + 1)
            v.wait_ge(S["gs_ready"], c + 1)
            for h in range(GH):
                src = PS[:, 6 + h // 2, h % 2 * GDV:(h % 2 + 1) * GDV]
                if c == 0:
                    v.tensor_copy(GS[:, h, :], src).then_inc(S["gs_step"], 1)
                else:
                    v.scalar_tensor_tensor(GS[:, h, :], GS[:, h, :], GDEC[:, h, c:c + 1], src, ALU.mult, ALU.add)\
                        .then_inc(S["gs_step"], 1)
            v.wait_ge(S["gs_step"], GH * (c + 1))
        om, ov, osq = small[:, 24:28], small[:, 28:32], small[:, 32:36]
        oj = area(GC + 6144, GH, GDV)
        for t in range(TT):
            v.wait_ge(S["o_copied"], t + 1)
            o = OT[:, t, :].rearrange("p (h e) -> p h e", h=GH)
            link(v.tensor_tensor(oj, o, o, ALU.mult))
            link(v.tensor_reduce(om, oj, AX, ALU.add))
            v.tensor_scalar(ov, om, 1.0 / GDV, EPS, ALU.mult, ALU.add).then_inc(S["gn_var"], 1)
            v.wait_ge(S["gn_root"], TT + t + 1)
            link(v.reciprocal(osq, osq))
            v.tensor_tensor(o, o, along(osq, GDV), ALU.mult).then_inc(S["on_ready"], 1)
        v.wait_ge(S["on_turned"], 1)
        v.wait_ge(S["gout_ready"], 1)
        for m in range(8):
            ins = v.scalar_tensor_tensor(actT[:, m, :], PS[:, 4 + m // 2, m % 2 * T:(m % 2 + 1) * T], col("gla_norm_g_2", m % 2),
                                         GOQ[:, m, :], ALU.mult, ALU.mult)
        ins.then_inc(S["on_read"], 2)
        qg = COL["nsa_q_norm_g_2"]
        link(v.tensor_scalar(QKG, pcol[:, qg + 1:qg + 4], pcol[:, qg:qg + 1], None, ALU.mult))
        v.wait_ge(S["k_sums"], 1)
        rk = SQ[:, 0:4, :].rearrange("p a t -> p (a t)")
        v.tensor_scalar(rk[:, 0:512], PS[:, 0, :], 1.0 / DH, EPS, ALU.mult, ALU.add)
        v.tensor_scalar(rk[:, 512:1024], PS[:, 3, :], 1.0 / DH, EPS, ALU.mult, ALU.add)
        v.tensor_scalar(QRS.rearrange("p t h -> p (t h)"), PS[:, 2, 0:TT * NH], 1.0 / DH, EPS, ALU.mult, ALU.add)\
            .then_inc(S["k_var"], 1)
        v.wait_ge(S["k_root"], 1)
        v.reciprocal(rk, rk)
        link(v.reciprocal(QRS, QRS))
        link(v.tensor_scalar(QRS, QRS, DH ** -0.5, None, ALU.mult))
        for s in range(2):
            k = NK[:, 4 + 2 * s:6 + 2 * s, :].rearrange("p a t -> p (a t)")
            v.scalar_tensor_tensor(k, k, QKG[:, 1 + s:2 + s], rk[:, 512 * s:512 * s + 512], ALU.mult, ALU.mult).then_inc(S["nk_ready"], 1)
        v.wait_ge(S["vcmp_copied"], 1)
        link(v.tensor_copy(KCMP, PS[:, 1, 0:2 * NB]))
        v.tensor_tensor(KCSQ, KCMP, KCMP, ALU.mult).then_inc(S["kc_squared"], 1)
        v.wait_ge(S["k_sums"], 2)
        v.tensor_scalar(KCSQ, PS[:, 2, 0:2 * NB], 1.0 / DH, EPS, ALU.mult, ALU.add).then_inc(S["k_var"], 1)
        v.wait_ge(S["k_root"], 2)
        link(v.reciprocal(KCSQ, KCSQ))
        v.scalar_tensor_tensor(KCMP, KCMP, QKG[:, 0:1], KCSQ, ALU.mult, ALU.mult).then_inc(S["nk_ready"], 1)
        for t in range(TT):
            nk = (t + 1) * P
            v.wait_ge(S["cs_ready"], t + 1)
            v.tensor_tensor(PCM[:, t], PS[:, 2, 0:NH * NB].rearrange("p (h n) -> p h n", h=NH), along(QRS[:, t, :], NB), ALU.mult)\
                .then_inc(S["cs_read"], 1)
            v.wait_ge(S["cs_read"], t + 1)
            link(v.tensor_tensor(PCM[:, t], PCM[:, t], over(con("cmpbias")[:, t * NB:(t + 1) * NB], NH), ALU.add))
            for s in range(2):
                for h in range(NH):
                    u = (t * 2 + s) * NH + h
                    v.wait_ge(S["sc_ready"], u + 1)
                    v.scalar_tensor_tensor(PSW[t][:, s, h, :], PS[:, 4 + u % 4, 0:nk], QRS[:, t, h:h + 1],
                                           con("causal")[:, 2 * P - nk:2 * P] if t else con("causal")[:, P:2 * P],
                                           ALU.mult, ALU.add).then_inc(S["sc_read"], 1)
            v.wait_ge(S["sc_read"], (t + 1) * 2 * NH)
            for s in range(3):
                link(v.tensor_reduce(MX[:, t, s, :], PCM[:, t] if s == 2 else PSW[t][:, s], AX, ALU.max))
                v.tensor_scalar(MX[:, t, s, :], MX[:, t, s, :], -1.0, None, ALU.mult).then_inc(S["max_ready"], 1)
        for t in range(TT):
            for s in range(3):
                a = PCM[:, t] if s == 2 else PSW[t][:, s]
                v.wait_ge(S["exp_done"], t * 3 + s + 1)
                link(v.reciprocal(WT[:, t, s, :], SM[:, t, s, :]))
                gate = gates[:, t, :].rearrange("p (h j) -> p j h", j=3)[:, (s + 1) % 3, :]
                link(v.tensor_tensor(WT[:, t, s, :], WT[:, t, s, :], gate, ALU.mult))
                if s == 2:
                    link(v.tensor_tensor(a, a, over(con("cmpseen")[:, t * NB:(t + 1) * NB], NH), ALU.mult))
                v.tensor_tensor(a, a, along(WT[:, t, s, :], a.shape[2]), ALU.mult).then_inc(S["prob_ready"], 1)
        with v.Fori(0, 2) as i:
            for j in range(2):
                add_out(i * 2 + (N_OUT2 + j + 1), j, i * (2 * CW) + j * CW, "on_read")
        v.wait_ge(S["on_read"], 6)
        norm("n5", "ffn_norm_g_2")
        with v.Fori(0, FF2 // CW) as i:
            v.wait_ge(S["n5_act"], i + 5)
            v.wait_ge(S["w_used"], i * 2 + (N_GU + 2))
            v.tensor_tensor(HT2[:, bass.ds(i * 4, 4), :], half(1), up_gate, ALU.mult).then_inc(S["n5_dve"], 1)
        with v.Fori(0, 2) as i:
            for g in range(2):
                add_out(i * 8 + (N_DOWN2 + 4 * g + 4), g, i * (2 * CW) + g * CW, "n5_dve")

    @block.gpsimd
    def _(pool):
        steps = [0]

        def link(ins):
            steps[0] += 1
            ins.then_inc(S["pool_step"], 1)
            pool.wait_ge(S["pool_step"], steps[0])

        pool.memset(prow, 0.0).then_inc(S["zeroed"], 1)
        pool.memset(Z[:, :, 0:1], 0.0).then_inc(S["zeroed"], 1)
        pool.wait_ge(S["norm_xn"], TT)
        for b in PB:
            pool.memset(b[:, 0:16], 0.0)
        link(pool.memset(ZP[:, :, 0:16], 0.0))
        pool.wait_ge(S["const_loaded"], 16)
        pool.wait_ge(S["z_copied"], 10)
        for m in range(HM):
            g = m // 2
            src = ZP[:, m, :]
            for k in range(g + 1):
                dst = PB[k % 2]
                link(pool.tensor_tensor(dst[:, 16:PW], src[:, 16:PW], src[:, 16 - 2 ** k:PW - 2 ** k], ALU.add))
                src = dst
            pool.tensor_tensor(src[:, 16:32], src[:, 16:32], con("invcnt")[:, 16 * g:16 * g + 16], ALU.mult)
            link(pool.tensor_scalar(src[:, 32:PW], src[:, 32:PW], 0.5 ** (g + 1), None, ALU.mult))
            link(pool.tensor_tensor(ZP[:, m, 16:PW], src[:, 16:PW], ZP[:, m, 16:PW], ALU.subtract))
        pool.tensor_copy(PB[0][:, 0:1], PB[1][:, 0:1]).then_inc(S["pool_ready"], 1)
        pool.wait_ge(S["mix_step"], 2)
        pool.dma_start(ptok, inp["p"][0, 0].rearrange("(t p) d -> p t d", p=P)).then_inc(S["ptok_loaded"], 16)
        pool.dma_start(GW2, W["gla_gate_w2_2"]).then_inc(S["gw2_loaded"], 16)
        pool.wait_ge(S["w_used"], N_GATE)
        pool.dma_start(pproj, W["w_ple_proj"].rearrange("(k p) n -> p k n", p=P)).then_inc(S["pproj_loaded"], 16)
        pool.dma_start(fing, inp["final_norm"].unsqueeze(0).broadcast_to([P, D])).then_inc(S["fing_loaded"], 16)
        pool.wait_ge(S["p_copied"], 1)
        pool.dma_start(SW[:, :, 0:16], wcols("w_in_2", 2048, 16)).then_inc(S["sw_loaded"], 16)
        pool.dma_start(SW[:, :, 16:40], wcols("w_in_2", 5648, 24)).then_inc(S["sw_loaded"], 16)
        pool.wait_ge(S["fin_done"], 2)
        pool.memset(ZG[:, :, 0:3], 0.0).then_inc(S["zeroed"], 1)
        pool.wait_ge(S["conv_v"], 1)
        pool.dma_start(glamask.rearrange("p n j -> p (n j)"), consts[:, GLAMASK_AT:]).then_inc(S["glamask_loaded"], 16)
        pool.wait_ge(S["gqk_ready"], 1)
        pool.wait_ge(S["gsc_summed"], len(GLA_HALF))
        for i, n in enumerate(("k", "v")):
            pool.dma_start(PTAB[i], W[f"cmp_{n}_pos_2"]).then_inc(S["pos_loaded"], 16)
            pool.dma_start(CW2[i], W[f"cmp_{n}_w2_2"]).then_inc(S["pos_loaded"], 16)
        pool.wait_ge(S["n4_act"], 15)
        for i in range(2):
            for kv in range(KVH):
                for l in range(2):
                    ins = pool.tensor_copy(XC[i][:, CST * l:CST * (l + 1), kv * NB:(kv + 1) * NB],
                                           NK[:, 2 * i + kv, CST * l:CST * (l + NB)].rearrange("p (n l) -> p l n", l=CST))
        ins.then_inc(S["xc_ready"], 1)
        pool.wait_ge(S["xc_ready"], 1)
        pool.tensor_tensor(SQ[:, 0:8, :], GOQ[:, 8:16, :], GOQ[:, 8:16, :], ALU.mult)
        pool.tensor_tensor(SQ[:, 8:12, :], NK[:, 4:8, :], NK[:, 4:8, :], ALU.mult).then_inc(S["nsq_ready"], 1)

    ctx.close()

INPUTS = ["x", "p", "attn_norm", "w_in", "mu_shift", "pool_w", "pool_scale", "w0", "w_up", "a0", "a_up", "g_up",
          "k_k", "k_a", "r_k", "gn_g", "gn_b", "w_out", "mlp_norm", "w_ffn_up", "w_ffn_down", "ple_norm",
          "w_ple_gate", "w_ple_proj", "final_norm", "attn_norm_g_2", "w_in_2", "gla_conv_w_2", "gla_gate_w2_2",
          "gla_gate_b_2", "gla_norm_g_2", "nsa_q_norm_g_2", "nsa_kc_norm_g_2", "nsa_ks_norm_g_2",
          "nsa_kw_norm_g_2", "cmp_k_pos_2", "cmp_k_w1_2", "cmp_k_w2_2", "cmp_v_pos_2", "cmp_v_w1_2",
          "cmp_v_w2_2", "w_out_2", "ffn_norm_g_2", "w_gate_2", "w_up_2", "w_down_2"]


def kernel(**inputs):
    import concourse.bacc as bacc
    from concourse.bass_utils import run_bass_kernel_spmd

    nc = bacc.Bacc("TRN2", target_bir_lowering=False, num_devices=1)
    arrays, aps = {}, {}
    for name in INPUTS:
        a = np.ascontiguousarray(inputs[name])
        arrays[f"in_{name}"] = a
        aps[name] = nc.dram_tensor(f"in_{name}", a.shape, mybir.dt.from_np(a.dtype), kind="ExternalInput").ap()
    arrays["in_constants"] = pack_constants()
    consts = nc.dram_tensor("in_constants", arrays["in_constants"].shape, F32, kind="ExternalInput").ap()
    out = nc.dram_tensor("out_y", (1, T, D), F32, kind="ExternalOutput").ap()
    build(nc, aps, consts, out)
    r = run_bass_kernel_spmd(nc, [arrays], core_ids=[0])
    return r.results[0]["out_y"]
```

```python
from contextlib import ExitStack

import numpy as np

import concourse.bass as bass
from concourse import mybir

F32 = mybir.dt.float32
ALU = mybir.AluOpType
ACT = mybir.ActivationFunctionType
AX = mybir.AxisListType.X

P = 128
T = 256
TT = T // P
D = 2048
KT = D // P
CW = 512
FF1 = 8192
FF2 = 5632
EPS = 1e-6
RW = 1024
HM = RW // P
C = 64
NCH = T // C
KAPPA = float(np.exp(-0.5))
GN_EPS = 64e-5
LEVELS = (2, 4, 8, 16, 32)
GH, GDK, GDV = 4, 128, 256
GTAU = 16.0
GLA_HALF = (32, 16, 8, 4, 2, 1)
NH, KVH, DH = 8, 2, 128
GRP = NH // KVH
CB, CST = 32, 16
NB = (T - CB) // CST + 1
NEG = -1e30


def constants():
    p = np.arange(P)[:, None]
    q = p % C
    j = np.arange(C)[None, :]
    c = {}
    c["ident"] = np.eye(P)
    c["tri"] = np.concatenate([q < j, q <= j], 1)
    c["levels"] = np.concatenate([((q // b) % 2 == 1) & (j // b == q // b - 1) for b in LEVELS], 1)
    c["level1"] = (j % 2 == 1) & (q == j - 1)
    c["eye64"] = q == j
    c["headones"] = (p // C) == (np.arange(P)[None, :] // C)
    c["ones"] = np.ones((P, P))
    c["keep"] = np.broadcast_to(np.arange(T)[None, :] % C != 0, (P, T))
    t16 = np.arange(16)
    c["invcnt"] = np.broadcast_to(
        np.concatenate([1.0 / np.minimum(t16 + 1, w) for w in (2, 4, 8, 16)])[None, :], (P, 64))
    s = np.arange(P)[None, :]
    c["causal"] = np.concatenate([np.zeros((P, P)), np.where(s > p, NEG, 0.0)], 1)
    end = np.arange(NB)[None, :] * CST + CB - 1
    seen = np.concatenate([end <= p + P * t for t in range(TT)], 1)
    c["cmpseen"] = seen
    c["cmpbias"] = np.where(seen, 0.0, NEG)
    c["glamask"] = GDK ** -0.5 * np.concatenate(
        [((q // w) % 2 == 0) & (j // w == q // w + 1) for w in GLA_HALF] + [q == j], 1)
    return {k: np.asarray(v, np.float32) for k, v in c.items()}


CONST_AT = {}


def pack_constants():
    parts, at = constants(), 0
    for k, v in parts.items():
        CONST_AT[k] = (at, v.shape[1])
        at += v.shape[1]
    return np.ascontiguousarray(np.concatenate(list(parts.values()), 1))


ROWS = [[("attn_norm", 16), ("mlp_norm", 16), ("ple_norm", 16), ("attn_norm_g_2", 16), ("ffn_norm_g_2", 16),
         ("mu_shift", 26), ("mu_tail", 1), ("pool_scale", 8), ("w0", 8)],
        [("a0", 8), ("k_k", 8), ("k_a", 8), ("r_k", 8), ("gla_conv_w_2", 64), ("gla_gate_b_2", 4),
         ("gla_norm_g_2", 2), ("nsa_q_norm_g_2", 1), ("nsa_kc_norm_g_2", 1), ("nsa_ks_norm_g_2", 1),
         ("nsa_kw_norm_g_2", 1), ("gn_g", 8), ("gn_b", 8)]]
COL = {}
for _t, _rows in enumerate(ROWS):
    _at = P * _t
    for _n, _r in _rows:
        COL[_n] = _at
        _at += _r
    assert _at <= P * (_t + 1)


SIGNALS = """
    w_used const_loaded zeroed rows_loaded norm_xn waup_loaded gup_loaded y_ready x_loaded sum_step out_stored
    w_low x_low norm_turned side_turned z_copied wa_ready head_sums kk_squared head_acts rkr_ready bk_ready
    bonus_ready bk_copied bk_turned score_masked score_ready pool_ready pool_sums dt_ready d_turned d_ready
    d_added dt_added f_ready pool_out f_masked df_ready dft_ready v_ready v_turned v_placed at_placed s_placed0
    s_placed1 zc_ready zc_copied u_ready u_placed0 u_placed1 s_ready y_copied yn_ready yn_turned ffn1_relu
    ffn1_low ptok_loaded side_copied pproj_loaded proj_ready sw_loaded low_rank n4_act gw2_loaded silu_qk lb_in
    level_ready gsc_masked gsc_ready gqk_ready gk_turned gv_ready gv_turned gsc_summed gkv_copied gs_step
    go_ready gs_ready on_ready on_turned pos_loaded xc_ready nsq_ready k_sums hid_ready cmp_ready kc_squared
    nk_ready on_read cs_read cs_ready sc_read sc_ready att_out pt_copied prob_ready pt_ready pt_used gla_low
    ffn2_silu ffn2_mul ffn2_low act_step norm_sum0 norm_mean norm_root w_high x0_loaded x1_loaded wag_shifted
    lc_ready sd_ready bonus_done gn_var gn_root mixed mixed_high gate_ready fin_done la_soft conv_done gd_ready
    gexp_ready level_diff level_exp gout_ready o_copied k_var k_root gla_high max_ready exp_done att_high
    dve_step x_high ar_ready ffn1_high fing_loaded glamask_loaded ffn2_high pool_step n1_dve n1_act n4_dve
    w_loaded0 w_loaded1 w_loaded2 w_loaded3
"""


def build(nc, inp, consts, out):
    ctx = ExitStack()

    places = {}

    def sbuf(name, shape, *r32_places):
        t = ctx.enter_context(nc.sbuf_tensor(name, shape, F32))
        at = nc.sbuf_base - 4 * int(np.prod(shape[1:]))
        places[name] = [(c, n, nc.alloc_sbuf_tensor_at(f"{name}_r{c}", [P, n], mybir.dt.float32r, offset=at + 4 * c))
                        for c, n in r32_places]
        return t

    def r32(ap):
        for c, n, t in places[ap.tensor.name]:
            if c <= ap.offset < c + n:
                return bass.AP(tensor=t, offset=ap.offset - c, ap=[[n, P]] + [list(d) for d in ap.ap][1:])

    def high_of(ap):
        return r32(ap).bitcast(F32)

    xs = sbuf("xs", [P, TT, D])
    actT = sbuf("actT", [P, KT, T], (0, KT * T))
    ring = sbuf("ring", [P, 2, KT * CW], *((2048 * j, 2048) for j in range(8)))
    GLAMASK_AT = CONST_AT["glamask"][0]
    cst = sbuf("cst", [P, GLAMASK_AT])
    pcol = sbuf("pcol", [P, 2 * P])
    small = sbuf("small", [P, 64])
    NA = 26560
    HIW_AT, XH_AT, HTH_AT, HTL_AT = 16896, 12288, 0, 4096
    R32_AT = [(HIW_AT + 2048 * j, 2048) for j in range(4)] + [(at, KT * T) for at in (XH_AT, HTH_AT, HTL_AT)]
    arena = sbuf("arena", [P, NA], *R32_AT)
    PS = ctx.enter_context(nc.psum_tensor("PS", [P, 8, 512], F32))

    S = {n: ctx.enter_context(nc.semaphore(n)) for n in SIGNALS.split()}

    def con(name):
        at, n = CONST_AT[name]
        return cst[:, at:at + n]

    def col(name, i=0):
        return pcol[:, COL[name] + i:COL[name] + i + 1]

    def split(v, dims):
        if len(dims) == 2:
            return v.rearrange("p (a b) -> p a b", a=dims[0])
        if len(dims) == 3:
            return v.rearrange("p (a b c) -> p a b c", a=dims[0], b=dims[1])
        if len(dims) == 4:
            return v.rearrange("p (a b c d) -> p a b c d", a=dims[0], b=dims[1], c=dims[2])
        return v

    def area(at, *dims):
        n = int(np.prod(dims))
        assert at + n <= NA, (at, dims)
        return split(arena[:, at:at + n], dims)

    def over(ap, n):
        return ap.unsqueeze(1).broadcast_to([ap.shape[0], n, ap.shape[1]])

    def along(ap, n):
        return ap.unsqueeze(len(ap.shape)).broadcast_to(list(ap.shape) + [n])

    ident, tri, eye64 = con("ident"), con("tri"), con("eye64")
    pair = [PS[:, 0:2, :], PS[:, 2:4, :]]

    def half(g):
        return pair[g].rearrange("p b (f t) -> p (b f) t", f=2)


    def out_rows(g):
        return pair[g].rearrange("p b (h t) -> p h b t", h=2)

    def by_half(a):
        return a.rearrange("p (h b) t -> p h b t", h=2)

    def unit_at(s, j):
        return ring[:, s, 2048 * j:2048 * (j + 1)]

    def slot(s):
        return ring[:, s, :].rearrange("p (k n) -> p k n", k=KT)

    LO, HI = slice(0, C), slice(C, P)
    HALF = [LO, HI]

    ss, ms, sq, rs = (small[:, 2 * i:2 * i + 2] for i in range(4))
    gnm, gnv, gns = (small[:, 8 + 16 * i:24 + 16 * i] for i in range(3))

    ZW = T + 1
    Z = area(0, 27, ZW)
    zr, zk, zv = (Z[:, 8 * i:8 * i + 8, 1:ZW] for i in range(3))
    B = 27 * ZW
    tmp1, tmp2, lw, ga, kk = (area(B + 2048 * i, HM, T) for i in range(5))
    AR_AT = B + 5 * 2048
    AR = area(AR_AT, HM, NCH, P)
    BK = area(AR_AT + 4096, HM, NCH, P)
    SD_AT = AR_AT + 8192
    PEND = area(SD_AT + 512, HM, NCH)
    ZSB = area(SD_AT + 544, HM, C)
    prow = area(AR_AT + 4096, 2, P)
    G = area(B, HM, 2, NCH, P)
    DTi = area(AR_AT + 4096, HM, NCH, C)
    Di = area(AR_AT + 6144, HM, NCH, C)
    Fi = area(B + 4 * 2048, HM, NCH, C)
    UVa = [area(AR_AT + 6144, 2, HM, 2, C), area(B + 4 * 2048, 2, HM, 2, C)]

    def UV(c):
        return UVa[c // 2][:, c % 2]

    def BKtok(c):
        if c < 2:
            v = actT[:, 8 + 4 * c:12 + 4 * c, :].rearrange("p a b -> p (a b)")
        else:
            v = area(8 * ZW + (c - 2) * 1024, 1024)
        return v.rearrange("p (m j) -> p m j", m=HM)

    bonus = zr
    Ytok = area(16 * ZW, TT, RW)
    xflat = xs[:, :, :].rearrange("p a b -> p (a b)")
    waup = xflat[:, 0:RW]
    PW = T + 16
    ZP = xflat[:, RW:RW + HM * PW].rearrange("p (m t) -> p m t", m=HM)
    PB = [xflat[:, RW + HM * PW + i * PW:RW + HM * PW + (i + 1) * PW] for i in range(2)]
    SD = [xflat[:, 3072 + 512 * i:3584 + 512 * i].rearrange("p (m i) -> p m i", m=HM) for i in range(2)]
    XN = {p: area(AR_AT if p in ("n1", "n4") else 0, TT, D) for p in ("n1", "n2", "n3", "fin", "n4", "n5")}
    poolw = ring[:, 1, 0:2048].rearrange("p (q n) -> p q n", q=8)
    gup, gup2 = ring[:, 1, 2048:3072], ring[0:32, 1, 3072:4096]

    HIW = [area(HIW_AT + 2048 * j, 2048) for j in range(4)]
    XH = area(XH_AT, KT, T)
    HTH, HTL = area(HTH_AT, KT, T), area(HTL_AT, KT, T)
    RQ = [area(8192 + 1024 * b, 4, T) for b in range(2)]
    pproj = area(8192, 2, D)
    ptok = area(AR_AT + 8192, TT, 256)
    pT = area(16384, 2, T)
    fing = area(4096, D)
    gate_sb = [area(6144 + 1024 * b, TT, CW) for b in range(2)]

    GC = 16 * (T + 3)
    ZG = area(0, 16, T + 3)
    CV = area(GC, 16, T)
    LB = area(GC + 4096, GH, T)
    Q1, K4 = area(GC + 5120, GH, T), area(GC + 8192, GH, T)
    WD = [area(GC + 6144 + 1024 * i, GH, T) for i in range(2)]
    KTOK = area(GC + 9216, TT, GH, GDK)
    SCT = area(GC + 10240, GH, TT, C)
    GS = area(GC + 10752, GH, GDV)
    OT = area(GC + 11776, TT, RW)
    GN_AT = GC + 13824
    GOQ = area(GN_AT, 16, T)
    NK = area(GN_AT + 4096, 8, T)
    VSW = area(GN_AT + 6144, 2, TT, 256)
    SW = area(GN_AT + 7168, KT, 40)
    LR = area(GN_AT + 7808, T)[0:16]
    GW2 = area(GN_AT + 8064, 512)[0:16]
    GE = [area(1024 * i, GH, T) for i in range(2)]
    glamask, SCTMP = area(2048, len(GLA_HALF) + 1, C), area(3072, 512)
    GDEC = small[:, 8:8 + GH * NCH].rearrange("p (h c) -> p h c", h=GH)
    VTOK = area(GC + 2048, TT, RW)
    gates = area(GN_AT + 7168, TT, 24)
    XC = [area(992 * i, CB, 31) for i in range(2)]
    CW2 = [area(1984 + 128 * i, P) for i in range(2)]
    PTAB = [area(2240 + 128 * i, P)[0:CB] for i in range(2)]
    HB = [area(2496 + 2 * i, 2) for i in range(2)]
    HID = [area(2500 + 30 * i, 2 * NB) for i in range(2)]
    KCMP = area(2560, 2 * NB)
    KCSQ = area(2590, 2 * NB)
    QKG = area(2620, 3)
    QRS, RSP = area(2623, TT, NH), area(2639, TT, NH)
    VCMP = area(GN_AT + 7808, KVH, DH)[0:NB]
    SQ = area(2912, 12, T)
    PCM = area(5984, TT, NH, NB)
    PSW = [area(6224, 2, NH, P), area(8272, 2, NH, T)]
    PTR = [area(12368 + 512 * i, 512) for i in range(4)]
    PTC = [area(14416 + 512 * i, 512)[0:NB] for i in range(4)]
    MX, SM, WT = (area(16464 + 48 * i, TT, 3, NH) for i in range(3))
    XH2 = HTH

    W = {n: a[0] if n not in ("final_norm", "x", "p") else a for n, a in inp.items()}
    xin, xout = (a.rearrange("o (t p) d -> p (o t) d", p=P) for a in (inp["x"], out))

    def wcols(name, c0, n=CW, k0=0, nk=KT):
        return W[name].rearrange("(k p) n -> p k n", p=P)[:, k0:k0 + nk, c0:c0 + n]

    N_WAG, N_RKV, N_POOL, N_SMALL, N_OUT, N_F1, N_GATE = 0, 1, 7, 9, 10, 14, 46
    N_GLA, N_GOQ, N_KCVC, N_KSVS, N_KWVW, N_CMP, N_OUT2, N_F2, N_END = 50, 54, 58, 59, 60, 61, 62, 66, 104
    F1_PARTS = 4
    F2_PARTS, F2_GROUPS = 3, 3
    F2_LAST = FF2 // CW - F2_PARTS * F2_GROUPS
    F2_N = 2 * F2_GROUPS + 4
    UNITS = {4: (0, 1, 2, 3), 3: (0, 1, 2), 2: (0, 2)}

    def used(n, i=None, per=2, unit=4):
        v = 4 * n + unit
        return v if i is None else i * (4 * per) + v

    def split_count(n, j, i=None, per=2):
        v = 4 * (n - N_OUT if n < N_GLA else n - N_OUT2 + N_GLA - N_OUT) + j + 1
        return v if i is None else i * (4 * per) + v

    def counts(units, j):
        q = units.index(j)
        return (units[q + 1] if q + 1 < len(units) else 4) - j

    SUM = {"out": 2, "ffn1": 6, "gate": 22, "out2": 26, "ffn2": 30, "end": 46}
    NORMS = {"n1": 0, "n2": 1, "n3": 2, "n4": 3, "n5": 4}
    XSPLIT = {"n2": 0, "n3": 8, "n5": 16}
    RMS = {"n1": 1, "n2": 2, "n3": 3, "fin": 4, "n4": 5, "n5": 6}

    block = ctx.enter_context(nc.Block())

    @block.sync
    def _(sp):
        def load(n, dsts, srcs, i=None, per=2):
            for h in range(2):
                if n >= 2:
                    sp.wait_ge(S["w_used"], used(n - 2, i, per, 2 * (h + 1)))
                sp.dma_start(dsts[h], srcs[h]).then_inc(S[f"w_loaded{2 * (n % 2) + h}"], 16)

        def k_halves(n, name, c0, nc=CW, k0=0, nk=KT // 2, i=None, per=2, step=0, k_step=0):
            w = W[name].rearrange("(k p) n -> p k n", p=P)
            dsts, srcs = [], []
            for h in range(2):
                m = nk if isinstance(nk, int) else nk[h]
                first = nk if isinstance(nk, int) else nk[0]
                ks = slice(k0 + h * first, k0 + h * first + m) if i is None or not k_step else \
                    bass.ds(i * k_step + (k0 + h * first), m)
                cs = slice(c0, c0 + nc) if i is None or not step else bass.ds(i * step + c0, nc)
                dsts.append(slot(n % 2)[:, 8 * h:8 * h + m, 0:nc])
                srcs.append(w[:, ks, cs])
            load(n, dsts, srcs, i, per)

        def column_halves(n, name, c0, i=None, per=2, step=0):
            w = W[name].rearrange("(k p) n -> p k n", p=P)
            dsts, srcs = [], []
            for h in range(2):
                at = c0 + h * CW // 2
                dsts.append(ring[:, n % 2, 4096 * h:4096 * (h + 1)].rearrange("p (k n) -> p k n", k=KT))
                srcs.append(w[:, :, slice(at, at + CW // 2) if i is None else bass.ds(i * step + at, CW // 2)])
            load(n, dsts, srcs, i, per)

        def load_loop(first, count, name, c0):
            with sp.Fori(0, count // 2) as i:
                for j in range(2):
                    k_halves(first + j, name, c0 + j * CW, i=i, step=2 * CW)

        sp.dma_start(cst[:], consts[:, 0:GLAMASK_AT]).then_inc(S["const_loaded"], 16)
        sp.wait_ge(S["zeroed"], 1)
        for t, rows in enumerate(ROWS):
            at = 0
            for name, n in rows:
                dst = prow[at:at + n, t, :]
                if name == "mu_shift":
                    src = W["mu_shift"][0:26 * P].rearrange("(r c) -> r c", c=P)
                elif name == "mu_tail":
                    dst, src = prow[at:at + 1, t, 0:32], W["mu_shift"][26 * P:].unsqueeze(0)
                elif name == "r_k":
                    src = W["r_k"].rearrange("(r e) c -> r (e c)", e=2)
                elif name == "gla_conv_w_2":
                    src = W[name].rearrange("w (r c) -> (w r) c", c=P)
                else:
                    src = W[name].rearrange("(r c) -> r c", c=P)
                sp.dma_start(dst, src).then_inc(S["rows_loaded"], 16)
                at += n
        k_halves(0, "w_in", 4096, 288)
        k_halves(1, "w_in", 1024)
        k_halves(2, "w_in", 1536)
        sp.wait_ge(S["norm_xn"], 2)
        sp.dma_start(waup[LO], W["w_up"]).then_inc(S["waup_loaded"], 16)
        sp.dma_start(waup[HI], W["a_up"]).then_inc(S["waup_loaded"], 16)
        for n in range(3, 7):
            k_halves(n, "w_in", 512 + 512 * n)
        for n in range(7, 9):
            k_halves(n, "w_in", 512 * (n - 7))
        wp = W["pool_w"].rearrange("g (k p) n -> p (g k) n", p=P)
        load(N_SMALL, [poolw[:, 0:4], poolw[:, 4:8]], [wp[:, 0:4], wp[:, 4:8]])
        sp.dma_start(gup, W["g_up"][0:P]).then_inc(S["gup_loaded"], 16)
        sp.dma_start(gup2, W["g_up"][P:]).then_inc(S["gup_loaded"], 16)
        k_halves(N_OUT, "w_out", 0)
        sp.wait_ge(S["y_ready"], NCH)
        sp.dma_start(xs[:], xin).then_inc(S["x_loaded"], 16)
        for n in range(N_OUT + 1, N_F1):
            k_halves(n, "w_out", CW * (n - N_OUT))
        with sp.Fori(0, F1_PARTS) as i:
            for c in range(4):
                column_halves(N_F1 + c, "w_ffn_up", CW * c, i, 8, 4 * CW)
            for g in range(4):
                k_halves(N_F1 + 4 + g, "w_ffn_down", CW * g, i=i, per=8, k_step=KT)
        load_loop(N_GATE, 4, "w_ple_gate", 0)
        load_loop(N_GLA, 4, "w_in_2", 0)
        load_loop(N_GOQ, 4, "w_in_2", 2064)
        for n in range(N_KCVC, N_CMP):
            k_halves(n, "w_in_2", 4112 + CW * (n - N_KCVC))
        cw = slot(N_CMP % 2).rearrange("p k n -> p (k n)").rearrange("p (s l h) -> p s l h", s=2, l=CB)
        load(N_CMP, [cw[:, 0], cw[:, 1]], [W[f"cmp_{n}_w1_2"].rearrange("(l d) h -> d l h", d=DH) for n in ("k", "v")])
        load_loop(N_OUT2, 4, "w_out_2", 0)

        def ffn2_part(n, c0, groups, i=None):
            for m in range(groups):
                for j, name in enumerate(("w_gate_2", "w_up_2")):
                    column_halves(n + 2 * m + j, name, c0 + m * CW, i, F2_N, F2_GROUPS * CW)
            for g in range(4):
                k_halves(n + 2 * groups + g, "w_down_2", CW * g, k0=c0 // P, nk=(8, 4) if groups == 3 else 4,
                         i=i, per=F2_N, k_step=4 * F2_GROUPS)

        with sp.Fori(0, F2_PARTS) as i:
            ffn2_part(N_F2, 0, F2_GROUPS, i)
        ffn2_part(N_F2 + F2_PARTS * F2_N, F2_PARTS * F2_GROUPS * CW, F2_LAST)
        for g in range(4):
            sp.wait_ge(S["sum_step"], SUM["end"] - 3 + g)
            sp.dma_start(xout[:, :, CW * g:CW * (g + 1)], xs[:, :, CW * g:CW * (g + 1)]).then_inc(S["out_stored"], 16)
        sp.wait_ge(S["out_stored"], 64)

    @block.tensor
    def _(pe):
        def loaded(n, i=None):
            v = 16 * (n // 2 + 1)
            for h in range(2):
                pe.wait_ge(S[f"w_loaded{2 * (n % 2) + h}"], v if i is None else i * 16 + v)

        def rows_out(n, dst, m, k_tiles=KT, f0=0):
            for k in range(k_tiles):
                mm = pe.matmul(dst, slot(n % 2)[:, k, f0:f0 + m], actT[:, k, :], start=(k == 0), stop=(k == k_tiles - 1))
            return mm

        def chunk_rows(n, g, tiles=4):
            for f in range(tiles):
                mm = rows_out(n, half(g)[:, f, :], P, f0=f * P)
            return mm

        def three(dst, weights, tokens, first, last):
            (wh, wl), (xh, xl) = weights, tokens
            for q, (w, x) in enumerate(((wh, xh), (wh, xl), (wl, xh))):
                mm = pe.matmul(dst, r32(w), r32(x), start=first and q == 0, stop=last and q == 2)
            return mm

        def split_rows(n, g, i=None, per=2):
            for j in range(4):
                pe.wait_ge(S["w_low"], split_count(n, j, i, per))
                h, k0 = j // 2, j % 2 * 8
                wh, wl = (a.rearrange("p (k n) -> p k n", k=8) for a in (HIW[j], unit_at(n % 2, j)))
                for f in range(2):
                    for k in range(8):
                        c = slice(f * P, (f + 1) * P)
                        mm = three(pair[g][:, f, h * T:(h + 1) * T], (wh[:, k, c], wl[:, k, c]),
                                   (XH[:, k0 + k, :], actT[:, k0 + k, :]), k0 + k == 0, k0 + k == KT - 1)
                mm.then_inc(S["w_used"], 1)

        def split_tokens(n, out, xh, xl, i=None, per=2, units=UNITS[4], ready=None):
            for q, j in enumerate(units):
                pe.wait_ge(S["w_low"], split_count(n, j, i, per))
                if ready is not None:
                    ready(q)
                wh, wl = (a.rearrange("p (k n) -> p k n", k=4) for a in (HIW[j], unit_at(n % 2, j)))
                for k in range(4):
                    for t in range(TT):
                        x, tok = 4 * q + k, slice(t * P, (t + 1) * P)
                        mm = three(out[:, t, :], (xh(x)[:, tok], xl(x)[:, tok]), (wh[:, k, :], wl[:, k, :]),
                                   x == 0, x == 4 * len(units) - 1)
                mm.then_inc(S["w_used"], counts(units, j))

        def norm(p):
            pe.wait_ge(S["norm_xn"], TT * (NORMS[p] + 1))
            for j in range(KT // 2):
                if j >= 4:
                    if p in XSPLIT:
                        pe.wait_ge(S["x_low"], XSPLIT[p] + j - 3)
                    else:
                        pe.wait_ge(S[f"{p}_dve" if j % 2 == 0 else f"{p}_act"], (j - 4) // 2 + 1)
                for q in range(2):
                    for t in range(TT):
                        k = 2 * j + q
                        mm = pe.transpose(PS[:, 4 + j % 4, q * T + t * P:q * T + (t + 1) * P],
                                          XN[p][:, t, k * P:(k + 1) * P], ident)
                mm.then_inc(S["norm_turned"], 1)
            if p in XSPLIT:
                pe.wait_ge(S["x_low"], XSPLIT[p] + 8)
            else:
                pe.wait_ge(S[f"{p}_dve"], 4)
                pe.wait_ge(S[f"{p}_act"], 4)

        pe.wait_ge(S["const_loaded"], 16)
        pe.wait_ge(S["rows_loaded"], 16 * sum(len(r) for r in ROWS))
        for t in range(2):
            mm = pe.transpose(PS[:, 0, t * P:(t + 1) * P], prow[:, t, :], ident)
        mm.then_inc(S["side_turned"], 1)

        norm("n1")
        pe.wait_ge(S["z_copied"], 1)
        loaded(0)
        for f in range(2):
            rows_out(0, half(0)[:, f, :], P, f0=f * P)
        rows_out(0, half(0)[0:32, 2, :], 32, f0=2 * P).then_inc(S["w_used"], 4)
        with pe.Fori(0, 3) as i:
            for j in range(2):
                n = N_RKV + j
                loaded(n, i)
                pe.wait_ge(S["z_copied"], i * 2 + n)
                chunk_rows(n, n % 2).then_inc(S["w_used"], 4)
        pe.wait_ge(S["waup_loaded"], 32)
        pe.wait_ge(S["wa_ready"], 2)
        for m in range(HM):
            mm = pe.matmul(PS[:, 4 + m // 2, m % 2 * T:(m % 2 + 1) * T], waup[LO, m * P:(m + 1) * P],
                           Z[LO, 24, 1:ZW], start=True, stop=True)
        mm.then_inc(S["head_sums"], 1)
        pe.wait_ge(S["z_copied"], 8)
        for m in range(HM):
            mm = pe.matmul(PS[:, m // 2, m % 2 * T:(m % 2 + 1) * T], waup[HI, m * P:(m + 1) * P],
                           Z[HI, 24, 1:ZW], start=True, stop=True)
        mm.then_inc(S["head_sums"], 1)
        pe.wait_ge(S["kk_squared"], 1)
        pe.wait_ge(S["head_acts"], 1)
        for m in range(HM):
            mm = pe.matmul(PS[:, 4 + m // 2, m % 2 * T:(m % 2 + 1) * T], con("headones"), tmp2[:, m, :],
                           start=True, stop=True)
        mm.then_inc(S["head_sums"], 1)
        pe.wait_ge(S["head_acts"], 2)
        for n in range(N_POOL, N_POOL + 2):
            loaded(n)
            chunk_rows(n, n % 2).then_inc(S["w_used"], 4)
        pe.wait_ge(S["rkr_ready"], 1)
        pe.wait_ge(S["head_acts"], 3)
        for m in range(HM):
            mm = pe.matmul(PS[:, 4 + m // 2, m % 2 * T:(m % 2 + 1) * T], con("headones"), tmp1[:, m, :],
                           start=True, stop=True)
        mm.then_inc(S["head_sums"], 1)
        pe.wait_ge(S["bk_ready"], 1)
        pe.wait_ge(S["bonus_ready"], 1)
        for g in range(2 * NCH):
            c, m0 = g // 2, g % 2 * 4
            if g >= 4:
                pe.wait_ge(S["bk_copied"], g - 3)
            for m in range(4):
                mm = pe.transpose(PS[:, 4 + g % 4, m * P:(m + 1) * P], BK[:, m0 + m, c, :], ident)
            mm.then_inc(S["bk_turned"], 1)
        pe.wait_ge(S["z_copied"], 10)
        for g in range(2 * HM):
            m, e = g // 2, g % 2
            if g >= 4:
                pe.wait_ge(S["score_masked"], g - 3)
            for c in range(NCH):
                mm = pe.matmul(PS[:, g % 4, c * P:(c + 1) * P], BK[HALF[e], m, c, :], AR[HALF[e], m, c, :],
                               start=True, stop=True)
            mm.then_inc(S["score_ready"], 1)
        loaded(N_SMALL)
        pe.wait_ge(S["pool_ready"], 1)
        pe.wait_ge(S["bk_copied"], 8)
        for m in range(HM):
            for k in range(2):
                g = m // 2
                mm = pe.matmul(PS[:, 4 + m // 2, m % 2 * T:(m % 2 + 1) * T],
                               poolw[:, 2 * g + k, m % 2 * P:(m % 2 + 1) * P], ZP[:, 2 * g + k, 16:PW],
                               start=(k == 0), stop=(k == 1))
        mm.then_inc(S["pool_sums"], 1)
        pe.wait_ge(S["dt_ready"], 1)

        def inverse_group(g, bank, lhs, rhs):
            for m in range(2 * g, 2 * g + 2):
                for c in range(NCH):
                    for e in range(2):
                        h = HALF[e]
                        at = (m % 2 * NCH + c) * C
                        mm = pe.matmul(PS[h, bank, at:at + C], lhs(h, m, c, e), rhs(h, m, c, e), start=True, stop=True)
            return mm

        for g in range(4):
            inverse_group(g, g, lambda h, m, c, e: DTi[h, m, c, :], lambda h, m, c, e: eye64[h]).then_inc(S["d_turned"], 1)
        for lv in range(len(LEVELS)):
            last = lv == len(LEVELS) - 1
            for g in range(4):
                if lv == 0:
                    pe.wait_ge(S["d_ready"], g + 1)
                else:
                    pe.wait_ge(S["d_added"], 4 * (lv - 1) + g + 1)
                    pe.wait_ge(S["dt_added"], 4 * (lv - 1) + g + 1)
                inverse_group(g, g, lambda h, m, c, e: G[h, m, e, c, 0:C], lambda h, m, c, e: Di[h, m, c, :])\
                    .then_inc(S["f_ready"], 1)
            if lv == 0:
                pe.wait_ge(S["pool_out"], 1)
            for g in range(4):
                pe.wait_ge(S["f_masked"], 4 * lv + g + 1)
                if not last:
                    inverse_group(g, 4 + g, lambda h, m, c, e: DTi[h, m, c, :], lambda h, m, c, e: Fi[h, m, c, :])\
                        .then_inc(S["df_ready"], 1)
                inverse_group(g, g, lambda h, m, c, e: Fi[h, m, c, :], lambda h, m, c, e: DTi[h, m, c, :])\
                    .then_inc(S["dft_ready"], 1)
        pe.wait_ge(S["dt_added"], 4 * len(LEVELS))
        pe.wait_ge(S["v_ready"], 1)
        for c in range(NCH):
            for m in range(HM):
                for e in range(2):
                    mm = pe.matmul(PS[HALF[1 - e], 4 + c, m * C:(m + 1) * C], zv[HALF[e], m, c * C:(c + 1) * C],
                                   eye64[HALF[e]], start=True, stop=True)
            mm.then_inc(S["v_turned"], 1)
        pe.wait_ge(S["v_placed"], NCH)
        pe.wait_ge(S["at_placed"], 2)
        for c in range(NCH):
            pe.wait_ge(S["s_placed0"], c + 1)
            pe.wait_ge(S["s_placed1"], c + 1)
            for m in range(HM):
                for e in range(2):
                    mm = pe.matmul(PS[HALF[e], 0, m * C:(m + 1) * C], G[:, m, e, c, 0:C], UV(c)[:, m, e, :],
                                   start=True, stop=True)
            mm.then_inc(S["zc_ready"], 1)
            pe.wait_ge(S["zc_copied"], c + 1)
            for m in range(HM):
                for e in range(2):
                    mm = pe.matmul(PS[HALF[e], 1, m * C:(m + 1) * C], DTi[HALF[e], m, c, :], ZSB[HALF[e], m, :],
                                   start=True, stop=True)
            mm.then_inc(S["u_ready"], 1)
            pe.wait_ge(S["u_placed0"], c + 1)
            pe.wait_ge(S["u_placed1"], c + 1)
            if c < NCH - 1:
                for m in range(HM):
                    for e in range(2):
                        mm = pe.matmul(PS[HALF[e], 2, m * C:(m + 1) * C], BKtok(c)[:, m, e * C:(e + 1) * C],
                                       UV(c)[:, m, e, :], start=True, stop=True)
                mm.then_inc(S["s_ready"], 1)
            for m in range(HM):
                for e in range(2):
                    y = PS[HALF[c % 2], 4 + 2 * (c // 2) + e, m * C:(m + 1) * C]
                    pe.matmul(y, AR[HALF[e], m, c, C:P], SD[c % 2][HALF[e], m, :], start=True, stop=False)
                    mm = pe.matmul(y, G[:, m, e, c, C:P], UV(c)[:, m, e, :], start=False, stop=True)
            mm.then_inc(S["y_ready"], 1)
        pe.wait_ge(S["gup_loaded"], 32)
        for m in range(HM):
            dst = PS[:, m // 2, m % 2 * T:(m % 2 + 1) * T]
            pe.matmul(dst, gup[:, m * P:(m + 1) * P], Z[:, 25, 1:ZW], start=True, stop=False)
            mm = pe.matmul(dst, gup2[:, m * P:(m + 1) * P], Z[0:32, 26, 1:ZW], start=False, stop=True)
        mm.then_inc(S["w_used"], 4)
        pe.wait_ge(S["y_copied"], 2)
        for t in range(TT):
            pe.wait_ge(S["yn_ready"], t + 1)
            for m in range(HM):
                at = m % 2 * T + t * P
                mm = pe.transpose(PS[:, 4 + m // 2, at:at + P], Ytok[:, t, m * P:(m + 1) * P], ident)
        mm.then_inc(S["yn_turned"], 1)

        pe.wait_ge(S["sum_step"], 2)
        with pe.Fori(0, 2) as i:
            for j in range(2):
                pe.wait_ge(S["sum_step"], i * 2 + (SUM["out"] + j - 1))
                split_tokens(N_OUT + j, pair[j], lambda k: XH[:, k, :], lambda k: actT[:, k, :], i)
        norm("n2")
        with pe.Fori(0, F1_PARTS) as i:
            for c in range(4):
                if c < 2:
                    pe.wait_ge(S["sum_step"], i * 4 + (SUM["ffn1"] - 1 + c))
                else:
                    pe.wait_ge(S["ffn1_relu"], i * 4 + (c - 1))
                split_rows(N_F1 + c, c % 2, i, 8)
            for g in range(4):
                if g < 2:
                    pe.wait_ge(S["ffn1_relu"], i * 4 + (3 + g))
                else:
                    pe.wait_ge(S["sum_step"], i * 4 + (SUM["ffn1"] + g - 1))
                split_tokens(N_F1 + 4 + g, pair[g % 2], lambda k: HTH[:, k, :], lambda k: HTL[:, k, :], i, 8,
                             ready=(lambda q: pe.wait_ge(S["ffn1_low"], i * 4 + (q + 1))) if g == 0 else None)
        pe.wait_ge(S["ptok_loaded"], 16)
        for t in range(TT):
            for k in range(2):
                mm = pe.transpose(PS[:, 4, k * T + t * P:k * T + (t + 1) * P], ptok[:, t, k * P:(k + 1) * P], ident)
        mm.then_inc(S["side_turned"], 1)
        pe.wait_ge(S["side_copied"], 1)
        norm("n3")
        pe.wait_ge(S["pproj_loaded"], 16)
        with pe.Fori(0, 2) as i:
            for j in range(2):
                pe.wait_ge(S["sum_step"], i * 2 + (SUM["gate"] + j - 1))
                split_tokens(N_GATE + j, pair[j], lambda k: XH[:, k, :], lambda k: actT[:, k, :], i)
                for t in range(TT):
                    for k in range(2):
                        mm = pe.matmul(PS[:, 4 + 2 * j + t, :], pT[:, k, t * P:(t + 1) * P],
                                       pproj[:, k, bass.ds(i * (2 * CW) + j * CW, CW)], start=(k == 0), stop=(k == 1))
                mm.then_inc(S["proj_ready"], 1)

        norm("n4")
        pe.wait_ge(S["sw_loaded"], 32)
        for k in range(KT):
            mm = pe.matmul(PS[0:16, 4, 0:T], SW[:, k, 0:16], actT[:, k, :], start=(k == 0), stop=(k == KT - 1))
        mm.then_inc(S["low_rank"], 1)
        for t in range(TT):
            for k in range(KT):
                mm = pe.matmul(PS[:, 5, t * 24:t * 24 + 24], actT[:, k, t * P:(t + 1) * P], SW[:, k, 16:40],
                               start=(k == 0), stop=(k == KT - 1))
        mm.then_inc(S["low_rank"], 1)
        with pe.Fori(0, 2) as i:
            for j in range(2):
                n = N_GLA + j
                loaded(n, i)
                pe.wait_ge(S["n4_act"], i * 2 + (j + 3))
                chunk_rows(n, j).then_inc(S["w_used"], 4)
        pe.wait_ge(S["side_copied"], 2)
        pe.wait_ge(S["gw2_loaded"], 16)
        for h in range(GH):
            mm = pe.matmul(PS[:, 6 + h // 2, h % 2 * T:(h % 2 + 1) * T], GW2[:, h * P:(h + 1) * P], LR, start=True, stop=True)
        mm.then_inc(S["low_rank"], 1)
        with pe.Fori(0, 2) as i:
            for j in range(2):
                n = N_GOQ + j
                loaded(n, i)
                pe.wait_ge(S["n4_act"], i * 2 + (j + 7))
                chunk_rows(n, j).then_inc(S["w_used"], 4)
        def gla_scores(n):
            lhs, rhs = (CV[:, 4:8, :], CV[:, 0:4, :]) if n == 0 else (WD[(n - 1) % 2],) * 2
            if n == 0:
                pe.wait_ge(S["silu_qk"], 1)
                pe.wait_ge(S["lb_in"], 1)
                pe.wait_ge(S["side_copied"], 3)
            else:
                pe.wait_ge(S["level_ready"], n)
            if n >= 4:
                pe.wait_ge(S["gsc_masked"], n - 3)
            for c in range(NCH):
                for h in range(GH):
                    at = (h * TT + c // 2) * C
                    mm = pe.matmul(PS[HALF[c % 2], 4 + n % 4, at:at + C], lhs[:, h, c * C:(c + 1) * C],
                                   rhs[:, h, c * C:(c + 1) * C], start=True, stop=True)
            mm.then_inc(S["gsc_ready"], 1)

        for n in range(3):
            gla_scores(n)
        loaded(N_KCVC)
        pe.wait_ge(S["n4_act"], 11)
        chunk_rows(N_KCVC, 0).then_inc(S["w_used"], 4)
        for n in (N_KSVS, N_KWVW):
            g = n % 2
            gla_scores(3 + 2 * (n - N_KSVS))
            gla_scores(4 + 2 * (n - N_KSVS))
            loaded(n)
            pe.wait_ge(S["n4_act"], 12 + n - N_KSVS)
            chunk_rows(n, g, 2)
            for t in range(TT):
                for k in range(KT):
                    mm = pe.matmul(pair[g][:, 1, t * T:(t + 1) * T], actT[:, k, t * P:(t + 1) * P],
                                   slot(n % 2)[:, k, 256:512], start=(k == 0), stop=(k == KT - 1))
            mm.then_inc(S["w_used"], 4)
        pe.wait_ge(S["gqk_ready"], 1)
        pe.wait_ge(S["gsc_masked"], len(GLA_HALF) + 1)
        for t in range(TT):
            for h in range(GH):
                mm = pe.transpose(PS[:, 6 + t, h * P:(h + 1) * P], K4[:, h, t * P:(t + 1) * P], ident)
        mm.then_inc(S["gk_turned"], 1)
        pe.wait_ge(S["gv_ready"], 1)
        pe.wait_ge(S["n4_act"], 15)
        for t in range(TT):
            for m in range(8):
                mm = pe.transpose(PS[:, 2 * t + m // 4, m % 4 * P:(m % 4 + 1) * P], CV[:, 8 + m, t * P:(t + 1) * P], ident)
        mm.then_inc(S["gv_turned"], 1)
        pe.wait_ge(S["gsc_summed"], len(GLA_HALF))
        pe.wait_ge(S["gkv_copied"], 3)
        for c in range(NCH):
            t, hf = c // 2, HALF[c % 2]
            if c:
                pe.wait_ge(S["gs_step"], GH * c)
            for h in range(GH):
                o = PS[hf, 2 * t + h // 2, h % 2 * GDV:(h % 2 + 1) * GDV]
                if c:
                    pe.matmul(o, Q1[:, h, c * C:(c + 1) * C], GS[:, h, :], start=True, stop=False)
                mm = pe.matmul(o, SCT[hf, h, t, :], VTOK[hf, t, h * GDV:(h + 1) * GDV], start=(c == 0), stop=True)
            mm.then_inc(S["go_ready"], 1)
            if c < NCH - 1:
                for h in range(GH):
                    mm = pe.matmul(PS[:, 6 + h // 2, h % 2 * GDV:(h % 2 + 1) * GDV], KTOK[hf, t, h, :],
                                   VTOK[hf, t, h * GDV:(h + 1) * GDV], start=True, stop=True)
                mm.then_inc(S["gs_ready"], 1)
        pe.wait_ge(S["gs_step"], GH * (NCH - 1))
        for t in range(TT):
            pe.wait_ge(S["on_ready"], t + 1)
            for m in range(8):
                at = m % 2 * T + t * P
                mm = pe.transpose(PS[:, 4 + m // 2, at:at + P], OT[:, t, m * P:(m + 1) * P], ident)
        mm.then_inc(S["on_turned"], 1)
        pe.wait_ge(S["pos_loaded"], 64)
        for i in range(2):
            mm = pe.transpose(PS[:, 0, i * CB:(i + 1) * CB], PTAB[i], ident[0:CB, 0:CB])
        mm.then_inc(S["side_turned"], 1)
        loaded(N_CMP)
        cw = slot(N_CMP % 2).rearrange("p k n -> p (k n)").rearrange("p (s l h) -> p s l h", s=2, l=CB)
        pe.wait_ge(S["xc_ready"], 1)
        pe.wait_ge(S["side_copied"], 5)
        for i in range(2):
            for l in range(CB):
                mm = pe.matmul(PS[:, 1, i * 31:(i + 1) * 31], cw[:, i, l, :], XC[i][:, l, :], start=(l == 0), stop=(l == CB - 1))
        mm.then_inc(S["w_used"], 4)
        pe.wait_ge(S["nsq_ready"], 1)
        for t in range(TT):
            for h in range(NH):
                mm = pe.matmul(PS[:, 2, t * NH + h:t * NH + h + 1], SQ[:, h, t * P:(t + 1) * P], con("ones")[:, 0:1],
                               start=True, stop=True)
        for i in range(2):
            mm = pe.matmul(PS[:, 3, :] if i else PS[:, 0, :], con("ones"), SQ[:, 8 + 2 * i:10 + 2 * i, :].rearrange("p a b -> p (a b)"),
                           start=True, stop=True)
        mm.then_inc(S["k_sums"], 1)
        pe.wait_ge(S["hid_ready"], 2)
        pe.matmul(PS[:, 1, 0:2 * NB], CW2[0], HID[0], start=True, stop=True)
        for kv in range(KVH):
            mm = pe.matmul(PS[0:NB, 1, P + kv * DH:P + (kv + 1) * DH], HID[1][:, kv * NB:(kv + 1) * NB], CW2[1], start=True, stop=True)
        mm.then_inc(S["cmp_ready"], 1)
        pe.wait_ge(S["kc_squared"], 1)
        pe.matmul(PS[:, 2, 0:2 * NB], con("ones"), KCSQ, start=True, stop=True).then_inc(S["k_sums"], 1)
        pe.wait_ge(S["nk_ready"], 3)
        pe.wait_ge(S["on_read"], 1)
        for t in range(TT):
            if t:
                pe.wait_ge(S["cs_read"], 1)
            for h in range(NH):
                mm = pe.matmul(PS[:, 2, h * NB:(h + 1) * NB], GOQ[:, 8 + h, t * P:(t + 1) * P],
                               KCMP[:, h // GRP * NB:(h // GRP + 1) * NB], start=True, stop=True)
            mm.then_inc(S["cs_ready"], 1)
            nk = (t + 1) * P
            for s in range(2):
                for h in range(NH):
                    u = (t * 2 + s) * NH + h
                    if u >= 4:
                        pe.wait_ge(S["sc_read"], u - 3)
                    pe.matmul(PS[:, 4 + u % 4, 0:nk], GOQ[:, 8 + h, t * P:(t + 1) * P], NK[:, 4 + 2 * s + h // GRP, 0:nk],
                              start=True, stop=True).then_inc(S["sc_ready"], 1)
        pe.wait_ge(S["sc_read"], 32)
        pe.wait_ge(S["side_copied"], 6)
        g = 0
        for t in range(TT):
            for kv in range(KVH):
                o = PS[:, kv, :]
                if t:
                    pe.wait_ge(S["att_out"], kv + 1)
                parts = [(2, 0)] + [(s, kt) for s in range(2) for kt in range(t + 1)]
                for q, (s, kt) in enumerate(parts):
                    if g >= 4:
                        pe.wait_ge(S["pt_copied"], g - 3)
                    pe.wait_ge(S["prob_ready"], t * 3 + s + 1)
                    for j in range(GRP):
                        h = kv * GRP + j
                        if s == 2:
                            mm = pe.transpose(PS[0:NB, 4 + g % 4, j * P:(j + 1) * P], PCM[:, t, h, :], ident)
                        else:
                            mm = pe.transpose(PS[:, 4 + g % 4, j * P:(j + 1) * P], PSW[t][:, s, h, kt * P:(kt + 1) * P], ident)
                    mm.then_inc(S["pt_ready"], 1)
                    g += 1
                g -= len(parts)
                for q, (s, kt) in enumerate(parts):
                    pe.wait_ge(S["pt_copied"], g + 1)
                    if s == 2:
                        mm = pe.matmul(o, VCMP[:, kv, :], PTC[g % 4], start=True, stop=False)
                    else:
                        mm = pe.matmul(o, VSW[:, s, kt, kv * DH:(kv + 1) * DH], PTR[g % 4], start=False, stop=(q == len(parts) - 1))
                    mm.then_inc(S["pt_used"], 1)
                    g += 1

        pe.wait_ge(S["gla_low"], 1)
        pe.wait_ge(S["att_out"], TT * KVH)
        with pe.Fori(0, 2) as i:
            for j in range(2):
                pe.wait_ge(S["sum_step"], i * 2 + (SUM["out2"] + j - 1))
                split_tokens(N_OUT2 + j, pair[j], lambda k: XH2[:, k, :], lambda k: actT[:, k, :], i)
        norm("n5")

        def ffn2_part(n, groups, silus, sums, i=None, per=F2_N):
            def at(v, step):
                return v if i is None else i * step + v

            units = UNITS[groups]
            for m in range(groups):
                if m == 0:
                    pe.wait_ge(S["sum_step"], at(sums - 1, 4))
                else:
                    pe.wait_ge(S["ffn2_silu"], at(silus + m, F2_GROUPS))
                split_rows(n + 2 * m, 0, i, per)
                if m == 0:
                    pe.wait_ge(S["sum_step"], at(sums, 4))
                else:
                    pe.wait_ge(S["ffn2_mul"], at(silus + m, F2_GROUPS))
                split_rows(n + 2 * m + 1, 1, i, per)
            for g in range(4):
                if g < 2:
                    pe.wait_ge(S["ffn2_silu" if g == 0 else "ffn2_mul"], at(silus + groups, F2_GROUPS))
                else:
                    pe.wait_ge(S["sum_step"], at(sums + g - 1, 4))
                split_tokens(n + 2 * groups + g, pair[g % 2], lambda k: HTH[:, k, :], lambda k: HTL[:, k, :], i, per, units,
                             (lambda q: pe.wait_ge(S["ffn2_low"], at(silus + q + 1, F2_GROUPS))) if g == 0 else None)

        with pe.Fori(0, F2_PARTS) as i:
            ffn2_part(N_F2, F2_GROUPS, 0, SUM["ffn2"], i)
        ffn2_part(N_F2 + F2_PARTS * F2_N, F2_LAST, F2_PARTS * F2_GROUPS, SUM["ffn2"] + 4 * F2_PARTS)

    @block.scalar
    def _(act):
        steps = [0]

        def link(ins):
            steps[0] += 1
            ins.then_inc(S["act_step"], 1)
            act.wait_ge(S["act_step"], steps[0])

        def copy(dst, src, scale=1.0):
            return act.activation(dst, src, ACT.Copy, scale=scale)

        def square_sum(p):
            act.activation(XN[p][:, 0, :], xs[:, 0, :], ACT.Square, accum_out=ss[:, 0:1]).then_inc(S["norm_sum0"], 1)

        def root(p):
            act.wait_ge(S["norm_mean"], RMS[p])
            act.activation(sq, ms, ACT.Sqrt).then_inc(S["norm_root"], 1)

        def norm(p, gain):
            square_sum(p)
            root(p)
            for j in range(0 if p in XSPLIT else 1, KT // 2, 1 if p in XSPLIT else 2):
                act.wait_ge(S["norm_turned"], KT // 2 * NORMS[p] + j + 1)
                for q in range(2):
                    k = 2 * j + q
                    dst = r32(XH[:, k, :]) if p in XSPLIT else actT[:, k, :]
                    ins = copy(dst, PS[:, 4 + j % 4, q * T:(q + 1) * T], col(gain, k))
                ins.then_inc(S["x_high" if p in XSPLIT else f"{p}_act"], 1)

        def high(n, js, i=None, per=2, units=UNITS[4]):
            for j in js:
                if j % 2 == 0:
                    v = 16 * (n // 2 + 1)
                    act.wait_ge(S[f"w_loaded{2 * (n % 2) + j // 2}"], v if i is None else i * (8 * per) + v)
                act.wait_ge(S["w_used"], used(n - 1, i, per, j + 1))
                copy(r32(HIW[j]), unit_at(n % 2, j)).then_inc(S["w_high"], counts(units, j))

        act.dma_start(xs[:, 0, :], xin[:, 0, :]).then_inc(S["x0_loaded"], 16)
        act.dma_start(xs[:, 1, :], xin[:, 1, :]).then_inc(S["x1_loaded"], 16)
        act.wait_ge(S["side_turned"], 1)
        copy(pcol[:], PS[:, 0, 0:2 * P]).then_inc(S["z_copied"], 1)
        act.wait_ge(S["z_copied"], 1)
        act.wait_ge(S["x0_loaded"], 16)
        norm("n1", "attn_norm")
        act.wait_ge(S["w_used"], used(N_WAG))
        copy(Z[:, 24:26, 1:ZW], half(0)[:, 0:2, :])
        copy(Z[0:32, 26, 1:ZW], half(0)[0:32, 2, :]).then_inc(S["z_copied"], 1)
        act.wait_ge(S["wag_shifted"], 1)
        act.activation(Z[LO, 24, 1:ZW], Z[LO, 24, 1:ZW], ACT.Tanh).then_inc(S["wa_ready"], 1)
        act.activation(Z[:, 25, 1:ZW], Z[:, 25, 1:ZW], ACT.Sigmoid)
        act.activation(Z[0:32, 26, 1:ZW], Z[0:32, 26, 1:ZW], ACT.Sigmoid).then_inc(S["wa_ready"], 1)
        with act.Fori(0, 3) as i:
            for j in range(2):
                n = N_RKV + j
                act.wait_ge(S["w_used"], used(n, i))
                copy(Z[:, bass.ds(i * 8 + 4 * j, 4), 1:ZW], half(n % 2)).then_inc(S["z_copied"], 1)
        act.wait_ge(S["head_sums"], 1)
        for m in range(HM):
            ins = act.activation(lw[:, m, :], PS[:, 4 + m // 2, m % 2 * T:(m % 2 + 1) * T], ACT.Sigmoid, bias=col("w0", m))
        ins.then_inc(S["head_acts"], 1)
        act.wait_ge(S["head_sums"], 2)
        for m in range(HM):
            ins = act.activation(ga[:, m, :], PS[:, m // 2, m % 2 * T:(m % 2 + 1) * T], ACT.Sigmoid, bias=col("a0", m))
        ins.then_inc(S["head_acts"], 1)
        act.wait_ge(S["head_sums"], 3)
        act.wait_ge(S["v_ready"], 1)
        act.activation(tmp1.rearrange("p m t -> p (m t)"), PS[:, 4:8, :].rearrange("p b n -> p (b n)"), ACT.Sqrt)\
            .then_inc(S["head_acts"], 1)
        act.wait_ge(S["lc_ready"], 1)
        link(act.activation(tmp2, lw, ACT.Exp, scale=KAPPA))
        act.activation(lw, lw, ACT.Exp, scale=-KAPPA).then_inc(S["head_acts"], 1)
        for n in range(N_POOL, N_POOL + 2):
            act.wait_ge(S["w_used"], used(n))
            copy(ZP[:, 4 * (n - N_POOL):4 * (n - N_POOL) + 4, 16:PW], half(n % 2)).then_inc(S["z_copied"], 1)
        for g in range(2 * NCH):
            c, m0 = g // 2, g % 2 * 4
            act.wait_ge(S["bk_turned"], g + 1)
            copy(BKtok(c)[:, m0:m0 + 4, :], PS[:, 4 + g % 4, :].rearrange("p (m j) -> p m j", m=4)).then_inc(S["bk_copied"], 1)
        act.wait_ge(S["pool_sums"], 1)
        for m in range(HM):
            ins = copy(actT[:, m, :], PS[:, 4 + m // 2, m % 2 * T:(m % 2 + 1) * T], col("pool_scale", m))
        ins.then_inc(S["pool_out"], 1)
        for g in range(4):
            act.wait_ge(S["d_turned"], g + 1)
            copy(Di[:, 2 * g:2 * g + 2].rearrange("p m c j -> p (m c j)"), PS[:, g, :]).then_inc(S["d_ready"], 1)
        for c in range(NCH):
            act.wait_ge(S["v_turned"], c + 1)
            for e in range(2):
                h = HALF[1 - e]
                ins = copy(UV(c)[h, :, e, :], PS[h, 4 + c, :].rearrange("p (m i) -> p m i", m=HM))
            ins.then_inc(S["v_placed"], 1)
        for c in range(NCH):
            act.wait_ge(S["u_ready"], c + 1)
            copy(UV(c)[LO, :, 0, :], PS[LO, 1, :].rearrange("p (m i) -> p m i", m=HM)).then_inc(S["u_placed0"], 1)
            if c < NCH - 1:
                act.wait_ge(S["sd_ready"], c + 1)
                copy(UV(c + 1)[LO, :, 0, :], SD[(c + 1) % 2][LO]).then_inc(S["s_placed0"], 1)
            if c % 2:
                t = c // 2
                act.wait_ge(S["y_ready"], c + 1)
                act.wait_ge(S["bonus_done"], 1)
                copy(Ytok[:, t, :].rearrange("p (m e i) -> p e m i", m=HM, e=2),
                     PS[:, 4 + 2 * t:6 + 2 * t, :].rearrange("p e (m i) -> p e m i", m=HM)).then_inc(S["y_copied"], 1)
        for t in range(TT):
            act.wait_ge(S["gn_var"], t + 1)
            act.activation(gns, gnv, ACT.Sqrt).then_inc(S["gn_root"], 1)
        act.wait_ge(S["y_ready"], NCH)
        high(N_OUT, (0, 1, 2))
        for h in range(2):
            if h:
                act.wait_ge(S["mixed"], 1)
            copy(r32(XH[:, 8 * h:8 * h + 8, :]), actT[:, 8 * h:8 * h + 8, :]).then_inc(S["mixed_high"], 1)
        with act.Fori(0, 2) as i:
            for j in range(2):
                high(N_OUT + j, (3,), i)
                high(N_OUT + j + 1, (0, 1, 2), i)
        act.wait_ge(S["sum_step"], SUM["ffn1"])
        norm("n2", "mlp_norm")
        with act.Fori(0, F1_PARTS) as i:
            for c in range(8):
                n = N_F1 + c
                high(n, (3,), i, 8)
                high(n + 1, (0, 1, 2), i, 8)
                if c < 4:
                    act.wait_ge(S["w_used"], used(n, i, 8))
                    act.activation(by_half(RQ[c % 2]), out_rows(c % 2), ACT.Relu).then_inc(S["ffn1_relu"], 1)
        act.wait_ge(S["side_turned"], 2)
        copy(pT.rearrange("p k t -> p (k t)"), PS[:, 4, :]).then_inc(S["side_copied"], 1)
        act.wait_ge(S["sum_step"], SUM["gate"])
        norm("n3", "ple_norm")
        for c in range(4):
            n = N_GATE + c
            high(n, (3,))
            if c < 3:
                high(n + 1, (0, 1, 2))
            act.wait_ge(S["w_used"], used(n))
            if c >= 2:
                act.wait_ge(S["sum_step"], SUM["gate"] + c - 1)
            act.activation(gate_sb[c % 2], pair[c % 2], ACT.Sigmoid).then_inc(S["gate_ready"], 1)
        act.wait_ge(S["sum_step"], SUM["out2"])
        square_sum("fin")
        root("fin")

        act.wait_ge(S["fin_done"], 2)
        norm("n4", "attn_norm_g_2")
        act.wait_ge(S["low_rank"], 1)
        copy(LR, PS[0:16, 4, 0:T]).then_inc(S["side_copied"], 1)
        act.wait_ge(S["low_rank"], 2)
        act.activation(gates.rearrange("p t n -> p (t n)"), PS[:, 5, 0:48], ACT.Sigmoid).then_inc(S["side_copied"], 1)
        with act.Fori(0, 2) as i:
            for j in range(2):
                act.wait_ge(S["w_used"], used(N_GLA + j, i))
                copy(ZG[:, bass.ds(i * 8 + 4 * j, 4), 3:T + 3], half(j)).then_inc(S["n4_act"], 1)
        act.wait_ge(S["lb_in"], 1)
        link(act.activation(Q1, LB, ACT.Abs))
        link(act.activation(Q1, Q1, ACT.Exp, scale=-1.0))
        act.activation(Q1, Q1, ACT.Ln, bias=1.0).then_inc(S["la_soft"], 1)
        act.wait_ge(S["conv_done"], 1)
        act.activation(CV[:, 0:8, :], CV[:, 0:8, :], ACT.Silu).then_inc(S["silu_qk"], 1)
        act.wait_ge(S["conv_done"], 2)
        act.activation(CV[:, 8:16, :], CV[:, 8:16, :], ACT.Silu).then_inc(S["gv_ready"], 1)
        act.wait_ge(S["gd_ready"], 1)
        lbc = LB.rearrange("p h (c j) -> p h c j", c=NCH)
        act.activation(GE[0], LB, ACT.Exp, scale=1 / GTAU)
        act.activation(GE[1], GE[1], ACT.Exp, scale=1 / GTAU)
        act.activation(GDEC, lbc[:, :, :, C - 1], ACT.Exp, scale=1 / GTAU).then_inc(S["gexp_ready"], 1)

        def level_exps(*levels):
            for n in levels:
                act.wait_ge(S["level_diff"], n + 1)
                act.activation(WD[n % 2], WD[n % 2], ACT.Exp, scale=1 / GTAU).then_inc(S["level_exp"], 1)

        level_exps(0, 1)
        with act.Fori(0, 2) as i:
            for j in range(2):
                act.wait_ge(S["w_used"], used(N_GOQ + j, i))
                copy(GOQ[:, bass.ds(i * 8 + 4 * j, 4), :], half(j)).then_inc(S["n4_act"], 1)
        act.wait_ge(S["n4_act"], 12)
        act.activation(GOQ[:, 0:8, :], GOQ[:, 0:8, :], ACT.Silu).then_inc(S["gout_ready"], 1)
        level_exps(2, 3)
        act.wait_ge(S["w_used"], used(N_KCVC))
        copy(NK[:, 0:4, :], half(0)).then_inc(S["n4_act"], 1)
        level_exps(4, 5)
        for n in (N_KSVS, N_KWVW):
            s = n - N_KSVS
            act.wait_ge(S["w_used"], used(n))
            copy(NK[:, 4 + 2 * s:6 + 2 * s, :], half(n % 2)[:, 0:2, :])
            copy(VSW[:, s], half(n % 2)[:, 2:4, :]).then_inc(S["n4_act"], 1)
        act.wait_ge(S["gk_turned"], 1)
        copy(KTOK.rearrange("p t h d -> p (t h d)"), PS[:, 6:8, :].rearrange("p b n -> p (b n)")).then_inc(S["gkv_copied"], 1)
        act.wait_ge(S["gv_turned"], 1)
        for t in range(TT):
            copy(VTOK[:, t, :], PS[:, 2 * t:2 * t + 2, :].rearrange("p b n -> p (b n)")).then_inc(S["gkv_copied"], 1)
        for t in range(TT):
            act.wait_ge(S["go_ready"], 2 * t + 2)
            copy(OT[:, t, :], PS[:, 2 * t:2 * t + 2, :].rearrange("p b n -> p (b n)")).then_inc(S["o_copied"], 1)
        for t in range(TT):
            act.wait_ge(S["gn_var"], TT + t + 1)
            act.activation(small[:, 32:36], small[:, 28:32], ACT.Sqrt).then_inc(S["gn_root"], 1)
        act.wait_ge(S["side_turned"], 3)
        for i in range(2):
            copy(XC[i][:, :, 30:31], PS[:, 0, i * CB:(i + 1) * CB].unsqueeze(2)).then_inc(S["side_copied"], 1)
        act.wait_ge(S["w_used"], used(N_CMP))
        for i in range(2):
            link(copy(HB[i][:, 0:1], PS[:, 1, i * 31 + 30:i * 31 + 31]))
            act.activation(HID[i], PS[:, 1, i * 31:i * 31 + 30], ACT.Silu, bias=HB[i][:, 0:1]).then_inc(S["hid_ready"], 1)
        act.wait_ge(S["k_var"], 1)
        act.activation(QRS, QRS, ACT.Sqrt)
        act.activation(SQ[:, 0:4, :], SQ[:, 0:4, :], ACT.Sqrt).then_inc(S["k_root"], 1)
        act.wait_ge(S["cmp_ready"], 1)
        copy(VCMP.rearrange("p v d -> p (v d)"), PS[0:NB, 1, P:P + KVH * DH]).then_inc(S["side_copied"], 1)
        act.wait_ge(S["on_read"], 1)
        copy(r32(XH2[:, 0:8, :]), actT[:, 0:8, :]).then_inc(S["gla_high"], 1)
        act.wait_ge(S["k_var"], 2)
        act.activation(KCSQ, KCSQ, ACT.Sqrt).then_inc(S["k_root"], 1)
        for t in range(TT):
            for s in range(3):
                act.wait_ge(S["max_ready"], t * 3 + s + 1)
                for h in range(NH):
                    a = PCM[:, t, h, :] if s == 2 else PSW[t][:, s, h, :]
                    ins = act.activation(a, a, ACT.Exp, bias=MX[:, t, s, h:h + 1], accum_out=SM[:, t, s, h:h + 1])
                ins.then_inc(S["exp_done"], 1)
        high(N_OUT2, (0, 1, 2))
        g = 0
        for t in range(TT):
            for kv in range(KVH):
                for s, kt in [(2, 0)] + [(s, kt) for s in range(2) for kt in range(t + 1)]:
                    act.wait_ge(S["pt_ready"], g + 1)
                    if g >= 4:
                        act.wait_ge(S["pt_used"], g - 3)
                    if s == 2:
                        ins = copy(PTC[g % 4], PS[0:NB, 4 + g % 4, :])
                    else:
                        ins = copy(PTR[g % 4], PS[:, 4 + g % 4, :])
                    ins.then_inc(S["pt_copied"], 1)
                    g += 1
                act.wait_ge(S["pt_used"], g)
                k = 8 + kv * GRP
                copy(r32(XH2[:, k:k + GRP, t * P:(t + 1) * P]), PS[:, kv, :].rearrange("p (h t) -> p h t", h=GRP))\
                    .then_inc(S["att_high"], 1)
        with act.Fori(0, 2) as i:
            for j in range(2):
                high(N_OUT2 + j, (3,), i)
                high(N_OUT2 + j + 1, (0, 1, 2), i)
        act.wait_ge(S["sum_step"], SUM["ffn2"])
        norm("n5", "ffn_norm_g_2")

        def ffn2_part(n0, groups, i=None, last=False):
            plan = [UNITS[4]] * (2 * groups) + [UNITS[groups]] * 4 + [UNITS[4]]
            for c, (units, after) in enumerate(zip(plan, plan[1:])):
                n = n0 + c
                high(n, units[-1:], i, F2_N, units)
                if not (last and c == len(plan) - 2):
                    high(n + 1, after[:-1], i, F2_N, after)
                if c < 2 * groups and c % 2 == 0:
                    act.wait_ge(S["w_used"], used(n, i, F2_N))
                    act.activation(by_half(RQ[0]), out_rows(0), ACT.Silu).then_inc(S["ffn2_silu"], 1)

        with act.Fori(0, F2_PARTS) as i:
            ffn2_part(N_F2, F2_GROUPS, i)
        ffn2_part(N_F2 + F2_PARTS * F2_N, F2_LAST, last=True)

    @block.vector
    def _(v):
        steps = [0]

        def link(ins):
            steps[0] += 1
            ins.then_inc(S["dve_step"], 1)
            v.wait_ge(S["dve_step"], steps[0])

        def rms(p):
            link(v.tensor_tensor_reduce(out=XN[p][:, 1, :], in0=xs[:, 1, :], in1=xs[:, 1, :], scale=1.0, scalar=0.0,
                                        op0=ALU.mult, op1=ALU.add, accum_out=ss[:, 1:2]))
            v.wait_ge(S["norm_sum0"], RMS[p])
            v.tensor_scalar(ms, ss, 1.0 / D, EPS, ALU.mult, ALU.add).then_inc(S["norm_mean"], 1)
            v.wait_ge(S["norm_root"], RMS[p])
            link(v.reciprocal(rs, sq))

        def norm(p, gain):
            rms(p)
            for t in range(TT):
                v.tensor_scalar(XN[p][:, t, :], xs[:, t, :], rs[:, t:t + 1], None, ALU.mult).then_inc(S["norm_xn"], 1)
            for j in range(0, KT // 2, 1 if p in XSPLIT else 2):
                if p in XSPLIT:
                    v.wait_ge(S["x_high"], XSPLIT[p] + j + 1)
                else:
                    v.wait_ge(S["norm_turned"], KT // 2 * NORMS[p] + j + 1)
                for q in range(2):
                    k = 2 * j + q
                    src = PS[:, 4 + j % 4, q * T:(q + 1) * T]
                    if p in XSPLIT:
                        ins = v.scalar_tensor_tensor(r32(actT[:, k, :]), src, col(gain, k), high_of(XH[:, k, :]), ALU.mult, ALU.subtract)
                    else:
                        ins = v.tensor_scalar(actT[:, k, :], src, col(gain, k), None, ALU.mult)
                ins.then_inc(S["x_low" if p in XSPLIT else f"{p}_dve"], 1)

        def low(n, js, i=None, per=2, units=UNITS[4]):
            for j in js:
                v.wait_ge(S["w_high"], split_count(n, j, i, per) + (counts(units, j) - 1))
                u = unit_at(n % 2, j)
                v.tensor_tensor(r32(u), u, high_of(HIW[j]), ALU.subtract).then_inc(S["w_low"], counts(units, j))

        def add_out(w, g, at):
            v.wait_ge(S["w_used"], w)
            r = xs[:, :, at if isinstance(at, slice) else bass.ds(at, CW)]
            v.tensor_tensor(r, pair[g], r, ALU.add).then_inc(S["sum_step"], 1)

        v.wait_ge(S["x1_loaded"], 16)
        v.wait_ge(S["x0_loaded"], 16)
        v.wait_ge(S["z_copied"], 1)
        norm("n1", "attn_norm")
        mu = COL["mu_shift"]
        v.wait_ge(S["zeroed"], 2)
        v.wait_ge(S["z_copied"], 2)
        v.tensor_tensor(tmp1[:, 0:2, :], Z[:, 24:26, 0:T], Z[:, 24:26, 1:ZW], ALU.subtract)
        link(v.tensor_tensor(tmp1[0:32, 2, :], Z[0:32, 26, 0:T], Z[0:32, 26, 1:ZW], ALU.subtract))
        for q, n in ((0, P), (1, P), (2, 32)):
            z = Z[0:n, 24 + q, 1:ZW]
            ins = v.scalar_tensor_tensor(z, tmp1[0:n, q, :], pcol[0:n, mu + 24 + q:mu + 25 + q], z, ALU.mult, ALU.add)
        ins.then_inc(S["wag_shifted"], 1)
        v.wait_ge(S["wag_shifted"], 1)
        for q in range(3):
            v.wait_ge(S["z_copied"], 4 + 2 * q)
            link(v.tensor_tensor(tmp1, Z[:, 8 * q:8 * q + 8, 0:T], Z[:, 8 * q:8 * q + 8, 1:ZW], ALU.subtract))
            for m in range(HM):
                z = Z[:, 8 * q + m, 1:ZW]
                ins = v.scalar_tensor_tensor(z, tmp1[:, m, :], pcol[:, mu + 8 * q + m:mu + 8 * q + m + 1], z, ALU.mult, ALU.add)
            if q < 2:
                link(ins)
            else:
                ins.then_inc(S["v_ready"], 1)
            if q == 1:
                for m in range(HM):
                    ins = v.tensor_scalar(kk[:, m, :], zk[:, m, :], col("k_k", m), None, ALU.mult)
                link(ins)
                v.tensor_tensor(tmp2, kk, kk, ALU.mult).then_inc(S["kk_squared"], 1)
        v.wait_ge(S["head_acts"], 1)
        for m in range(HM):
            ins = v.tensor_tensor_scan(lw[:, m, :], con("keep"), lw[:, m, :], 0.0, ALU.mult, ALU.add)
        ins.then_inc(S["lc_ready"], 1)
        v.wait_ge(S["head_acts"], 3)
        link(v.tensor_scalar(tmp1, tmp1, 1e-12, None, ALU.max))
        link(v.reciprocal(tmp1, tmp1))
        link(v.tensor_tensor(kk, kk, tmp1, ALU.mult))
        v.wait_ge(S["head_acts"], 2)
        for m in range(HM):
            ins = v.tensor_scalar(tmp1[:, m, :], ga[:, m, :], 1.0, col("k_a", m), ALU.subtract, ALU.mult)
        link(ins)
        link(v.scalar_tensor_tensor(zk, tmp1, 1.0, zk, ALU.add, ALU.mult))
        v.tensor_tensor(ga, kk, ga, ALU.mult)
        for m in range(HM):
            ins = v.scalar_tensor_tensor(tmp1[:, m, :], zr[:, m, :], col("r_k", m), zk[:, m, :], ALU.mult, ALU.mult)
        ins.then_inc(S["rkr_ready"], 1)
        v.wait_ge(S["rkr_ready"], 1)
        v.wait_ge(S["head_acts"], 4)
        lwc, kkc = (a.rearrange("p m (c j) -> p (m c) j", c=NCH) for a in (lw, kk))
        arf = AR.rearrange("p m c j -> p (m c) j")
        v.tensor_copy(PEND.rearrange("p m c -> p (m c)"), lwc[:, :, C - 1])
        v.tensor_scalar(arf[:, :, 0:1], kkc[:, :, 0:1], -1.0, None, ALU.mult)
        v.scalar_tensor_tensor(arf[:, :, 1:C], lwc[:, :, 0:C - 1], -1.0, kkc[:, :, 1:C], ALU.mult, ALU.mult)

        def chunks(a):
            return a.rearrange("p m (c j) -> p m c j", c=NCH)

        for e in range(2):
            h = HALF[e]
            v.tensor_tensor(BK[h, :, :, e * C:(e + 1) * C], chunks(ga)[h], chunks(tmp2)[h], ALU.mult)
            ins = v.tensor_tensor(BK[h, :, :, (1 - e) * C:(2 - e) * C], chunks(zk)[h], chunks(tmp2)[h], ALU.mult)
        ins.then_inc(S["bk_ready"], 1)
        v.tensor_tensor(AR[:, :, :, C:P], chunks(zr), chunks(lw), ALU.mult).then_inc(S["ar_ready"], 1)
        v.wait_ge(S["ar_ready"], 1)
        v.wait_ge(S["head_sums"], 4)
        v.tensor_tensor(bonus, PS[:, 4:8, :].rearrange("p b (q t) -> p (b q) t", q=2), zv, ALU.mult).then_inc(S["bonus_ready"], 1)
        v.wait_ge(S["bonus_ready"], 1)
        for m in range(HM):
            ins = v.tensor_scalar(bonus[:, m, :], bonus[:, m, :], col("gn_b", m), None, ALU.add)
        ins.then_inc(S["bonus_done"], 1)
        for g in range(2 * HM):
            m, e = g // 2, g % 2
            v.wait_ge(S["score_ready"], g + 1)
            v.tensor_tensor(G[:, m, e], PS[:, g % 4, :].rearrange("p (c j) -> p c j", c=NCH), over(tri, NCH), ALU.mult)\
                .then_inc(S["score_masked"], 1)
        v.wait_ge(S["score_masked"], 2 * HM)
        for e in range(2):
            h = HALF[e]
            l1 = con("level1")[h].unsqueeze(1).unsqueeze(1).broadcast_to([C, HM, NCH, C])
            ins = v.tensor_tensor(DTi[h], G[h, :, e, :, 0:C], l1, ALU.mult)
        link(ins)
        dtf = DTi.rearrange("p m c j -> p (m c) j")
        v.tensor_tensor(dtf, dtf, over(eye64, HM * NCH), ALU.add).then_inc(S["dt_ready"], 1)
        v.wait_ge(S["dt_ready"], 1)

        def eight(a, g):
            return a[:, 2 * g:2 * g + 2].rearrange("p m c j -> p (m c) j")

        def bank8(b):
            return PS[:, b, :].rearrange("p (q j) -> p q j", q=8)

        for lv in range(len(LEVELS)):
            mask = con("levels")[:, lv * C:(lv + 1) * C]
            for g in range(4):
                v.wait_ge(S["f_ready"], 4 * lv + g + 1)
                v.tensor_tensor(eight(Fi, g), bank8(g), over(mask, 8), ALU.mult).then_inc(S["f_masked"], 1)
            for g in range(4):
                if lv < len(LEVELS) - 1:
                    v.wait_ge(S["df_ready"], 4 * lv + g + 1)
                    v.tensor_tensor(eight(Di, g), bank8(4 + g), eight(Di, g), ALU.add).then_inc(S["d_added"], 1)
                v.wait_ge(S["dft_ready"], 4 * lv + g + 1)
                v.tensor_tensor(eight(DTi, g), bank8(g), eight(DTi, g), ALU.add).then_inc(S["dt_added"], 1)
        v.wait_ge(S["pool_sums"], 1)
        v.memset(SD[0], 0.0)
        for e in range(2):
            v.memset(UV(0)[HALF[e], :, e, :], 0.0).then_inc(S[f"s_placed{e}"], 1)
        for e in range(2):
            h = HALF[e]
            v.tensor_copy(G[h, :, e, :, 0:C], AR[h, :, :, 0:C]).then_inc(S["at_placed"], 1)
        for c in range(NCH):
            v.wait_ge(S["zc_ready"], c + 1)
            v.tensor_copy(ZSB.rearrange("p m i -> p (m i)"), PS[:, 0, :]).then_inc(S["zc_copied"], 1)
            v.wait_ge(S["u_ready"], c + 1)
            v.tensor_copy(UV(c)[HI, :, 1, :], PS[HI, 1, :].rearrange("p (m i) -> p m i", m=HM)).then_inc(S["u_placed1"], 1)
            if c < NCH - 1:
                v.wait_ge(S["s_ready"], c + 1)
                now, then = SD[c % 2], SD[(c + 1) % 2]
                link(v.tensor_tensor(then, PS[:, 2, :].rearrange("p (m i) -> p m i", m=HM), now, ALU.add))
                v.tensor_tensor(then, then, along(PEND[:, :, c], C), ALU.mult).then_inc(S["sd_ready"], 1)
                v.wait_ge(S["sd_ready"], c + 1)
                v.tensor_copy(UV(c + 1)[HI, :, 1, :], then[HI]).then_inc(S["s_placed1"], 1)
        gsq = area(B, 16, C)
        v.wait_ge(S["y_copied"], TT)
        for t in range(TT):
            y = Ytok[:, t, :].rearrange("p (h i) -> p h i", h=16)
            link(v.tensor_reduce(gnm, y, AX, ALU.add))
            link(v.tensor_scalar(gnm, gnm, 1.0 / C, None, ALU.mult))
            link(v.tensor_tensor(y, y, along(gnm, C), ALU.subtract))
            link(v.tensor_tensor(gsq, y, y, ALU.mult))
            link(v.tensor_reduce(gnv, gsq, AX, ALU.add))
            v.tensor_scalar(gnv, gnv, 1.0 / C, GN_EPS, ALU.mult, ALU.add).then_inc(S["gn_var"], 1)
            v.wait_ge(S["gn_root"], t + 1)
            link(v.reciprocal(gns, gns))
            v.tensor_tensor(y, y, along(gns, C), ALU.mult).then_inc(S["yn_ready"], 1)
        v.wait_ge(S["yn_turned"], 1)
        for m in range(HM):
            ins = v.scalar_tensor_tensor(actT[:, 8 + m, :], PS[:, 4 + m // 2, m % 2 * T:(m % 2 + 1) * T], col("gn_g", m),
                                         bonus[:, m, :], ALU.mult, ALU.add)
        link(ins)
        v.wait_ge(S["w_used"], used(N_SMALL))
        for m in range(HM):
            ins = v.tensor_tensor(actT[:, 8 + m, :], PS[:, m // 2, m % 2 * T:(m % 2 + 1) * T], actT[:, 8 + m, :], ALU.mult)
        ins.then_inc(S["mixed"], 1)

        low(N_OUT, (0, 1, 2))
        for h in range(2):
            v.wait_ge(S["mixed_high"], h + 1)
            x = actT[:, 8 * h:8 * h + 8, :]
            v.tensor_tensor(r32(x), x, high_of(XH[:, 8 * h:8 * h + 8, :]), ALU.subtract).then_inc(S["sum_step"], 1)
        v.wait_ge(S["x_loaded"], 16)
        with v.Fori(0, 2) as i:
            for j in range(2):
                low(N_OUT + j, (3,), i)
                low(N_OUT + j + 1, (0, 1, 2), i)
                add_out(used(N_OUT + j, i), j, i * (2 * CW) + j * CW)
        v.wait_ge(S["sum_step"], SUM["ffn1"])
        norm("n2", "mlp_norm")
        with v.Fori(0, F1_PARTS) as i:
            for c in range(8):
                n = N_F1 + c
                low(n, (3,), i, 8)
                if 1 <= c <= 4:
                    v.wait_ge(S["ffn1_high"], i * 4 + c)
                    tiles = slice(4 * (c - 1), 4 * c)
                    v.tensor_tensor(r32(HTL[:, tiles]), RQ[(c - 1) % 2], high_of(HTH[:, tiles]), ALU.subtract).then_inc(S["ffn1_low"], 1)
                low(n + 1, (0, 1, 2), i, 8)
                if c >= 4:
                    add_out(used(n, i, 8), c % 2, slice(CW * (c - 4), CW * (c - 3)))
        v.wait_ge(S["sum_step"], SUM["gate"])
        norm("n3", "ple_norm")
        for c in range(4):
            n, g, r = N_GATE + c, gate_sb[c % 2], xs[:, :, CW * c:CW * (c + 1)]
            low(n, (3,))
            if c < 3:
                low(n + 1, (0, 1, 2))
            v.wait_ge(S["gate_ready"], c + 1)
            v.wait_ge(S["proj_ready"], c + 1)
            link(v.tensor_tensor(g, PS[:, 4 + c % 2 * 2:6 + c % 2 * 2, :], g, ALU.mult))
            v.tensor_tensor(r, r, g, ALU.add).then_inc(S["sum_step"], 1)
        v.wait_ge(S["sum_step"], SUM["out2"])
        rms("fin")
        v.wait_ge(S["fing_loaded"], 16)
        for t in range(TT):
            v.scalar_tensor_tensor(xs[:, t, :], xs[:, t, :], rs[:, t:t + 1], fing, ALU.mult, ALU.mult).then_inc(S["fin_done"], 1)

        v.wait_ge(S["fin_done"], 2)
        norm("n4", "attn_norm_g_2")
        v.wait_ge(S["low_rank"], 3)
        for h in range(GH):
            ins = v.tensor_scalar(LB[:, h, :], PS[:, 6 + h // 2, h % 2 * T:(h % 2 + 1) * T], col("gla_gate_b_2", h), None, ALU.add)
        ins.then_inc(S["lb_in"], 1)
        v.wait_ge(S["zeroed"], 3)
        v.wait_ge(S["n4_act"], 8)

        def conv(m0):
            for w in range(4):
                for m in range(m0, m0 + 8):
                    tap, x = col("gla_conv_w_2", 16 * w + m), ZG[:, m, w:w + T]
                    if w == 0:
                        ins = v.tensor_scalar(CV[:, m, :], x, tap, None, ALU.mult)
                    else:
                        ins = v.scalar_tensor_tensor(CV[:, m, :], x, tap, CV[:, m, :], ALU.mult, ALU.add)
                if w < 3:
                    link(ins)
            return ins

        conv(0).then_inc(S["conv_done"], 1)
        v.wait_ge(S["la_soft"], 1)
        link(v.scalar_tensor_tensor(LB, LB, 0.0, Q1, ALU.min, ALU.subtract))
        for h in range(GH):
            ins = v.tensor_tensor_scan(LB[:, h, :], con("keep"), LB[:, h, :], 0.0, ALU.mult, ALU.add)
        link(ins)
        conv(8).then_inc(S["conv_done"], 1)
        v.wait_ge(S["conv_done"], 2)
        lbf = LB.rearrange("p h (c j) -> p (h c) j", c=NCH)
        v.tensor_tensor(GE[1].rearrange("p h (c j) -> p (h c) j", c=NCH), along(lbf[:, :, C - 1], C), lbf, ALU.subtract)\
            .then_inc(S["gd_ready"], 1)

        def halves(a, w, e):
            return a.rearrange("p h (n e w) -> p (h n) e w", e=2, w=w)[:, :, e, :]

        def level_diff(n):
            w = GLA_HALF[n]
            first = halves(LB, w, 0)
            ref = along(first[:, :, w - 1], w)
            v.tensor_tensor(halves(WD[n % 2], w, 0), ref, first, ALU.subtract)
            v.tensor_tensor(halves(WD[n % 2], w, 1), halves(LB, w, 1), ref, ALU.subtract).then_inc(S["level_diff"], 1)

        def level_product(n):
            w, d = GLA_HALF[n], WD[n % 2]
            v.wait_ge(S["level_exp"], n + 1)
            v.tensor_tensor(halves(d, w, 0), halves(d, w, 0), halves(CV[:, 4:8, :], w, 0), ALU.mult)
            v.tensor_tensor(halves(d, w, 1), halves(d, w, 1), halves(CV[:, 0:4, :], w, 1), ALU.mult)\
                .then_inc(S["level_ready"], 1)

        def add_scores(n):
            v.wait_ge(S["gsc_ready"], n + 1)
            sc = SCT.rearrange("p h t j -> p (h t) j")
            tmp = SCTMP.rearrange("p (q j) -> p q j", q=8)
            mask = over(glamask[:, (n - 1) % (len(GLA_HALF) + 1), :], 8)
            v.tensor_tensor(tmp if n else sc, bank8(4 + n % 4), mask, ALU.mult).then_inc(S["gsc_masked"], 1)
            v.wait_ge(S["gsc_masked"], n + 1)
            if n:
                v.tensor_tensor(sc, sc, tmp, ALU.add).then_inc(S["gsc_summed"], 1)
                v.wait_ge(S["gsc_summed"], n)

        level_diff(0)
        level_diff(1)
        v.wait_ge(S["silu_qk"], 1)
        level_product(0)
        level_product(1)
        v.wait_ge(S["gexp_ready"], 1)
        v.scalar_tensor_tensor(Q1, CV[:, 0:4, :], GDK ** -0.5, GE[0], ALU.mult, ALU.mult)
        v.tensor_tensor(K4, CV[:, 4:8, :], GE[1], ALU.mult).then_inc(S["gqk_ready"], 1)
        v.wait_ge(S["glamask_loaded"], 16)
        add_scores(0)
        for n in range(0, len(GLA_HALF), 2):
            add_scores(n + 1)
            add_scores(n + 2)
            if n + 2 < len(GLA_HALF):
                for q in (n + 2, n + 3):
                    level_diff(q)
                for q in (n + 2, n + 3):
                    level_product(q)
        for c in range(NCH - 1):
            v.wait_ge(S["go_ready"], c + 1)
            v.wait_ge(S["gs_ready"], c + 1)
            for h in range(GH):
                src = PS[:, 6 + h // 2, h % 2 * GDV:(h % 2 + 1) * GDV]
                if c == 0:
                    v.tensor_copy(GS[:, h, :], src).then_inc(S["gs_step"], 1)
                else:
                    v.scalar_tensor_tensor(GS[:, h, :], GS[:, h, :], GDEC[:, h, c:c + 1], src, ALU.mult, ALU.add)\
                        .then_inc(S["gs_step"], 1)
            v.wait_ge(S["gs_step"], GH * (c + 1))
        om, ov, osq = small[:, 24:28], small[:, 28:32], small[:, 32:36]
        oj = area(GC + 6144, GH, GDV)
        for t in range(TT):
            v.wait_ge(S["o_copied"], t + 1)
            o = OT[:, t, :].rearrange("p (h e) -> p h e", h=GH)
            link(v.tensor_tensor(oj, o, o, ALU.mult))
            link(v.tensor_reduce(om, oj, AX, ALU.add))
            v.tensor_scalar(ov, om, 1.0 / GDV, EPS, ALU.mult, ALU.add).then_inc(S["gn_var"], 1)
            v.wait_ge(S["gn_root"], TT + t + 1)
            link(v.reciprocal(osq, osq))
            v.tensor_tensor(o, o, along(osq, GDV), ALU.mult).then_inc(S["on_ready"], 1)
        v.wait_ge(S["on_turned"], 1)
        v.wait_ge(S["gout_ready"], 1)
        for m in range(8):
            ins = v.scalar_tensor_tensor(actT[:, m, :], PS[:, 4 + m // 2, m % 2 * T:(m % 2 + 1) * T], col("gla_norm_g_2", m % 2),
                                         GOQ[:, m, :], ALU.mult, ALU.mult)
        ins.then_inc(S["on_read"], 1)
        qg = COL["nsa_q_norm_g_2"]
        link(v.tensor_scalar(QKG, pcol[:, qg + 1:qg + 4], pcol[:, qg:qg + 1], None, ALU.mult))
        v.wait_ge(S["k_sums"], 1)
        rk = SQ[:, 0:4, :].rearrange("p a t -> p (a t)")
        v.tensor_scalar(rk[:, 0:512], PS[:, 0, :], 1.0 / DH, EPS, ALU.mult, ALU.add)
        v.tensor_scalar(rk[:, 512:1024], PS[:, 3, :], 1.0 / DH, EPS, ALU.mult, ALU.add)
        v.tensor_scalar(QRS.rearrange("p t h -> p (t h)"), PS[:, 2, 0:TT * NH], 1.0 / DH, EPS, ALU.mult, ALU.add)\
            .then_inc(S["k_var"], 1)
        v.wait_ge(S["k_root"], 1)
        v.reciprocal(rk, rk)
        link(v.reciprocal(QRS, QRS))
        link(v.tensor_scalar(QRS, QRS, DH ** -0.5, None, ALU.mult))
        for s in range(2):
            k = NK[:, 4 + 2 * s:6 + 2 * s, :].rearrange("p a t -> p (a t)")
            v.scalar_tensor_tensor(k, k, QKG[:, 1 + s:2 + s], rk[:, 512 * s:512 * s + 512], ALU.mult, ALU.mult).then_inc(S["nk_ready"], 1)
        v.wait_ge(S["side_copied"], 6)
        link(v.tensor_copy(KCMP, PS[:, 1, 0:2 * NB]))
        v.tensor_tensor(KCSQ, KCMP, KCMP, ALU.mult).then_inc(S["kc_squared"], 1)
        v.wait_ge(S["k_sums"], 2)
        v.tensor_scalar(KCSQ, PS[:, 2, 0:2 * NB], 1.0 / DH, EPS, ALU.mult, ALU.add).then_inc(S["k_var"], 1)
        v.wait_ge(S["k_root"], 2)
        link(v.reciprocal(KCSQ, KCSQ))
        v.scalar_tensor_tensor(KCMP, KCMP, QKG[:, 0:1], KCSQ, ALU.mult, ALU.mult).then_inc(S["nk_ready"], 1)
        for t in range(TT):
            nk = (t + 1) * P
            v.wait_ge(S["cs_ready"], t + 1)
            v.tensor_tensor(PCM[:, t], PS[:, 2, 0:NH * NB].rearrange("p (h n) -> p h n", h=NH), along(QRS[:, t, :], NB), ALU.mult)\
                .then_inc(S["cs_read"], 1)
            v.wait_ge(S["cs_read"], t + 1)
            link(v.tensor_tensor(PCM[:, t], PCM[:, t], over(con("cmpbias")[:, t * NB:(t + 1) * NB], NH), ALU.add))
            for s in range(2):
                for h in range(NH):
                    u = (t * 2 + s) * NH + h
                    v.wait_ge(S["sc_ready"], u + 1)
                    v.scalar_tensor_tensor(PSW[t][:, s, h, :], PS[:, 4 + u % 4, 0:nk], QRS[:, t, h:h + 1],
                                           con("causal")[:, 2 * P - nk:2 * P] if t else con("causal")[:, P:2 * P],
                                           ALU.mult, ALU.add).then_inc(S["sc_read"], 1)
            v.wait_ge(S["sc_read"], (t + 1) * 2 * NH)
            for s in range(3):
                link(v.tensor_reduce(MX[:, t, s, :], PCM[:, t] if s == 2 else PSW[t][:, s], AX, ALU.max))
                v.tensor_scalar(MX[:, t, s, :], MX[:, t, s, :], -1.0, None, ALU.mult).then_inc(S["max_ready"], 1)
        for t in range(TT):
            for s in range(3):
                a = PCM[:, t] if s == 2 else PSW[t][:, s]
                v.wait_ge(S["exp_done"], t * 3 + s + 1)
                link(v.reciprocal(WT[:, t, s, :], SM[:, t, s, :]))
                gate = gates[:, t, :].rearrange("p (h j) -> p j h", j=3)[:, (s + 1) % 3, :]
                link(v.tensor_tensor(WT[:, t, s, :], WT[:, t, s, :], gate, ALU.mult))
                if s == 2:
                    link(v.tensor_tensor(a, a, over(con("cmpseen")[:, t * NB:(t + 1) * NB], NH), ALU.mult))
                v.tensor_tensor(a, a, along(WT[:, t, s, :], a.shape[2]), ALU.mult).then_inc(S["prob_ready"], 1)
        low(N_OUT2, (0, 1, 2))
        v.wait_ge(S["gla_high"], 1)
        v.tensor_tensor(r32(actT[:, 0:8, :]), actT[:, 0:8, :], high_of(XH2[:, 0:8, :]), ALU.subtract).then_inc(S["gla_low"], 1)
        for t in range(TT):
            for kv in range(KVH):
                v.wait_ge(S["att_high"], t * KVH + kv + 1)
                k = 8 + kv * GRP
                v.tensor_tensor(r32(actT[:, k:k + GRP, t * P:(t + 1) * P]), PS[:, kv, :].rearrange("p (h t) -> p h t", h=GRP),
                                high_of(XH2[:, k:k + GRP, t * P:(t + 1) * P]), ALU.subtract).then_inc(S["att_out"], 1)
        with v.Fori(0, 2) as i:
            for j in range(2):
                low(N_OUT2 + j, (3,), i)
                low(N_OUT2 + j + 1, (0, 1, 2), i)
                add_out(used(N_OUT2 + j, i), j, i * (2 * CW) + j * CW)
        v.wait_ge(S["sum_step"], SUM["ffn2"])
        norm("n5", "ffn_norm_g_2")

        def ffn2_part(n0, groups, muls, i=None, last=False):
            def at(x):
                return x if i is None else i * F2_GROUPS + x

            plan = [UNITS[4]] * (2 * groups) + [UNITS[groups]] * 4 + [UNITS[4]]
            for c, (units, after) in enumerate(zip(plan, plan[1:])):
                n = n0 + c
                low(n, units[-1:], i, F2_N, units)
                if c % 2 == 0 and 2 <= c <= 2 * groups:
                    m = c // 2 - 1
                    v.wait_ge(S["ffn2_high"], at(muls + m + 1))
                    tiles = slice(4 * m, 4 * m + 4)
                    v.tensor_tensor(r32(HTL[:, tiles]), RQ[1], high_of(HTH[:, tiles]), ALU.subtract).then_inc(S["ffn2_low"], 1)
                if not (last and c == len(plan) - 2):
                    low(n + 1, after[:-1], i, F2_N, after)
                if c < 2 * groups and c % 2:
                    v.wait_ge(S["w_used"], used(n, i, F2_N))
                    v.wait_ge(S["ffn2_silu"], at(muls + c // 2 + 1))
                    v.tensor_tensor(by_half(RQ[1]), out_rows(1), by_half(RQ[0]), ALU.mult).then_inc(S["ffn2_mul"], 1)
                elif c >= 2 * groups:
                    g = c - 2 * groups
                    add_out(used(n, i, F2_N), g % 2, slice(CW * g, CW * (g + 1)))

        with v.Fori(0, F2_PARTS) as i:
            ffn2_part(N_F2, F2_GROUPS, 0, i)
        ffn2_part(N_F2 + F2_PARTS * F2_N, F2_LAST, F2_PARTS * F2_GROUPS, last=True)

    @block.gpsimd
    def _(pool):
        steps = [0]

        def link(ins):
            steps[0] += 1
            ins.then_inc(S["pool_step"], 1)
            pool.wait_ge(S["pool_step"], steps[0])

        pool.memset(prow, 0.0).then_inc(S["zeroed"], 1)
        pool.memset(Z[:, :, 0:1], 0.0).then_inc(S["zeroed"], 1)
        pool.wait_ge(S["norm_xn"], TT)
        for b in PB:
            pool.memset(b[:, 0:16], 0.0)
        link(pool.memset(ZP[:, :, 0:16], 0.0))
        pool.wait_ge(S["const_loaded"], 16)
        pool.wait_ge(S["z_copied"], 10)
        for m in range(HM):
            g = m // 2
            src = ZP[:, m, :]
            for k in range(g + 1):
                dst = PB[k % 2]
                link(pool.tensor_tensor(dst[:, 16:PW], src[:, 16:PW], src[:, 16 - 2 ** k:PW - 2 ** k], ALU.add))
                src = dst
            pool.tensor_tensor(src[:, 16:32], src[:, 16:32], con("invcnt")[:, 16 * g:16 * g + 16], ALU.mult)
            link(pool.tensor_scalar(src[:, 32:PW], src[:, 32:PW], 0.5 ** (g + 1), None, ALU.mult))
            link(pool.tensor_tensor(ZP[:, m, 16:PW], src[:, 16:PW], ZP[:, m, 16:PW], ALU.subtract))
        pool.tensor_copy(PB[0][:, 0:1], PB[1][:, 0:1]).then_inc(S["pool_ready"], 1)
        pool.wait_ge(S["sum_step"], 2)
        pool.dma_start(ptok, inp["p"][0, 0].rearrange("(t p) d -> p t d", p=P)).then_inc(S["ptok_loaded"], 16)
        pool.dma_start(GW2, W["gla_gate_w2_2"]).then_inc(S["gw2_loaded"], 16)
        with pool.Fori(0, F1_PARTS) as i:
            for c in range(4):
                pool.wait_ge(S["ffn1_relu"], i * 4 + (c + 1))
                r = RQ[c % 2]
                pool.tensor_tensor(r32(HTH[:, 4 * c:4 * c + 4]), r, r, ALU.mult)
                pool.tensor_tensor(r, r, r, ALU.mult).then_inc(S["ffn1_high"], 1)
        pool.wait_ge(S["w_used"], used(N_GATE - 1))
        pool.dma_start(pproj, W["w_ple_proj"].rearrange("(k p) n -> p k n", p=P)).then_inc(S["pproj_loaded"], 16)
        pool.dma_start(fing, inp["final_norm"].unsqueeze(0).broadcast_to([P, D])).then_inc(S["fing_loaded"], 16)
        pool.wait_ge(S["side_copied"], 1)
        pool.dma_start(SW[:, :, 0:16], wcols("w_in_2", 2048, 16)).then_inc(S["sw_loaded"], 16)
        pool.dma_start(SW[:, :, 16:40], wcols("w_in_2", 5648, 24)).then_inc(S["sw_loaded"], 16)
        pool.wait_ge(S["fin_done"], 2)
        pool.memset(ZG[:, :, 0:3], 0.0).then_inc(S["zeroed"], 1)
        pool.wait_ge(S["conv_done"], 2)
        pool.dma_start(glamask.rearrange("p n j -> p (n j)"), consts[:, GLAMASK_AT:]).then_inc(S["glamask_loaded"], 16)
        pool.wait_ge(S["gqk_ready"], 1)
        pool.wait_ge(S["gsc_summed"], len(GLA_HALF))
        for i, n in enumerate(("k", "v")):
            pool.dma_start(PTAB[i], W[f"cmp_{n}_pos_2"]).then_inc(S["pos_loaded"], 16)
            pool.dma_start(CW2[i], W[f"cmp_{n}_w2_2"]).then_inc(S["pos_loaded"], 16)
        pool.wait_ge(S["n4_act"], 15)
        for i in range(2):
            for kv in range(KVH):
                for l in range(2):
                    ins = pool.tensor_copy(XC[i][:, CST * l:CST * (l + 1), kv * NB:(kv + 1) * NB],
                                           NK[:, 2 * i + kv, CST * l:CST * (l + NB)].rearrange("p (n l) -> p l n", l=CST))
        ins.then_inc(S["xc_ready"], 1)
        pool.wait_ge(S["xc_ready"], 1)
        pool.tensor_tensor(SQ[:, 0:8, :], GOQ[:, 8:16, :], GOQ[:, 8:16, :], ALU.mult)
        pool.tensor_tensor(SQ[:, 8:12, :], NK[:, 4:8, :], NK[:, 4:8, :], ALU.mult).then_inc(S["nsq_ready"], 1)
        one = con("ones")[:, 0:1].unsqueeze(2).broadcast_to([P, 4, T])
        with pool.Fori(0, F2_PARTS) as i:
            for m in range(F2_GROUPS):
                pool.wait_ge(S["ffn2_mul"], i * F2_GROUPS + (m + 1))
                pool.tensor_tensor(r32(HTH[:, 4 * m:4 * m + 4]), RQ[1], one, ALU.mult).then_inc(S["ffn2_high"], 1)
        for m in range(F2_LAST):
            pool.wait_ge(S["ffn2_mul"], F2_PARTS * F2_GROUPS + m + 1)
            pool.tensor_tensor(r32(HTH[:, 4 * m:4 * m + 4]), RQ[1], one, ALU.mult).then_inc(S["ffn2_high"], 1)

    ctx.close()

INPUTS = ["x", "p", "attn_norm", "w_in", "mu_shift", "pool_w", "pool_scale", "w0", "w_up", "a0", "a_up", "g_up",
          "k_k", "k_a", "r_k", "gn_g", "gn_b", "w_out", "mlp_norm", "w_ffn_up", "w_ffn_down", "ple_norm",
          "w_ple_gate", "w_ple_proj", "final_norm", "attn_norm_g_2", "w_in_2", "gla_conv_w_2", "gla_gate_w2_2",
          "gla_gate_b_2", "gla_norm_g_2", "nsa_q_norm_g_2", "nsa_kc_norm_g_2", "nsa_ks_norm_g_2",
          "nsa_kw_norm_g_2", "cmp_k_pos_2", "cmp_k_w1_2", "cmp_k_w2_2", "cmp_v_pos_2", "cmp_v_w1_2",
          "cmp_v_w2_2", "w_out_2", "ffn_norm_g_2", "w_gate_2", "w_up_2", "w_down_2"]


def kernel(**inputs):
    import concourse.bacc as bacc
    from concourse.bass_utils import run_bass_kernel_spmd

    nc = bacc.Bacc("TRN2", target_bir_lowering=False, num_devices=1)
    arrays, aps = {}, {}
    for name in INPUTS:
        a = np.ascontiguousarray(inputs[name])
        arrays[f"in_{name}"] = a
        aps[name] = nc.dram_tensor(f"in_{name}", a.shape, mybir.dt.from_np(a.dtype), kind="ExternalInput").ap()
    arrays["in_constants"] = pack_constants()
    consts = nc.dram_tensor("in_constants", arrays["in_constants"].shape, F32, kind="ExternalInput").ap()
    out = nc.dram_tensor("out_y", (1, T, D), F32, kind="ExternalOutput").ap()
    build(nc, aps, consts, out)
    r = run_bass_kernel_spmd(nc, [arrays], core_ids=[0])
    return r.results[0]["out_y"]
```

```python
from contextlib import ExitStack

import numpy as np

import concourse.bass as bass
from concourse import mybir

F32 = mybir.dt.float32
ALU = mybir.AluOpType
ACT = mybir.ActivationFunctionType
AX = mybir.AxisListType.X

P = 128
T = 256
TT = T // P
D = 2048
KT = D // P
CW = 512
FF1 = 8192
FF2 = 5632
EPS = 1e-6
RW = 1024
HM = RW // P
C = 64
NCH = T // C
KAPPA = float(np.exp(-0.5))
GN_EPS = 64e-5
LEVELS = (2, 4, 8, 16, 32)
GH, GDK, GDV = 4, 128, 256
GTAU = 16.0
GLA_HALF = (32, 16, 8, 4, 2, 1)
NH, KVH, DH = 8, 2, 128
GRP = NH // KVH
CB, CST = 32, 16
NB = (T - CB) // CST + 1
NEG = -1e30


def constants():
    p = np.arange(P)[:, None]
    q = p % C
    j = np.arange(C)[None, :]
    c = {}
    c["ident"] = np.eye(P)
    c["tri"] = np.concatenate([q < j, q <= j], 1)
    c["levels"] = np.concatenate([((q // b) % 2 == 1) & (j // b == q // b - 1) for b in LEVELS], 1)
    c["level1"] = (j % 2 == 1) & (q == j - 1)
    c["eye64"] = q == j
    c["headones"] = (p // C) == (np.arange(P)[None, :] // C)
    c["ones"] = np.ones((P, P))
    c["keep"] = np.broadcast_to(np.arange(T)[None, :] % C != 0, (P, T))
    t16 = np.arange(16)
    c["invcnt"] = np.broadcast_to(
        np.concatenate([1.0 / np.minimum(t16 + 1, w) for w in (2, 4, 8, 16)])[None, :], (P, 64))
    s = np.arange(P)[None, :]
    c["causal"] = np.concatenate([np.zeros((P, P)), np.where(s > p, NEG, 0.0)], 1)
    end = np.arange(NB)[None, :] * CST + CB - 1
    seen = np.concatenate([end <= p + P * t for t in range(TT)], 1)
    c["cmpseen"] = seen
    c["cmpbias"] = np.where(seen, 0.0, NEG)
    c["glamask"] = GDK ** -0.5 * np.concatenate(
        [((q // w) % 2 == 0) & (j // w == q // w + 1) for w in GLA_HALF] + [q == j], 1)
    return {k: np.asarray(v, np.float32) for k, v in c.items()}


CONST_AT = {}


def pack_constants():
    parts, at = constants(), 0
    for k, v in parts.items():
        CONST_AT[k] = (at, v.shape[1])
        at += v.shape[1]
    return np.ascontiguousarray(np.concatenate(list(parts.values()), 1))


ROWS = [[("attn_norm", 16), ("mlp_norm", 16), ("ple_norm", 16), ("attn_norm_g_2", 16), ("ffn_norm_g_2", 16),
         ("mu_shift", 26), ("mu_tail", 1), ("pool_scale", 8), ("w0", 8)],
        [("a0", 8), ("k_k", 8), ("k_a", 8), ("r_k", 8), ("gla_conv_w_2", 64), ("gla_gate_b_2", 4),
         ("gla_norm_g_2", 2), ("nsa_q_norm_g_2", 1), ("nsa_kc_norm_g_2", 1), ("nsa_ks_norm_g_2", 1),
         ("nsa_kw_norm_g_2", 1), ("gn_g", 8), ("gn_b", 8)]]
COL = {}
for _t, _rows in enumerate(ROWS):
    _at = P * _t
    for _n, _r in _rows:
        COL[_n] = _at
        _at += _r
    assert _at <= P * (_t + 1)


SIGNALS = """
    w_used const_loaded zeroed rows_loaded norm_turned waup_loaded gup_loaded y_ready x_loaded sum_step
    out_stored w_low x_low rms_placed side_turned z_copied x1_low in_low head_sums wa_ready kk_squared head_acts
    rkr_ready bk_ready bk_copied bk_turned ar_ready score_masked score_ready dt_ready d_turned d_ready d_added
    dt_added f_ready f_masked df_ready dft_ready v_ready v_turned v_placed at_placed s_placed0 s_placed1
    zc_ready zc_copied u_ready u_placed0 u_placed1 s_ready pool_ready y_copied gate_copied yn_ready yn_turned
    ffn1_relu ffn1_low ptok_loaded side_copied pproj_loaded proj_ready groups_read x_whole sw_loaded low_rank
    gw2_loaded silu_qk lb_in level_ready gsc_masked gsc_ready gv_turned gkv_copied gsc_summed gs_step o_copied
    go_ready gs_ready gqk_ready gk_turned gv_ready pos_loaded xc_ready on_ready on_turned nsq_ready k_sums
    hid_ready cmp_ready nk_ready on_read sc_read sc_ready kc_squared cs_read cs_ready att_out pt_copied
    prob_ready pt_ready pt_used gla_low ffn2_silu ffn2_mul ffn2_low act_step norm_sum0 norm_mean norm_root
    w_high x0_loaded x1_loaded n1_dve n1_act x1_high in_high wag_shifted lc_ready sd_ready gn_var gn_root
    pool_out mixed_high mixed fin_done conv_done la_soft gd_ready gexp_ready level_diff level_exp gout_ready
    k_var k_root gla_high max_ready exp_done att_high dve_step x_high bonus_done ffn1_high fing_loaded
    glamask_loaded ffn2_high pool_step w_loaded0 w_loaded1 w_loaded2 w_loaded3
"""


def build(nc, inp, consts, out):
    ctx = ExitStack()

    places = {}

    def sbuf(name, shape, *r32_places):
        t = ctx.enter_context(nc.sbuf_tensor(name, shape, F32))
        at = nc.sbuf_base - 4 * int(np.prod(shape[1:]))
        places[name] = [(c, n, nc.alloc_sbuf_tensor_at(f"{name}_r{c}", [P, n], mybir.dt.float32r, offset=at + 4 * c))
                        for c, n in r32_places]
        return t

    def r32(ap, early=False):
        end = ap.offset + sum((n - 1) * step for step, n in list(ap.ap)[1:])
        known = places[ap.tensor.name]
        if ap.tensor.name == "arena":
            known = known[-EARLY:] if early else known[:-EARLY]
        for c, n, t in known:
            if c <= ap.offset and end < c + n:
                return bass.AP(tensor=t, offset=ap.offset - c, ap=[[n, P]] + [list(d) for d in ap.ap][1:])

    def high_of(ap, early=False):
        return r32(ap, early).bitcast(F32)

    xs = sbuf("xs", [P, TT, D], (RW, 2048))
    actT = sbuf("actT", [P, KT, T], (0, KT * T))
    ring = sbuf("ring", [P, 2, KT * CW], *((2048 * j, 2048) for j in range(8)))
    GLAMASK_AT = CONST_AT["glamask"][0]
    cst = sbuf("cst", [P, GLAMASK_AT])
    pcol = sbuf("pcol", [P, 2 * P])
    small = sbuf("small", [P, 64])
    NA = 26560
    HIW_AT, XH_AT, HTH_AT, HTL_AT = 16896, 12336, 0, 4144
    R32_AT = [(HIW_AT + 2048 * j, 2048) for j in range(4)] + [(at, KT * T) for at in (XH_AT, HTH_AT, HTL_AT)]
    Z_AT = 16 * (T + 1)
    GA_AT, A_AT = 27 * (T + 1) + 3 * 2048, 27 * (T + 1) + 5 * 2048
    R32_AT += [(at // 8 * 8, n + 8) for at, n in ((Z_AT, 2048), (GA_AT, 2048), (A_AT, KT * T), (A_AT + 6144, 2048))]
    EARLY = 4
    arena = sbuf("arena", [P, NA], *R32_AT)
    PS = ctx.enter_context(nc.psum_tensor("PS", [P, 8, 512], F32))

    S = {n: ctx.enter_context(nc.semaphore(n)) for n in SIGNALS.split()}

    def con(name):
        at, n = CONST_AT[name]
        return cst[:, at:at + n]

    def col(name, i=0):
        return pcol[:, COL[name] + i:COL[name] + i + 1]

    def split(v, dims):
        if len(dims) == 2:
            return v.rearrange("p (a b) -> p a b", a=dims[0])
        if len(dims) == 3:
            return v.rearrange("p (a b c) -> p a b c", a=dims[0], b=dims[1])
        if len(dims) == 4:
            return v.rearrange("p (a b c d) -> p a b c d", a=dims[0], b=dims[1], c=dims[2])
        return v

    def area(at, *dims):
        n = int(np.prod(dims))
        assert at + n <= NA, (at, dims)
        return split(arena[:, at:at + n], dims)

    def over(ap, n):
        return ap.unsqueeze(1).broadcast_to([ap.shape[0], n, ap.shape[1]])

    def along(ap, n):
        return ap.unsqueeze(len(ap.shape)).broadcast_to(list(ap.shape) + [n])

    ident, tri, eye64 = con("ident"), con("tri"), con("eye64")
    pair = [PS[:, 0:2, :], PS[:, 2:4, :]]

    def half(g):
        return pair[g].rearrange("p b (f t) -> p (b f) t", f=2)


    def out_rows(g):
        return pair[g].rearrange("p b (h t) -> p h b t", h=2)

    def by_half(a):
        return a.rearrange("p (h b) t -> p h b t", h=2)

    def unit_at(s, j):
        return ring[:, s, 2048 * j:2048 * (j + 1)]

    def slot(s):
        return ring[:, s, :].rearrange("p (k n) -> p k n", k=KT)

    LO, HI = slice(0, C), slice(C, P)
    HALF = [LO, HI]

    ss, ms, sq, rs = (small[:, 2 * i:2 * i + 2] for i in range(4))
    gnm, gnv, gns = (small[:, 8 + 16 * i:24 + 16 * i] for i in range(3))

    ZW = T + 1
    Z = area(0, 27, ZW)
    zr, zk, zv = (Z[:, 8 * i:8 * i + 8, 1:ZW] for i in range(3))
    B = 27 * ZW
    tmp1, tmp2, lw, ga, kk = (area(B + 2048 * i, HM, T) for i in range(5))
    AR_AT = B + 5 * 2048
    AR = area(AR_AT, HM, NCH, P)
    BK = area(AR_AT + 4096, HM, NCH, P)
    SD_AT = AR_AT + 8192
    PEND = area(SD_AT + 512, HM, NCH)
    ZSB = area(SD_AT + 544, HM, C)
    prow = area(AR_AT + 4096, 2, P)
    G = area(B, HM, 2, NCH, P)
    DTi = area(AR_AT + 4096, HM, NCH, C)
    Di = area(AR_AT + 6144, HM, NCH, C)
    Fi = area(B + 4 * 2048, HM, NCH, C)
    UVa = [area(AR_AT + 6144, 2, HM, 2, C), area(B + 4 * 2048, 2, HM, 2, C)]

    def UV(c):
        return UVa[c // 2][:, c % 2]

    xflat = xs[:, :, :].rearrange("p a b -> p (a b)")

    HIW1 = [area(Z_AT, 2048), xflat[:, RW:RW + 2048]]
    XH1 = area(AR_AT, KT, T)
    XL1 = [area(at, KT // 2, T) for at in (GA_AT, AR_AT + 6144)]

    def pool_bank(q):
        return 6 + q % 2 if q < 5 else 3

    def BKtok(c):
        v = area(8 * ZW + c * 1024, 1024) if c < 2 else xflat[:, 0:RW]
        return v.rearrange("p (m j) -> p m j", m=HM)

    bonus = zr
    Ytok = area(16 * ZW, TT, RW)
    waup = xflat[:, 0:RW]
    PW = T + 16
    ZP = xflat[:, RW:RW + HM * PW].rearrange("p (m t) -> p m t", m=HM)
    PB = [xflat[:, RW + HM * PW + i * PW:RW + HM * PW + (i + 1) * PW] for i in range(2)]
    SD = [area(SD_AT, HM, C), area(16 * ZW + RW, HM, C)]
    DIF = area(AR_AT + 4096, HM, T)
    GT = area(B + 2048, HM, T)
    XN = {p: area({"n1": AR_AT, "n4": 8192}.get(p, 0), TT, D) for p in ("n1", "n2", "n3", "fin", "n4", "n5")}

    def rms_diagonal(p):
        return XN[p][:, 1, 0:TT * P].rearrange("p (t j) -> p t j", t=TT)

    poolw = ring[:, 1, 0:2048].rearrange("p (q n) -> p q n", q=8)
    gup, gup2 = ring[:, 1, 2048:3072], ring[0:32, 1, 3072:4096]

    HIW = [area(HIW_AT + 2048 * j, 2048) for j in range(4)]
    XH = area(XH_AT, KT, T)
    HTH, HTL = area(HTH_AT, KT, T), area(HTL_AT, KT, T)
    RQ = [area(8240 + 1024 * b, 4, T) for b in range(2)]
    pproj = area(8192, 2, D)
    ptok = area(AR_AT + 8192, TT, 256)
    pT = area(AR_AT + 8192, 2, T)
    fing = area(4096, D)
    gate_sb = [area(6144 + 1024 * b, TT, CW) for b in range(2)]

    GC = 16 * (T + 3)
    ZG = area(0, 16, T + 3)
    LB = area(GC, GH, T)
    WD = [area(GC + 1024 + 1024 * i, GH, T) for i in range(2)]
    CV = area(GC + 4096, 16, T)
    Q1, K4 = area(GC + 3072, GH, T), area(GC + 8192, GH, T)
    KTOK = area(GC + 9216, TT, GH, GDK)
    SCT = area(GC + 10240, GH, TT, C)
    GS = area(GC + 10752, GH, GDV)
    OT = area(GC + 11776, TT, RW)
    GN_AT = GC + 13824
    GOQ = area(GN_AT, 16, T)
    NK = area(GN_AT + 4096, 8, T)
    VSW = area(GN_AT + 6144, 2, TT, 256)
    SW = area(GN_AT + 7168, KT, 40)
    LR = area(GN_AT + 7808, T)[0:16]
    GW2 = area(GN_AT + 8064, 512)[0:16]
    GE = [area(1024 * i, GH, T) for i in range(2)]
    glamask, SCTMP = area(2048, len(GLA_HALF) + 1, C), area(3072, 512)
    GDEC = small[:, 8:8 + GH * NCH].rearrange("p (h c) -> p h c", h=GH)
    VTOK = area(GC, TT, RW)
    gates = area(GN_AT + 7168, TT, 24)
    XC = [area(992 * i, CB, 31) for i in range(2)]
    CW2 = [area(1984 + 128 * i, P) for i in range(2)]
    PTAB = [area(2240 + 128 * i, P)[0:CB] for i in range(2)]
    HB = [area(2496 + 2 * i, 2) for i in range(2)]
    HID = [area(2500 + 30 * i, 2 * NB) for i in range(2)]
    KCMP = area(2560, 2 * NB)
    KCSQ = area(2590, 2 * NB)
    QKG = area(2620, 3)
    QRS, RSP = area(2623, TT, NH), area(2639, TT, NH)
    VCMP = area(GN_AT + 7808, KVH, DH)[0:NB]
    SQ = area(2912, 12, T)
    RK = area(16640, 2, 2 * T)
    PCM = area(5984, TT, NH, NB)
    PSW = [area(6224, 2, NH, P), area(8272, 2, NH, T)]
    PTR = [area(12368 + 512 * i, 512) for i in range(4)]
    PTC = [area(14416 + 512 * i, 512)[0:NB] for i in range(4)]
    MX, SM, WT = (area(16464 + 48 * i, TT, 3, NH) for i in range(3))
    XL_IN2 = HTL
    XH2 = HTH

    W = {n: a[0] if n not in ("final_norm", "x", "p") else a for n, a in inp.items()}
    xin, xout = (a.rearrange("o (t p) d -> p (o t) d", p=P) for a in (inp["x"], out))

    def wcols(name, c0, n=CW, k0=0, nk=KT):
        return W[name].rearrange("(k p) n -> p k n", p=P)[:, k0:k0 + nk, c0:c0 + n]

    N_WAG, N_KRV, N_POOL, N_SMALL, N_OUT, N_F1, N_GATE = 0, 1, 7, 9, 10, 14, 46
    N_GLA, N_KCVC, N_KSVS, N_KWVW, N_GOQ, N_CMP, N_OUT2, N_F2, N_END = 50, 54, 55, 56, 57, 61, 62, 66, 104
    F1_PARTS = 4
    F2_PARTS, F2_GROUPS = 3, 3
    F2_LAST = FF2 // CW - F2_PARTS * F2_GROUPS
    F2_N = 2 * F2_GROUPS + 4
    UNITS = {4: (0, 1, 2, 3), 3: (0, 1, 2), 2: (0, 2)}

    def used(n, i=None, per=2, unit=4):
        v = 4 * n + unit
        return v if i is None else i * (4 * per) + v

    def split_count(n, j, i=None, per=2):
        v = 4 * (n - N_OUT if n < N_GOQ else n - N_OUT2 + N_GOQ - N_OUT) + j + 1
        return v if i is None else i * (4 * per) + v

    def counts(units, j):
        q = units.index(j)
        return (units[q + 1] if q + 1 < len(units) else 4) - j

    SUM = {"out": 2, "ffn1": 6, "gate": 22, "out2": 26, "ffn2": 30, "end": 46}
    NORMS = {"n1": 0, "n2": 1, "n3": 2, "n4": 3, "n5": 4}
    XSPLIT = {"n2": 0, "n3": 8, "n4": 16, "n5": 24}
    RMS = {"n1": 1, "n2": 2, "n3": 3, "fin": 4, "n4": 5, "n5": 6}

    block = ctx.enter_context(nc.Block())

    @block.sync
    def _(sp):
        def load(n, dsts, srcs, i=None, per=2):
            for h in range(2):
                if n >= 2:
                    whole = n - 2 in (N_POOL, N_POOL + 1, N_SMALL)
                    sp.wait_ge(S["w_used"], used(n - 2, i, per, 4 if whole else 2 * (h + 1)))
                sp.dma_start(dsts[h], srcs[h]).then_inc(S[f"w_loaded{2 * (n % 2) + h}"], 16)

        def k_halves(n, name, c0, nc=CW, k0=0, nk=KT // 2, i=None, per=2, step=0, k_step=0):
            w = W[name].rearrange("(k p) n -> p k n", p=P)
            dsts, srcs = [], []
            for h in range(2):
                m = nk if isinstance(nk, int) else nk[h]
                first = nk if isinstance(nk, int) else nk[0]
                ks = slice(k0 + h * first, k0 + h * first + m) if i is None or not k_step else \
                    bass.ds(i * k_step + (k0 + h * first), m)
                cs = slice(c0, c0 + nc) if i is None or not step else bass.ds(i * step + c0, nc)
                dsts.append(slot(n % 2)[:, 8 * h:8 * h + m, 0:nc])
                srcs.append(w[:, ks, cs])
            load(n, dsts, srcs, i, per)

        def column_halves(n, name, c0, i=None, per=2, step=0):
            w = W[name].rearrange("(k p) n -> p k n", p=P)
            dsts, srcs = [], []
            for h in range(2):
                at = c0 + h * CW // 2
                dsts.append(ring[:, n % 2, 4096 * h:4096 * (h + 1)].rearrange("p (k n) -> p k n", k=KT))
                srcs.append(w[:, :, slice(at, at + CW // 2) if i is None else bass.ds(i * step + at, CW // 2)])
            load(n, dsts, srcs, i, per)

        def load_loop(first, count, name, c0):
            with sp.Fori(0, count // 2) as i:
                for j in range(2):
                    k_halves(first + j, name, c0 + j * CW, i=i, step=2 * CW)

        sp.dma_start(cst[:], consts[:, 0:GLAMASK_AT]).then_inc(S["const_loaded"], 16)
        sp.wait_ge(S["zeroed"], 1)
        for t, rows in enumerate(ROWS):
            at = 0
            for name, n in rows:
                dst = prow[at:at + n, t, :]
                if name == "mu_shift":
                    src = W["mu_shift"][0:26 * P].rearrange("(r c) -> r c", c=P)
                elif name == "mu_tail":
                    dst, src = prow[at:at + 1, t, 0:32], W["mu_shift"][26 * P:].unsqueeze(0)
                elif name == "r_k":
                    src = W["r_k"].rearrange("(r e) c -> r (e c)", e=2)
                elif name == "gla_conv_w_2":
                    src = W[name].rearrange("w (r c) -> (w r) c", c=P)
                else:
                    src = W[name].rearrange("(r c) -> r c", c=P)
                sp.dma_start(dst, src).then_inc(S["rows_loaded"], 16)
                at += n
        k_halves(0, "w_in", 4096, 288)
        column_halves(1, "w_in", 2048)
        column_halves(2, "w_in", 2560)
        sp.wait_ge(S["norm_turned"], KT // 2)
        sp.dma_start(waup[LO], W["w_up"]).then_inc(S["waup_loaded"], 16)
        sp.dma_start(waup[HI], W["a_up"]).then_inc(S["waup_loaded"], 16)
        for n, c0 in ((3, 1024), (4, 1536)):
            column_halves(n, "w_in", c0)
        for n, c0 in ((5, 3072), (6, 3584)):
            k_halves(n, "w_in", c0)
        for n in range(7, 9):
            k_halves(n, "w_in", 512 * (n - 7))
        wp = W["pool_w"].rearrange("g (k p) n -> p (g k) n", p=P)
        load(N_SMALL, [poolw[:, 0:4], poolw[:, 4:8]], [wp[:, 0:4], wp[:, 4:8]])
        sp.dma_start(gup, W["g_up"][0:P]).then_inc(S["gup_loaded"], 16)
        sp.dma_start(gup2, W["g_up"][P:]).then_inc(S["gup_loaded"], 16)
        k_halves(N_OUT, "w_out", 0)
        sp.wait_ge(S["y_ready"], NCH)
        sp.wait_ge(S["w_used"], used(N_SMALL))
        sp.dma_start(xs[:], xin).then_inc(S["x_loaded"], 16)
        for n in range(N_OUT + 1, N_F1):
            k_halves(n, "w_out", CW * (n - N_OUT))
        with sp.Fori(0, F1_PARTS) as i:
            for c in range(4):
                column_halves(N_F1 + c, "w_ffn_up", CW * c, i, 8, 4 * CW)
            for g in range(4):
                k_halves(N_F1 + 4 + g, "w_ffn_down", CW * g, i=i, per=8, k_step=KT)
        load_loop(N_GATE, 4, "w_ple_gate", 0)
        with sp.Fori(0, 2) as i:
            for j in range(2):
                column_halves(N_GLA + j, "w_in_2", j * CW, i, step=2 * CW)
        for n in range(N_KCVC, N_GOQ):
            column_halves(n, "w_in_2", 4112 + CW * (n - N_KCVC))
        load_loop(N_GOQ, 4, "w_in_2", 2064)
        cw = slot(N_CMP % 2).rearrange("p k n -> p (k n)").rearrange("p (s l h) -> p s l h", s=2, l=CB)
        load(N_CMP, [cw[:, 0], cw[:, 1]], [W[f"cmp_{n}_w1_2"].rearrange("(l d) h -> d l h", d=DH) for n in ("k", "v")])
        load_loop(N_OUT2, 4, "w_out_2", 0)

        def ffn2_part(n, c0, groups, i=None):
            for m in range(groups):
                for j, name in enumerate(("w_gate_2", "w_up_2")):
                    column_halves(n + 2 * m + j, name, c0 + m * CW, i, F2_N, F2_GROUPS * CW)
            for g in range(4):
                k_halves(n + 2 * groups + g, "w_down_2", CW * g, k0=c0 // P, nk=(8, 4) if groups == 3 else 4,
                         i=i, per=F2_N, k_step=4 * F2_GROUPS)

        with sp.Fori(0, F2_PARTS) as i:
            ffn2_part(N_F2, 0, F2_GROUPS, i)
        ffn2_part(N_F2 + F2_PARTS * F2_N, F2_PARTS * F2_GROUPS * CW, F2_LAST)
        for g in range(4):
            sp.wait_ge(S["sum_step"], SUM["end"] - 3 + g)
            sp.dma_start(xout[:, :, CW * g:CW * (g + 1)], xs[:, :, CW * g:CW * (g + 1)]).then_inc(S["out_stored"], 16)
        sp.wait_ge(S["out_stored"], 64)

    @block.tensor
    def _(pe):
        def loaded(n, i=None):
            v = 16 * (n // 2 + 1)
            for h in range(2):
                pe.wait_ge(S[f"w_loaded{2 * (n % 2) + h}"], v if i is None else i * 16 + v)

        def rows_out(n, dst, m, k_tiles=KT, f0=0):
            for k in range(k_tiles):
                mm = pe.matmul(dst, slot(n % 2)[:, k, f0:f0 + m], actT[:, k, :], start=(k == 0), stop=(k == k_tiles - 1))
            return mm

        def chunk_rows(n, g, tiles=4):
            for f in range(tiles):
                mm = rows_out(n, half(g)[:, f, :], P, f0=f * P)
            return mm

        def three(dst, weights, tokens, first, last, early=False):
            (wh, wl), (xh, xl) = weights, tokens
            for q, (w, x) in enumerate(((wh, xh), (wh, xl), (wl, xh))):
                mm = pe.matmul(dst, r32(w, early), r32(x, early), start=first and q == 0, stop=last and q == 2)
            return mm

        def split_rows(n, g, i=None, per=2, low_part=actT, p=None):
            for j in range(4):
                pe.wait_ge(S["w_low"], split_count(n, j, i, per))
                h, k0 = j // 2, j % 2 * 8
                if p and j == 1:
                    pe.wait_ge(S["x_low"], XSPLIT[p] + 8)
                wh, wl = (a.rearrange("p (k n) -> p k n", k=8) for a in (HIW[j], unit_at(n % 2, j)))
                for f in range(2):
                    for k in range(8):
                        c = slice(f * P, (f + 1) * P)
                        mm = three(pair[g][:, f, h * T:(h + 1) * T], (wh[:, k, c], wl[:, k, c]),
                                   (XH[:, k0 + k, :], low_part[:, k0 + k, :]), k0 + k == 0, k0 + k == KT - 1)
                mm.then_inc(S["w_used"], 1)

        def split_tokens(n, out, xh, xl, i=None, per=2, units=UNITS[4], ready=None):
            for q, j in enumerate(units):
                pe.wait_ge(S["w_low"], split_count(n, j, i, per))
                if ready is not None:
                    ready(q)
                wh, wl = (a.rearrange("p (k n) -> p k n", k=4) for a in (HIW[j], unit_at(n % 2, j)))
                for k in range(4):
                    for t in range(TT):
                        x, tok = 4 * q + k, slice(t * P, (t + 1) * P)
                        mm = three(out[:, t, :], (xh(x)[:, tok], xl(x)[:, tok]), (wh[:, k, :], wl[:, k, :]),
                                   x == 0, x == 4 * len(units) - 1)
                mm.then_inc(S["w_used"], counts(units, j))

        def norm(p):
            pe.wait_ge(S["rms_placed"], TT * (NORMS[p] + 1))
            for j in range(KT // 2):
                if j >= 4:
                    if p in XSPLIT:
                        pe.wait_ge(S["x_low"], XSPLIT[p] + j - 3)
                    else:
                        pe.wait_ge(S[f"{p}_dve" if j % 2 == 0 else f"{p}_act"], (j - 4) // 2 + 1)
                for q in range(2):
                    for t in range(TT):
                        k = 2 * j + q
                        mm = pe.matmul(PS[:, 4 + j % 4, q * T + t * P:q * T + (t + 1) * P], xs[:, t, k * P:(k + 1) * P],
                                       rms_diagonal(p)[:, t, :], start=True, stop=True)
                mm.then_inc(S["norm_turned"], 1)
            if p not in XSPLIT:
                pe.wait_ge(S[f"{p}_dve"], 4)
                pe.wait_ge(S[f"{p}_act"], 4)

        pe.wait_ge(S["const_loaded"], 16)
        pe.wait_ge(S["rows_loaded"], 16 * sum(len(r) for r in ROWS))
        for t in range(2):
            mm = pe.transpose(PS[:, 0, t * P:(t + 1) * P], prow[:, t, :], ident)
        mm.then_inc(S["side_turned"], 1)

        norm("n1")
        pe.wait_ge(S["z_copied"], 1)
        loaded(0)
        for f in range(2):
            rows_out(0, half(0)[:, f, :], P, f0=f * P)
        rows_out(0, half(0)[0:32, 2, :], 32, f0=2 * P).then_inc(S["w_used"], 4)
        def split_kr(n):
            pe.wait_ge(S["z_copied"], n)
            for j in range(4):
                if n == N_KRV and j < 2:
                    pe.wait_ge(S["x1_low"], j + 1)
                pe.wait_ge(S["in_low"], 4 * (n - N_KRV) + j + 1)
                h, k0 = j // 2, j % 2 * 8
                wh, wl = (a.rearrange("p (k n) -> p k n", k=8) for a in (HIW1[j % 2], unit_at(n % 2, j)))
                for f in range(2):
                    for k in range(8):
                        c = slice(f * P, (f + 1) * P)
                        mm = three(pair[n % 2][:, f, h * T:(h + 1) * T], (wh[:, k, c], wl[:, k, c]),
                                   (XH1[:, k0 + k, :], XL1[j % 2][:, k, :]), k0 + k == 0, k0 + k == KT - 1, True)
                mm.then_inc(S["w_used"], 1)

        def krv(n):
            loaded(n)
            pe.wait_ge(S["z_copied"], n)
            chunk_rows(n, n % 2).then_inc(S["w_used"], 4)

        def heads(lhs, rhs):
            for m in range(HM):
                mm = pe.matmul(PS[:, 4 + m // 2, m % 2 * T:(m % 2 + 1) * T], lhs(m), rhs(m), start=True, stop=True)
            mm.then_inc(S["head_sums"], 1)

        split_kr(1)
        split_kr(2)
        pe.wait_ge(S["waup_loaded"], 32)
        pe.wait_ge(S["wa_ready"], 2)
        heads(lambda m: waup[LO, m * P:(m + 1) * P], lambda m: Z[LO, 24, 1:ZW])
        split_kr(3)
        pe.wait_ge(S["kk_squared"], 1)
        pe.wait_ge(S["head_acts"], 1)
        heads(lambda m: con("headones"), lambda m: tmp2[:, m, :])
        split_kr(4)
        pe.wait_ge(S["head_acts"], 2)
        heads(lambda m: waup[HI, m * P:(m + 1) * P], lambda m: Z[HI, 24, 1:ZW])
        krv(5)
        pe.wait_ge(S["rkr_ready"], 1)
        pe.wait_ge(S["head_acts"], 4)
        heads(lambda m: con("headones"), lambda m: tmp1[:, m, :])
        krv(6)
        pe.wait_ge(S["bk_ready"], 1)
        pe.wait_ge(S["head_acts"], 5)
        for g in range(2 * (NCH - 1)):
            c, m0 = g // 2, g % 2 * 4
            if g >= 4:
                pe.wait_ge(S["bk_copied"], g - 3)
            for m in range(4):
                mm = pe.transpose(PS[:, 4 + g % 4, m * P:(m + 1) * P], BK[:, m0 + m, c, :], ident)
            mm.then_inc(S["bk_turned"], 1)
        pe.wait_ge(S["ar_ready"], 1)
        pe.wait_ge(S["z_copied"], 8)
        for g in range(2 * HM):
            m, e = g // 2, g % 2
            if g >= 4:
                pe.wait_ge(S["score_masked"], g - 3)
            for c in range(NCH):
                mm = pe.matmul(PS[:, g % 4, c * P:(c + 1) * P], BK[HALF[e], m, c, :], AR[HALF[e], m, c, :],
                               start=True, stop=True)
            mm.then_inc(S["score_ready"], 1)

        def pool_tile(q, half):
            n, f = N_POOL + q // 4, q % 4
            if half == 0:
                if f == 0:
                    loaded(n)
                if q < 2:
                    pe.wait_ge(S["bk_copied"], 2 * (NCH - 1))
                elif q != 5:
                    pe.wait_ge(S["z_copied"], 7 + q if q < 5 else 8 + q)
            for k in range(8 * half, 8 * half + 8):
                mm = pe.matmul(PS[:, pool_bank(q), 0:T], slot(n % 2)[:, k, f * P:(f + 1) * P], actT[:, k, :],
                               start=(k == 0), stop=(k == KT - 1))
            if half:
                mm.then_inc(S["w_used"], 1)

        def pool_half(x):
            pool_tile(2 + x // 2, x % 2)

        for q in range(2):
            pool_tile(q, 0)
            pool_tile(q, 1)
        pe.wait_ge(S["dt_ready"], 1)

        def inverse_group(g, bank, lhs, rhs):
            for m in range(2 * g, 2 * g + 2):
                for c in range(NCH):
                    for e in range(2):
                        h = HALF[e]
                        at = (m % 2 * NCH + c) * C
                        mm = pe.matmul(PS[h, bank, at:at + C], lhs(h, m, c, e), rhs(h, m, c, e), start=True, stop=True)
            return mm

        for g in range(4):
            inverse_group(g, g, lambda h, m, c, e: DTi[h, m, c, :], lambda h, m, c, e: eye64[h]).then_inc(S["d_turned"], 1)
        for lv in range(len(LEVELS)):
            last = lv == len(LEVELS) - 1
            pool_half(lv)
            for g in range(4):
                if lv == 0:
                    pe.wait_ge(S["d_ready"], g + 1)
                else:
                    pe.wait_ge(S["d_added"], 4 * (lv - 1) + g + 1)
                    pe.wait_ge(S["dt_added"], 4 * (lv - 1) + g + 1)
                inverse_group(g, g, lambda h, m, c, e: G[h, m, e, c, 0:C], lambda h, m, c, e: Di[h, m, c, :])\
                    .then_inc(S["f_ready"], 1)
            for g in range(4):
                pe.wait_ge(S["f_masked"], 4 * lv + g + 1)
                if not last:
                    if g >= 2:
                        pe.wait_ge(S["d_added"], 4 * lv + g - 1)
                    inverse_group(g, 4 + g % 2, lambda h, m, c, e: DTi[h, m, c, :], lambda h, m, c, e: Fi[h, m, c, :])\
                        .then_inc(S["df_ready"], 1)
                inverse_group(g, g, lambda h, m, c, e: Fi[h, m, c, :], lambda h, m, c, e: DTi[h, m, c, :])\
                    .then_inc(S["dft_ready"], 1)
        pool_half(len(LEVELS))
        pe.wait_ge(S["dt_added"], 4 * len(LEVELS))
        pe.wait_ge(S["v_ready"], 1)
        pe.wait_ge(S["z_copied"], 13)
        for c in range(NCH):
            for m in range(HM):
                for e in range(2):
                    mm = pe.matmul(PS[HALF[1 - e], 4 + c, m * C:(m + 1) * C], zv[HALF[e], m, c * C:(c + 1) * C],
                                   eye64[HALF[e]], start=True, stop=True)
            mm.then_inc(S["v_turned"], 1)
        pe.wait_ge(S["v_placed"], NCH)
        pe.wait_ge(S["at_placed"], 2)

        for c in range(NCH):
            pe.wait_ge(S["s_placed0"], c + 1)
            pe.wait_ge(S["s_placed1"], c + 1)
            for m in range(HM):
                for e in range(2):
                    mm = pe.matmul(PS[HALF[e], 0, m * C:(m + 1) * C], G[:, m, e, c, 0:C], UV(c)[:, m, e, :],
                                   start=True, stop=True)
            mm.then_inc(S["zc_ready"], 1)
            if c < 3:
                pool_half(6 + 2 * c)
            pe.wait_ge(S["zc_copied"], c + 1)
            for m in range(HM):
                for e in range(2):
                    mm = pe.matmul(PS[HALF[e], 1, m * C:(m + 1) * C], DTi[HALF[e], m, c, :], ZSB[HALF[e], m, :],
                                   start=True, stop=True)
            mm.then_inc(S["u_ready"], 1)
            if c < 3:
                pool_half(7 + 2 * c)
            pe.wait_ge(S["u_placed0"], c + 1)
            pe.wait_ge(S["u_placed1"], c + 1)
            if c < NCH - 1:
                for m in range(HM):
                    for e in range(2):
                        mm = pe.matmul(PS[HALF[e], 2, m * C:(m + 1) * C], BKtok(c)[:, m, e * C:(e + 1) * C],
                                       UV(c)[:, m, e, :], start=True, stop=True)
                mm.then_inc(S["s_ready"], 1)
            for m in range(HM):
                for e in range(2):
                    y = PS[HALF[c % 2], 4 + 2 * (c // 2) + e, m * C:(m + 1) * C]
                    pe.matmul(y, AR[HALF[e], m, c, C:P], SD[c % 2][HALF[e], m, :], start=True, stop=False)
                    mm = pe.matmul(y, G[:, m, e, c, C:P], UV(c)[:, m, e, :], start=False, stop=True)
            mm.then_inc(S["y_ready"], 1)
        loaded(N_SMALL)
        pe.wait_ge(S["pool_ready"], 1)
        pe.wait_ge(S["z_copied"], 16)
        for m in range(HM):
            for k in range(2):
                g = m // 2
                mm = pe.matmul(PS[:, m // 2, m % 2 * T:(m % 2 + 1) * T],
                               poolw[:, 2 * g + k, m % 2 * P:(m % 2 + 1) * P], ZP[:, 2 * g + k, 16:PW],
                               start=(k == 0), stop=(k == 1))
        mm.then_inc(S["w_used"], 2)
        pe.wait_ge(S["gup_loaded"], 32)
        pe.wait_ge(S["y_copied"], 2)
        for m in range(HM):
            dst = PS[:, 4 + m // 2, m % 2 * T:(m % 2 + 1) * T]
            pe.matmul(dst, gup[:, m * P:(m + 1) * P], Z[:, 25, 1:ZW], start=True, stop=False)
            mm = pe.matmul(dst, gup2[:, m * P:(m + 1) * P], Z[0:32, 26, 1:ZW], start=False, stop=True)
        mm.then_inc(S["w_used"], 2)
        pe.wait_ge(S["gate_copied"], 1)
        for t in range(TT):
            pe.wait_ge(S["yn_ready"], t + 1)
            for m in range(HM):
                at = m % 2 * T + t * P
                mm = pe.transpose(PS[:, 4 + m // 2, at:at + P], Ytok[:, t, m * P:(m + 1) * P], ident)
        mm.then_inc(S["yn_turned"], 1)

        with pe.Fori(0, 2) as i:
            for j in range(2):
                pe.wait_ge(S["sum_step"], i * 2 + (SUM["out"] + j - 1))
                split_tokens(N_OUT + j, pair[j], lambda k: XH[:, k, :], lambda k: actT[:, k, :], i,
                             ready=(lambda q: pe.wait_ge(S["sum_step"], i * 2 + (1 + q // 2))) if j == 0 else None)
        norm("n2")
        with pe.Fori(0, F1_PARTS) as i:
            for c in range(4):
                if c < 2:
                    pe.wait_ge(S["sum_step"], i * 4 + (SUM["ffn1"] - 1 + c))
                else:
                    pe.wait_ge(S["ffn1_relu"], i * 4 + (c - 1))
                split_rows(N_F1 + c, c % 2, i, 8, p="n2" if c == 0 else None)
            for g in range(4):
                if g < 2:
                    pe.wait_ge(S["ffn1_relu"], i * 4 + (3 + g))
                else:
                    pe.wait_ge(S["sum_step"], i * 4 + (SUM["ffn1"] + g - 1))
                split_tokens(N_F1 + 4 + g, pair[g % 2], lambda k: HTH[:, k, :], lambda k: HTL[:, k, :], i, 8,
                             ready=(lambda q: pe.wait_ge(S["ffn1_low"], i * 4 + (q + 1))) if g == 0 else None)
        pe.wait_ge(S["ptok_loaded"], 16)
        for t in range(TT):
            for k in range(2):
                mm = pe.transpose(PS[:, 4, k * T + t * P:k * T + (t + 1) * P], ptok[:, t, k * P:(k + 1) * P], ident)
        mm.then_inc(S["side_turned"], 1)
        pe.wait_ge(S["side_copied"], 1)
        norm("n3")
        pe.wait_ge(S["pproj_loaded"], 16)
        with pe.Fori(0, 2) as i:
            for j in range(2):
                pe.wait_ge(S["sum_step"], i * 2 + (SUM["gate"] + j - 1))
                split_tokens(N_GATE + j, pair[j], lambda k: XH[:, k, :], lambda k: actT[:, k, :], i,
                             ready=(lambda q: pe.wait_ge(S["x_low"], XSPLIT["n3"] + 4 + q // 2 * 4)) if j == 0 else None)
                for t in range(TT):
                    for k in range(2):
                        mm = pe.matmul(PS[:, 4 + 2 * j + t, :], pT[:, k, t * P:(t + 1) * P],
                                       pproj[:, k, bass.ds(i * (2 * CW) + j * CW, CW)], start=(k == 0), stop=(k == 1))
                mm.then_inc(S["proj_ready"], 1)

        norm("n4")
        with pe.Fori(0, 2) as i:
            for j in range(2):
                pe.wait_ge(S["groups_read"], i * 2 + (j + 3))
                split_rows(N_GLA + j, j, i, low_part=XL_IN2, p="n4" if j == 0 else None)
        for n in range(N_KCVC, N_GOQ):
            g = n % 2
            pe.wait_ge(S["groups_read"], 7 + n - N_KCVC)
            for j in range(4):
                pe.wait_ge(S["w_low"], split_count(n, j))
                h, k0 = j // 2, j % 2 * 8
                wh, wl = (a.rearrange("p (k n) -> p k n", k=8) for a in (HIW[j % 2], unit_at(n % 2, j)))
                for f in range(2):
                    c = slice(f * P, (f + 1) * P)
                    for k in range(8):
                        dst, x = pair[g][:, f, h * T:(h + 1) * T], (XH[:, k0 + k, :], XL_IN2[:, k0 + k, :])
                        first, last = k0 + k == 0, k0 + k == KT - 1
                        if n == N_KCVC or h == 0:
                            mm = three(dst, (wh[:, k, c], wl[:, k, c]), x, first, last)
                        else:
                            mm = three(dst, (x[0][:, c], x[1][:, c]), (wh[:, k, :], wl[:, k, :]), first, last)
                mm.then_inc(S["w_used"], 1)
        pe.wait_ge(S["x_whole"], 1)
        pe.wait_ge(S["sw_loaded"], 32)
        for k in range(KT):
            mm = pe.matmul(PS[0:16, 4, 0:T], SW[:, k, 0:16], actT[:, k, :], start=(k == 0), stop=(k == KT - 1))
        mm.then_inc(S["low_rank"], 1)
        for t in range(TT):
            for k in range(KT):
                mm = pe.matmul(PS[:, 5, t * 24:t * 24 + 24], actT[:, k, t * P:(t + 1) * P], SW[:, k, 16:40],
                               start=(k == 0), stop=(k == KT - 1))
        mm.then_inc(S["low_rank"], 1)
        pe.wait_ge(S["side_copied"], 2)
        pe.wait_ge(S["gw2_loaded"], 16)
        for h in range(GH):
            mm = pe.matmul(PS[:, 6 + h // 2, h % 2 * T:(h % 2 + 1) * T], GW2[:, h * P:(h + 1) * P], LR, start=True, stop=True)
        mm.then_inc(S["low_rank"], 1)
        def gla_scores(n):
            lhs, rhs = (CV[:, 4:8, :], CV[:, 0:4, :]) if n == 0 else (WD[(n - 1) % 2],) * 2
            if n == 0:
                pe.wait_ge(S["silu_qk"], 1)
                pe.wait_ge(S["lb_in"], 1)
                pe.wait_ge(S["side_copied"], 3)
            else:
                pe.wait_ge(S["level_ready"], n)
            if n >= 4:
                pe.wait_ge(S["gsc_masked"], n - 3)
            for c in range(NCH):
                for h in range(GH):
                    at = (h * TT + c // 2) * C
                    mm = pe.matmul(PS[HALF[c % 2], 4 + n % 4, at:at + C], lhs[:, h, c * C:(c + 1) * C],
                                   rhs[:, h, c * C:(c + 1) * C], start=True, stop=True)
            mm.then_inc(S["gsc_ready"], 1)

        def gate_query(c, f, between=None):
            n = N_GOQ + c
            if f == 0:
                loaded(n)
                pe.wait_ge(S["groups_read"], 10 + c)
            for k in range(KT):
                mm = pe.matmul(half(n % 2)[:, f, :], slot(n % 2)[:, k, f * P:(f + 1) * P], actT[:, k, :],
                               start=(k == 0), stop=(k == KT - 1))
                if between and k % 4 == 3 and k < KT - 1:
                    between(k // 4)
            if f == 3:
                mm.then_inc(S["w_used"], 4)

        def v_turn(t):
            for m in range(8):
                mm = pe.transpose(PS[:, 4 + 2 * t + m // 4, m % 4 * P:(m % 4 + 1) * P], CV[:, 8 + m, t * P:(t + 1) * P], ident)
            mm.then_inc(S["gv_turned"], 1)

        def scan_step(c):
            t, hf = c // 2, HALF[c % 2]
            if c == 0:
                pe.wait_ge(S["gkv_copied"], 3)
                pe.wait_ge(S["gsc_summed"], len(GLA_HALF))
            else:
                pe.wait_ge(S["gs_step"], GH * c)
            if c == 2:
                pe.wait_ge(S["o_copied"], 1)
            for h in range(GH):
                o = PS[hf, 4 + h // 2, h % 2 * GDV:(h % 2 + 1) * GDV]
                if c:
                    pe.matmul(o, Q1[:, h, c * C:(c + 1) * C], GS[:, h, :], start=True, stop=False)
                mm = pe.matmul(o, SCT[hf, h, t, :], VTOK[hf, t, h * GDV:(h + 1) * GDV], start=(c == 0), stop=True)
            mm.then_inc(S["go_ready"], 1)
            if c < NCH - 1:
                for h in range(GH):
                    mm = pe.matmul(PS[:, 6 + h // 2, h % 2 * GDV:(h % 2 + 1) * GDV], KTOK[hf, t, h, :],
                                   VTOK[hf, t, h * GDV:(h + 1) * GDV], start=True, stop=True)
                mm.then_inc(S["gs_ready"], 1)

        for f in range(4):
            gate_query(0, f)
        for n in range(3):
            gla_scores(n)
        for f in range(3):
            gate_query(1, f)
        for n in (3, 4):
            gla_scores(n)
        gate_query(1, 3)
        for f in range(2):
            gate_query(2, f)
        for n in (5, 6):
            gla_scores(n)
        for f in (2, 3):
            gate_query(2, f)
        pe.wait_ge(S["gqk_ready"], 1)
        pe.wait_ge(S["gsc_masked"], len(GLA_HALF) + 1)
        for t in range(TT):
            for h in range(GH):
                mm = pe.transpose(PS[:, 6 + t, h * P:(h + 1) * P], K4[:, h, t * P:(t + 1) * P], ident)
        mm.then_inc(S["gk_turned"], 1)
        pe.wait_ge(S["gv_ready"], 1)
        v_turn(0)
        gate_query(3, 0)
        pe.wait_ge(S["gkv_copied"], 1)
        v_turn(1)
        cw = slot(N_CMP % 2).rearrange("p k n -> p (k n)").rearrange("p (s l h) -> p s l h", s=2, l=CB)

        def compress(i, ls):
            for l in ls:
                mm = pe.matmul(PS[:, 3, i * 31:(i + 1) * 31], cw[:, i, l, :], XC[i][:, l, :], start=(l == 0), stop=(l == CB - 1))
            return mm

        pe.wait_ge(S["pos_loaded"], 64)
        pe.wait_ge(S["groups_read"], 14)
        for i in range(2):
            mm = pe.transpose(PS[:, 2, i * CB:(i + 1) * CB], PTAB[i], ident[0:CB, 0:CB])
        mm.then_inc(S["side_turned"], 1)
        gate_query(3, 1)
        scan_step(0)
        loaded(N_CMP)
        pe.wait_ge(S["xc_ready"], 1)
        pe.wait_ge(S["side_copied"], 5)
        for f in (2, 3):
            gate_query(3, f, lambda q: compress(0, range(16 * (f - 2) + 5 * q, 16 * (f - 2) + 5 * q + 5)))
            compress(0, [16 * (f - 2) + 15])
            scan_step(f - 1)
        scan_step(NCH - 1)
        compress(1, range(CB // 2))
        pe.wait_ge(S["o_copied"], 2)
        pe.wait_ge(S["gs_step"], GH * (NCH - 1))
        for t in range(TT):
            pe.wait_ge(S["on_ready"], t + 1)
            for m in range(8):
                at = m % 2 * T + t * P
                mm = pe.transpose(PS[:, 4 + m // 2, at:at + P], OT[:, t, m * P:(m + 1) * P], ident)
        mm.then_inc(S["on_turned"], 1)
        pe.wait_ge(S["groups_read"], 15)
        pe.wait_ge(S["nsq_ready"], 1)
        for i in range(2):
            mm = pe.matmul(PS[:, i, :], con("ones"), SQ[:, 8 + 2 * i:10 + 2 * i, :].rearrange("p a b -> p (a b)"),
                           start=True, stop=True)
        mm.then_inc(S["k_sums"], 1)
        for t in range(TT):
            for h in range(NH):
                mm = pe.matmul(PS[:, 2, t * NH + h:t * NH + h + 1], SQ[:, h, t * P:(t + 1) * P], con("ones")[:, 0:1],
                               start=True, stop=True)
        mm.then_inc(S["k_sums"], 1)
        compress(1, range(CB // 2, CB)).then_inc(S["w_used"], 4)
        pe.wait_ge(S["hid_ready"], 2)
        pe.matmul(PS[:, 3, 0:2 * NB], CW2[0], HID[0], start=True, stop=True)
        for kv in range(KVH):
            mm = pe.matmul(PS[0:NB, 3, P + kv * DH:P + (kv + 1) * DH], HID[1][:, kv * NB:(kv + 1) * NB], CW2[1], start=True, stop=True)
        mm.then_inc(S["cmp_ready"], 1)
        pe.wait_ge(S["nk_ready"], 2)
        pe.wait_ge(S["on_read"], 1)
        for t in range(TT):
            nk = (t + 1) * P
            for s in range(2):
                for h in range(NH):
                    u = (t * 2 + s) * NH + h
                    if u >= 4:
                        pe.wait_ge(S["sc_read"], u - 3)
                    pe.matmul(PS[:, 4 + u % 4, 0:nk], GOQ[:, 8 + h, t * P:(t + 1) * P], NK[:, 4 + 2 * s + h // GRP, 0:nk],
                              start=True, stop=True).then_inc(S["sc_ready"], 1)
            if t == 0:
                pe.wait_ge(S["kc_squared"], 1)
                pe.matmul(PS[:, 2, 0:2 * NB], con("ones"), KCSQ, start=True, stop=True).then_inc(S["k_sums"], 1)
                pe.wait_ge(S["nk_ready"], 3)
            else:
                pe.wait_ge(S["cs_read"], 1)
            for h in range(NH):
                mm = pe.matmul(PS[:, 2, h * NB:(h + 1) * NB], GOQ[:, 8 + h, t * P:(t + 1) * P],
                               KCMP[:, h // GRP * NB:(h // GRP + 1) * NB], start=True, stop=True)
            mm.then_inc(S["cs_ready"], 1)
        pe.wait_ge(S["sc_read"], 32)
        pe.wait_ge(S["side_copied"], 6)
        g = 0
        for t in range(TT):
            for kv in range(KVH):
                o = PS[:, kv, :]
                if t:
                    pe.wait_ge(S["att_out"], kv + 1)
                parts = [(s, kt) for s in range(2) for kt in range(t + 1)] + [(2, 0)]
                for q, (s, kt) in enumerate(parts):
                    if g >= 4:
                        pe.wait_ge(S["pt_copied"], g - 3)
                    pe.wait_ge(S["prob_ready"], t * 3 + s + 1)
                    for j in range(GRP):
                        h = kv * GRP + j
                        if s == 2:
                            mm = pe.transpose(PS[0:NB, 4 + g % 4, j * P:(j + 1) * P], PCM[:, t, h, :], ident)
                        else:
                            mm = pe.transpose(PS[:, 4 + g % 4, j * P:(j + 1) * P], PSW[t][:, s, h, kt * P:(kt + 1) * P], ident)
                    mm.then_inc(S["pt_ready"], 1)
                    g += 1
                g -= len(parts)
                for q, (s, kt) in enumerate(parts):
                    pe.wait_ge(S["pt_copied"], g + 1)
                    if s == 2:
                        mm = pe.matmul(o, VCMP[:, kv, :], PTC[g % 4], start=False, stop=True)
                    else:
                        mm = pe.matmul(o, VSW[:, s, kt, kv * DH:(kv + 1) * DH], PTR[g % 4], start=(q == 0), stop=False)
                    mm.then_inc(S["pt_used"], 1)
                    g += 1

        pe.wait_ge(S["gla_low"], 1)
        pe.wait_ge(S["att_out"], TT * KVH)
        with pe.Fori(0, 2) as i:
            for j in range(2):
                pe.wait_ge(S["sum_step"], i * 2 + (SUM["out2"] + j - 1))
                split_tokens(N_OUT2 + j, pair[j], lambda k: XH2[:, k, :], lambda k: actT[:, k, :], i)
        norm("n5")

        def ffn2_part(n, groups, silus, sums, i=None, per=F2_N):
            def at(v, step):
                return v if i is None else i * step + v

            units = UNITS[groups]
            for m in range(groups):
                if m == 0:
                    pe.wait_ge(S["sum_step"], at(sums - 1, 4))
                else:
                    pe.wait_ge(S["ffn2_silu"], at(silus + m, F2_GROUPS))
                split_rows(n + 2 * m, 0, i, per, p="n5" if m == 0 else None)
                if m == 0:
                    pe.wait_ge(S["sum_step"], at(sums, 4))
                else:
                    pe.wait_ge(S["ffn2_mul"], at(silus + m, F2_GROUPS))
                split_rows(n + 2 * m + 1, 1, i, per)
            for g in range(4):
                if g < 2:
                    pe.wait_ge(S["ffn2_silu" if g == 0 else "ffn2_mul"], at(silus + groups, F2_GROUPS))
                else:
                    pe.wait_ge(S["sum_step"], at(sums + g - 1, 4))
                split_tokens(n + 2 * groups + g, pair[g % 2], lambda k: HTH[:, k, :], lambda k: HTL[:, k, :], i, per, units,
                             (lambda q: pe.wait_ge(S["ffn2_low"], at(silus + q + 1, F2_GROUPS))) if g == 0 else None)

        with pe.Fori(0, F2_PARTS) as i:
            ffn2_part(N_F2, F2_GROUPS, 0, SUM["ffn2"], i)
        ffn2_part(N_F2 + F2_PARTS * F2_N, F2_LAST, F2_PARTS * F2_GROUPS, SUM["ffn2"] + 4 * F2_PARTS)

    @block.scalar
    def _(act):
        steps = [0]

        def link(ins):
            steps[0] += 1
            ins.then_inc(S["act_step"], 1)
            act.wait_ge(S["act_step"], steps[0])

        def copy(dst, src, scale=1.0):
            return act.activation(dst, src, ACT.Copy, scale=scale)

        def square_sum(p):
            act.activation(XN[p][:, 0, :], xs[:, 0, :], ACT.Square, accum_out=ss[:, 0:1]).then_inc(S["norm_sum0"], 1)

        def root(p):
            act.wait_ge(S["norm_mean"], RMS[p])
            act.activation(sq, ms, ACT.Sqrt).then_inc(S["norm_root"], 1)

        def norm(p, gain):
            if p != "n1":
                square_sum(p)
                root(p)
            for j in range(0 if p in XSPLIT else 1, KT // 2, 1 if p in XSPLIT else 2):
                act.wait_ge(S["norm_turned"], KT // 2 * NORMS[p] + j + 1)
                for q in range(2):
                    k = 2 * j + q
                    dst = r32(XH[:, k, :]) if p in XSPLIT else actT[:, k, :]
                    ins = copy(dst, PS[:, 4 + j % 4, q * T:(q + 1) * T], col(gain, k))
                ins.then_inc(S["x_high" if p in XSPLIT else f"{p}_act"], 1)

        def high(n, js, i=None, per=2, units=UNITS[4], free=False):
            for j in js:
                if j % 2 == 0:
                    v = 16 * (n // 2 + 1)
                    act.wait_ge(S[f"w_loaded{2 * (n % 2) + j // 2}"], v if i is None else i * (8 * per) + v)
                if not free:
                    act.wait_ge(S["w_used"], used(n - 1, i, per, j + 1))
                copy(r32(HIW[j]), unit_at(n % 2, j)).then_inc(S["w_high"], counts(units, j))

        act.dma_start(xs[:, 0, :], xin[:, 0, :]).then_inc(S["x0_loaded"], 16)
        act.dma_start(xs[:, 1, :], xin[:, 1, :]).then_inc(S["x1_loaded"], 16)
        act.wait_ge(S["x0_loaded"], 16)
        square_sum("n1")
        root("n1")
        act.wait_ge(S["side_turned"], 1)
        copy(pcol[:], PS[:, 0, 0:2 * P]).then_inc(S["z_copied"], 1)
        act.wait_ge(S["z_copied"], 1)
        norm("n1", "attn_norm")
        act.wait_ge(S["n1_dve"], 4)
        act.wait_ge(S["n1_act"], 4)
        for h in range(2):
            copy(r32(XH1[:, 8 * h:8 * h + 8, :], True), actT[:, 8 * h:8 * h + 8, :]).then_inc(S["x1_high"], 1)

        def high1(n, *js):
            for j in js:
                if j % 2 == 0:
                    act.wait_ge(S[f"w_loaded{2 * (n % 2) + j // 2}"], 16 * (n // 2 + 1))
                if n > N_KRV or j >= 2:
                    act.wait_ge(S["w_used"], 4 * n + j - 1)
                copy(r32(HIW1[j % 2], True), unit_at(n % 2, j)).then_inc(S["in_high"], 1)

        high1(1, 0, 1)
        act.wait_ge(S["w_used"], used(N_WAG))
        copy(Z[:, 24:26, 1:ZW], half(0)[:, 0:2, :])
        copy(Z[0:32, 26, 1:ZW], half(0)[0:32, 2, :]).then_inc(S["z_copied"], 1)
        act.wait_ge(S["wag_shifted"], 1)
        act.activation(Z[LO, 24, 1:ZW], Z[LO, 24, 1:ZW], ACT.Tanh).then_inc(S["wa_ready"], 1)
        act.activation(Z[:, 25, 1:ZW], Z[:, 25, 1:ZW], ACT.Sigmoid)
        act.activation(Z[0:32, 26, 1:ZW], Z[0:32, 26, 1:ZW], ACT.Sigmoid).then_inc(S["wa_ready"], 1)
        def z_out(n):
            act.wait_ge(S["w_used"], used(n))
            at = (8, 12, 0, 4, 16, 20)[n - N_KRV]
            if n <= N_KRV + 3:
                ins = copy(by_half(Z[:, at:at + 4, 1:ZW]), out_rows(n % 2))
            else:
                ins = copy(Z[:, at:at + 4, 1:ZW], half(n % 2))
            ins.then_inc(S["z_copied"], 1)

        def head_sigmoids(dst, bias):
            for m in range(HM):
                ins = act.activation(dst[:, m, :], PS[:, 4 + m // 2, m % 2 * T:(m % 2 + 1) * T], ACT.Sigmoid, bias=col(bias, m))
            ins.then_inc(S["head_acts"], 1)

        banks4 = PS[:, 4:8, :].rearrange("p b n -> p (b n)")
        high1(1, 2, 3)
        high1(2, 0, 1)
        z_out(1)
        high1(2, 2, 3)
        high1(3, 0, 1)
        z_out(2)
        act.wait_ge(S["head_sums"], 1)
        head_sigmoids(lw, "w0")
        high1(3, 2, 3)
        high1(4, 0, 1)
        z_out(3)
        act.wait_ge(S["head_sums"], 2)
        act.activation(tmp1.rearrange("p m t -> p (m t)"), banks4, ACT.Sqrt).then_inc(S["head_acts"], 1)
        high1(4, 2, 3)
        act.wait_ge(S["lc_ready"], 1)
        link(act.activation(tmp2, lw, ACT.Exp, scale=KAPPA))
        act.activation(lw, lw, ACT.Exp, scale=-KAPPA).then_inc(S["head_acts"], 1)
        z_out(4)
        act.wait_ge(S["head_sums"], 3)
        head_sigmoids(ga, "a0")
        z_out(5)
        act.wait_ge(S["head_sums"], 4)
        act.wait_ge(S["ar_ready"], 1)
        copy(kk.rearrange("p m t -> p (m t)"), banks4).then_inc(S["head_acts"], 1)
        z_out(6)
        for g in range(2 * (NCH - 1)):
            c, m0 = g // 2, g % 2 * 4
            act.wait_ge(S["bk_turned"], g + 1)
            copy(BKtok(c)[:, m0:m0 + 4, :], PS[:, 4 + g % 4, :].rearrange("p (m j) -> p m j", m=4)).then_inc(S["bk_copied"], 1)

        def pool_in(q):
            act.wait_ge(S["w_used"], used(N_POOL + q // 4, unit=q % 4 + 1))
            copy(ZP[:, q, 16:PW], PS[:, pool_bank(q), 0:T]).then_inc(S["z_copied"], 1)

        pool_in(0)
        pool_in(1)
        for g in range(4):
            act.wait_ge(S["d_turned"], g + 1)
            copy(Di[:, 2 * g:2 * g + 2].rearrange("p m c j -> p (m c j)"), PS[:, g, :]).then_inc(S["d_ready"], 1)
        for q in range(2, 5):
            pool_in(q)
        for c in range(NCH):
            act.wait_ge(S["v_turned"], c + 1)
            for e in range(2):
                h = HALF[1 - e]
                ins = copy(UV(c)[h, :, e, :], PS[h, 4 + c, :].rearrange("p (m i) -> p m i", m=HM))
            ins.then_inc(S["v_placed"], 1)
        for c in range(NCH):
            act.wait_ge(S["u_ready"], c + 1)
            copy(UV(c)[LO, :, 0, :], PS[LO, 1, :].rearrange("p (m i) -> p m i", m=HM)).then_inc(S["u_placed0"], 1)
            if c < 3:
                pool_in(5 + c)
            if c < NCH - 1:
                act.wait_ge(S["sd_ready"], c + 1)
                copy(UV(c + 1)[LO, :, 0, :], SD[(c + 1) % 2][LO]).then_inc(S["s_placed0"], 1)
            if c % 2:
                t = c // 2
                act.wait_ge(S["y_ready"], c + 1)
                copy(Ytok[:, t, :].rearrange("p (m e i) -> p e m i", m=HM, e=2),
                     PS[:, 4 + 2 * t:6 + 2 * t, :].rearrange("p e (m i) -> p e m i", m=HM)).then_inc(S["y_copied"], 1)
        for t in range(TT):
            act.wait_ge(S["gn_var"], t + 1)
            act.activation(gns, gnv, ACT.Sqrt).then_inc(S["gn_root"], 1)
            if t == 0:
                high(N_OUT, (0, 1, 2), free=True)
        act.wait_ge(S["w_used"], used(N_SMALL, unit=2))
        for m in range(HM):
            copy(actT[:, m, :], PS[:, m // 2, m % 2 * T:(m % 2 + 1) * T], col("pool_scale", m)).then_inc(S["pool_out"], 1)
        act.wait_ge(S["pool_out"], HM)

        def mixer_high(h):
            copy(r32(XH[:, 8 * h:8 * h + 8, :]), actT[:, 8 * h:8 * h + 8, :]).then_inc(S["mixed_high"], 1)

        mixer_high(0)
        act.wait_ge(S["w_used"], used(N_SMALL))
        copy(GT.rearrange("p m t -> p (m t)"), banks4).then_inc(S["gate_copied"], 1)
        act.wait_ge(S["mixed"], 1)
        mixer_high(1)
        with act.Fori(0, 2) as i:
            for j in range(2):
                high(N_OUT + j, (3,), i)
                high(N_OUT + j + 1, (0, 1, 2), i)
        act.wait_ge(S["sum_step"], SUM["ffn1"])
        norm("n2", "mlp_norm")
        with act.Fori(0, F1_PARTS) as i:
            for c in range(8):
                n = N_F1 + c
                high(n, (3,), i, 8)
                high(n + 1, (0, 1, 2), i, 8)
                if c < 4:
                    act.wait_ge(S["w_used"], used(n, i, 8))
                    act.activation(by_half(RQ[c % 2]), out_rows(c % 2), ACT.Relu).then_inc(S["ffn1_relu"], 1)
        act.wait_ge(S["side_turned"], 2)
        copy(pT.rearrange("p k t -> p (k t)"), PS[:, 4, :]).then_inc(S["side_copied"], 1)
        act.wait_ge(S["sum_step"], SUM["gate"])
        norm("n3", "ple_norm")
        for c in range(4):
            n = N_GATE + c
            high(n, (3,))
            high(n + 1, (0, 1, 2))
            act.wait_ge(S["w_used"], used(n))
            if c >= 2:
                act.wait_ge(S["sum_step"], SUM["gate"] + c - 1)
            act.activation(gate_sb[c % 2], pair[c % 2], ACT.Sigmoid).then_inc(S["groups_read"], 1)
        act.wait_ge(S["sum_step"], SUM["out2"])
        square_sum("fin")
        root("fin")

        act.wait_ge(S["fin_done"], 2)
        norm("n4", "attn_norm_g_2")
        def high2(n, *js):
            for j in js:
                if j % 2 == 0:
                    act.wait_ge(S[f"w_loaded{2 * (n % 2) + j // 2}"], 16 * (n // 2 + 1))
                act.wait_ge(S["w_used"], 4 * n + j - 1)
                copy(r32(HIW[j % 2]), unit_at(n % 2, j)).then_inc(S["w_high"], 1)

        for c in range(4):
            n = N_GLA + c
            high(n, (3,))
            if c < 3:
                high(n + 1, (0, 1, 2))
            else:
                high(n + 1, (0, 1))
            act.wait_ge(S["w_used"], used(n))
            copy(by_half(ZG[:, 4 * c:4 * c + 4, 3:T + 3]), out_rows(c % 2)).then_inc(S["groups_read"], 1)
        for n in range(N_KCVC, N_GOQ):
            high2(n, 2, 3)
            if n + 1 < N_GOQ:
                high2(n + 1, 0, 1)
            act.wait_ge(S["w_used"], used(n))
            if n == N_KCVC:
                copy(by_half(NK[:, 0:4, :]), out_rows(n % 2)).then_inc(S["groups_read"], 1)
            else:
                s = n - N_KSVS
                copy(NK[:, 4 + 2 * s:6 + 2 * s, :], pair[n % 2][:, :, 0:T])
                copy(VSW[:, s], pair[n % 2][:, :, T:2 * T]).then_inc(S["groups_read"], 1)
        act.wait_ge(S["conv_done"], 1)
        act.activation(CV[:, 0:8, :], CV[:, 0:8, :], ACT.Silu).then_inc(S["silu_qk"], 1)
        act.wait_ge(S["low_rank"], 1)
        copy(LR, PS[0:16, 4, 0:T]).then_inc(S["side_copied"], 1)
        act.wait_ge(S["low_rank"], 2)
        act.activation(gates.rearrange("p t n -> p (t n)"), PS[:, 5, 0:48], ACT.Sigmoid).then_inc(S["side_copied"], 1)
        act.wait_ge(S["lb_in"], 1)
        link(act.activation(Q1, LB, ACT.Abs))
        link(act.activation(Q1, Q1, ACT.Exp, scale=-1.0))
        act.activation(Q1, Q1, ACT.Ln, bias=1.0).then_inc(S["la_soft"], 1)
        act.wait_ge(S["conv_done"], 2)
        act.activation(CV[:, 8:16, :], CV[:, 8:16, :], ACT.Silu).then_inc(S["gv_ready"], 1)
        act.wait_ge(S["gd_ready"], 1)
        lbc = LB.rearrange("p h (c j) -> p h c j", c=NCH)
        act.activation(GE[0], LB, ACT.Exp, scale=1 / GTAU)
        act.activation(GE[1], GE[1], ACT.Exp, scale=1 / GTAU)
        act.activation(GDEC, lbc[:, :, :, C - 1], ACT.Exp, scale=1 / GTAU).then_inc(S["gexp_ready"], 1)

        def level_exps(*levels):
            for n in levels:
                act.wait_ge(S["level_diff"], n + 1)
                act.activation(WD[n % 2], WD[n % 2], ACT.Exp, scale=1 / GTAU).then_inc(S["level_exp"], 1)

        level_exps(0, 1)
        def gate_query(c):
            act.wait_ge(S["w_used"], used(N_GOQ + c))
            copy(GOQ[:, 4 * c:4 * c + 4, :], half((N_GOQ + c) % 2)).then_inc(S["groups_read"], 1)

        gate_query(0)
        level_exps(2, 3)
        gate_query(1)
        level_exps(4, 5)
        act.wait_ge(S["groups_read"], 13)
        act.activation(GOQ[:, 0:8, :], GOQ[:, 0:8, :], ACT.Silu).then_inc(S["gout_ready"], 1)
        gate_query(2)

        def v_copy(t):
            act.wait_ge(S["gv_turned"], t + 1)
            copy(VTOK[:, t, :], PS[:, 4 + 2 * t:6 + 2 * t, :].rearrange("p b n -> p (b n)")).then_inc(S["gkv_copied"], 1)

        def o_copy(t):
            act.wait_ge(S["go_ready"], 2 * t + 2)
            copy(OT[:, t, :], PS[:, 4:6, :].rearrange("p b n -> p (b n)")).then_inc(S["o_copied"], 1)

        act.wait_ge(S["gk_turned"], 1)
        copy(KTOK.rearrange("p t h d -> p (t h d)"), PS[:, 6:8, :].rearrange("p b n -> p (b n)")).then_inc(S["gkv_copied"], 1)
        v_copy(0)
        v_copy(1)
        act.wait_ge(S["side_turned"], 3)
        for i in range(2):
            copy(XC[i][:, :, 30:31], PS[:, 2, i * CB:(i + 1) * CB].unsqueeze(2)).then_inc(S["side_copied"], 1)
        o_copy(0)
        gate_query(3)
        o_copy(1)
        for t in range(TT):
            act.wait_ge(S["gn_var"], TT + t + 1)
            act.activation(small[:, 32:36], small[:, 28:32], ACT.Sqrt).then_inc(S["gn_root"], 1)
        act.wait_ge(S["k_var"], 1)
        act.activation(RK, RK, ACT.Sqrt).then_inc(S["k_root"], 1)
        act.wait_ge(S["k_var"], 2)
        act.activation(QRS, QRS, ACT.Sqrt).then_inc(S["k_root"], 1)
        act.wait_ge(S["w_used"], used(N_CMP))
        for i in range(2):
            link(copy(HB[i][:, 0:1], PS[:, 3, i * 31 + 30:i * 31 + 31]))
            act.activation(HID[i], PS[:, 3, i * 31:i * 31 + 30], ACT.Silu, bias=HB[i][:, 0:1]).then_inc(S["hid_ready"], 1)
        act.wait_ge(S["cmp_ready"], 1)
        copy(VCMP.rearrange("p v d -> p (v d)"), PS[0:NB, 3, P:P + KVH * DH]).then_inc(S["side_copied"], 1)
        act.wait_ge(S["on_read"], 1)
        copy(r32(XH2[:, 0:8, :]), actT[:, 0:8, :]).then_inc(S["gla_high"], 1)
        act.wait_ge(S["k_var"], 3)
        act.activation(KCSQ, KCSQ, ACT.Sqrt).then_inc(S["k_root"], 1)
        for t in range(TT):
            for s in range(3):
                act.wait_ge(S["max_ready"], t * 3 + s + 1)
                for h in range(NH):
                    a = PCM[:, t, h, :] if s == 2 else PSW[t][:, s, h, :]
                    ins = act.activation(a, a, ACT.Exp, bias=MX[:, t, s, h:h + 1], accum_out=SM[:, t, s, h:h + 1])
                ins.then_inc(S["exp_done"], 1)
        def attention_high(t, kv):
            k = 8 + kv * GRP
            copy(r32(XH2[:, k:k + GRP, t * P:(t + 1) * P]), PS[:, kv, :].rearrange("p (h t) -> p h t", h=GRP))\
                .then_inc(S["att_high"], 1)

        for kv in range(KVH):
            act.wait_ge(S["pt_used"], 3 * (kv + 1))
            attention_high(0, kv)
        high(N_OUT2, (0, 1, 2))
        g = 3 * KVH
        for kv in range(KVH):
            for s, kt in [(s, kt) for s in range(2) for kt in range(TT)] + [(2, 0)]:
                act.wait_ge(S["pt_ready"], g + 1)
                act.wait_ge(S["pt_used"], g - 3)
                if s == 2:
                    ins = copy(PTC[g % 4], PS[0:NB, 4 + g % 4, :])
                else:
                    ins = copy(PTR[g % 4], PS[:, 4 + g % 4, :])
                ins.then_inc(S["pt_copied"], 1)
                g += 1
            act.wait_ge(S["pt_used"], g)
            attention_high(1, kv)
        with act.Fori(0, 2) as i:
            for j in range(2):
                high(N_OUT2 + j, (3,), i)
                high(N_OUT2 + j + 1, (0, 1, 2), i)
        act.wait_ge(S["sum_step"], SUM["ffn2"])
        norm("n5", "ffn_norm_g_2")

        def ffn2_part(n0, groups, i=None, last=False):
            plan = [UNITS[4]] * (2 * groups) + [UNITS[groups]] * 4 + [UNITS[4]]
            for c, (units, after) in enumerate(zip(plan, plan[1:])):
                n = n0 + c
                high(n, units[-1:], i, F2_N, units)
                if not (last and c == len(plan) - 2):
                    high(n + 1, after[:-1], i, F2_N, after)
                if c < 2 * groups and c % 2 == 0:
                    act.wait_ge(S["w_used"], used(n, i, F2_N))
                    act.activation(by_half(RQ[0]), out_rows(0), ACT.Silu).then_inc(S["ffn2_silu"], 1)

        with act.Fori(0, F2_PARTS) as i:
            ffn2_part(N_F2, F2_GROUPS, i)
        ffn2_part(N_F2 + F2_PARTS * F2_N, F2_LAST, last=True)

    @block.vector
    def _(v):
        steps = [0]

        def link(ins):
            steps[0] += 1
            ins.then_inc(S["dve_step"], 1)
            v.wait_ge(S["dve_step"], steps[0])

        def rms(p):
            link(v.tensor_tensor_reduce(out=XN[p][:, 1, :], in0=xs[:, 1, :], in1=xs[:, 1, :], scale=1.0, scalar=0.0,
                                        op0=ALU.mult, op1=ALU.add, accum_out=ss[:, 1:2]))
            v.wait_ge(S["norm_sum0"], RMS[p])
            v.tensor_scalar(ms, ss, 1.0 / D, EPS, ALU.mult, ALU.add).then_inc(S["norm_mean"], 1)
            v.wait_ge(S["norm_root"], RMS[p])
            link(v.reciprocal(rs, sq))

        def norm(p, gain, low_part=actT):
            rms(p)
            for t in range(TT):
                v.tensor_scalar(rms_diagonal(p)[:, t, :], ident, rs[:, t:t + 1], None, ALU.mult).then_inc(S["rms_placed"], 1)
            if p == "n1":
                v.wait_ge(S["z_copied"], 1)
            for j in range(0, KT // 2, 1 if p in XSPLIT else 2):
                if p in XSPLIT:
                    v.wait_ge(S["x_high"], XSPLIT[p] + j + 1)
                else:
                    v.wait_ge(S["norm_turned"], KT // 2 * NORMS[p] + j + 1)
                for q in range(2):
                    k = 2 * j + q
                    src = PS[:, 4 + j % 4, q * T:(q + 1) * T]
                    if p in XSPLIT:
                        ins = v.scalar_tensor_tensor(r32(low_part[:, k, :]), src, col(gain, k), high_of(XH[:, k, :]), ALU.mult, ALU.subtract)
                    else:
                        ins = v.tensor_scalar(actT[:, k, :], src, col(gain, k), None, ALU.mult)
                ins.then_inc(S["x_low" if p in XSPLIT else f"{p}_dve"], 1)

        def low(n, js, i=None, per=2, units=UNITS[4]):
            for j in js:
                v.wait_ge(S["w_high"], split_count(n, j, i, per) + (counts(units, j) - 1))
                u = unit_at(n % 2, j)
                v.tensor_tensor(r32(u), u, high_of(HIW[j]), ALU.subtract).then_inc(S["w_low"], counts(units, j))

        def add_out(w, g, at):
            v.wait_ge(S["w_used"], w)
            r = xs[:, :, at if isinstance(at, slice) else bass.ds(at, CW)]
            v.tensor_tensor(r, pair[g], r, ALU.add).then_inc(S["sum_step"], 1)

        v.wait_ge(S["x1_loaded"], 16)
        v.wait_ge(S["const_loaded"], 16)
        norm("n1", "attn_norm")
        for h in range(2):
            v.wait_ge(S["x1_high"], h + 1)
            x = slice(8 * h, 8 * h + 8)
            v.tensor_tensor(r32(XL1[h], True), actT[:, x, :], high_of(XH1[:, x, :], True), ALU.subtract).then_inc(S["x1_low"], 1)

        def low1(n, *js):
            for j in js:
                v.wait_ge(S["in_high"], 4 * (n - N_KRV) + j + 1)
                u = unit_at(n % 2, j)
                v.tensor_tensor(r32(u), u, high_of(HIW1[j % 2], True), ALU.subtract).then_inc(S["in_low"], 1)

        low1(1, 0, 1)
        mu = COL["mu_shift"]
        v.wait_ge(S["zeroed"], 2)
        v.wait_ge(S["z_copied"], 2)
        v.tensor_tensor(DIF[:, 0:2, :], Z[:, 24:26, 0:T], Z[:, 24:26, 1:ZW], ALU.subtract)
        link(v.tensor_tensor(DIF[0:32, 2, :], Z[0:32, 26, 0:T], Z[0:32, 26, 1:ZW], ALU.subtract))
        for q, n in ((0, P), (1, P), (2, 32)):
            z = Z[0:n, 24 + q, 1:ZW]
            ins = v.scalar_tensor_tensor(z, DIF[0:n, q, :], pcol[0:n, mu + 24 + q:mu + 25 + q], z, ALU.mult, ALU.add)
        ins.then_inc(S["wag_shifted"], 1)
        v.wait_ge(S["wag_shifted"], 1)

        def shift(q, dif):
            link(v.tensor_tensor(dif, Z[:, 8 * q:8 * q + 8, 0:T], Z[:, 8 * q:8 * q + 8, 1:ZW], ALU.subtract))
            for m in range(HM):
                z = Z[:, 8 * q + m, 1:ZW]
                ins = v.scalar_tensor_tensor(z, dif[:, m, :], pcol[:, mu + 8 * q + m:mu + 8 * q + m + 1], z, ALU.mult, ALU.add)
            return ins

        low1(1, 2, 3)
        low1(2, 0, 1, 2, 3)
        low1(3, 0, 1)
        v.wait_ge(S["z_copied"], 4)
        link(shift(1, DIF))
        for m in range(HM):
            ins = v.tensor_scalar(kk[:, m, :], zk[:, m, :], col("k_k", m), None, ALU.mult)
        link(ins)
        low1(3, 2)
        v.tensor_tensor(tmp2, kk, kk, ALU.mult).then_inc(S["kk_squared"], 1)
        low1(3, 3)
        low1(4, 0, 1)
        v.wait_ge(S["head_acts"], 1)
        for m in range(HM):
            ins = v.tensor_tensor_scan(lw[:, m, :], con("keep"), lw[:, m, :], 0.0, ALU.mult, ALU.add)
        ins.then_inc(S["lc_ready"], 1)
        low1(4, 2, 3)
        v.wait_ge(S["head_acts"], 2)
        link(v.tensor_scalar(tmp1, tmp1, 1e-12, None, ALU.max))
        link(v.reciprocal(tmp1, tmp1))
        link(v.tensor_tensor(kk, kk, tmp1, ALU.mult))
        v.wait_ge(S["head_acts"], 3)
        lwc, kkc = (a.rearrange("p m (c j) -> p (m c) j", c=NCH) for a in (lw, kk))
        arf = AR.rearrange("p m c j -> p (m c) j")
        v.tensor_copy(PEND.rearrange("p m c -> p (m c)"), lwc[:, :, C - 1])
        v.wait_ge(S["z_copied"], 6)
        v.tensor_scalar(arf[:, :, 0:1], kkc[:, :, 0:1], -1.0, None, ALU.mult)
        v.scalar_tensor_tensor(arf[:, :, 1:C], lwc[:, :, 0:C - 1], -1.0, kkc[:, :, 1:C], ALU.mult, ALU.mult)
        link(shift(0, DIF))
        v.wait_ge(S["head_acts"], 4)
        for m in range(HM):
            ins = v.tensor_scalar(tmp1[:, m, :], ga[:, m, :], 1.0, col("k_a", m), ALU.subtract, ALU.mult)
        link(ins)
        link(v.scalar_tensor_tensor(zk, tmp1, 1.0, zk, ALU.add, ALU.mult))
        v.tensor_tensor(ga, kk, ga, ALU.mult)
        for m in range(HM):
            ins = v.scalar_tensor_tensor(tmp1[:, m, :], zr[:, m, :], col("r_k", m), zk[:, m, :], ALU.mult, ALU.mult)
        ins.then_inc(S["rkr_ready"], 1)
        v.wait_ge(S["rkr_ready"], 1)

        def chunks(a):
            return a.rearrange("p m (c j) -> p m c j", c=NCH)

        v.tensor_tensor(AR[:, :, :, C:P], chunks(zr), chunks(lw), ALU.mult).then_inc(S["ar_ready"], 1)
        for e in range(2):
            h = HALF[e]
            v.tensor_tensor(BK[h, :, :, e * C:(e + 1) * C], chunks(ga)[h], chunks(tmp2)[h], ALU.mult)
            ins = v.tensor_tensor(BK[h, :, :, (1 - e) * C:(2 - e) * C], chunks(zk)[h], chunks(tmp2)[h], ALU.mult)
        ins.then_inc(S["bk_ready"], 1)
        v.wait_ge(S["bk_ready"], 1)
        v.wait_ge(S["z_copied"], 8)
        v.wait_ge(S["zeroed"], 3)
        shift(2, tmp2).then_inc(S["v_ready"], 1)
        v.wait_ge(S["v_ready"], 1)
        for g in range(2 * HM):
            m, e = g // 2, g % 2
            v.wait_ge(S["score_ready"], g + 1)
            v.tensor_tensor(G[:, m, e], PS[:, g % 4, :].rearrange("p (c j) -> p c j", c=NCH), over(tri, NCH), ALU.mult)\
                .then_inc(S["score_masked"], 1)
        v.wait_ge(S["score_masked"], 2 * HM)
        for e in range(2):
            h = HALF[e]
            l1 = con("level1")[h].unsqueeze(1).unsqueeze(1).broadcast_to([C, HM, NCH, C])
            ins = v.tensor_tensor(DTi[h], G[h, :, e, :, 0:C], l1, ALU.mult)
        link(ins)
        dtf = DTi.rearrange("p m c j -> p (m c) j")
        v.tensor_tensor(dtf, dtf, over(eye64, HM * NCH), ALU.add).then_inc(S["dt_ready"], 1)
        v.wait_ge(S["dt_ready"], 1)

        def eight(a, g):
            return a[:, 2 * g:2 * g + 2].rearrange("p m c j -> p (m c) j")

        def bank8(b):
            return PS[:, b, :].rearrange("p (q j) -> p q j", q=8)

        v.wait_ge(S["bonus_done"], 1)
        for lv in range(len(LEVELS)):
            mask = con("levels")[:, lv * C:(lv + 1) * C]
            for g in range(4):
                v.wait_ge(S["f_ready"], 4 * lv + g + 1)
                v.tensor_tensor(eight(Fi, g), bank8(g), over(mask, 8), ALU.mult).then_inc(S["f_masked"], 1)
            for g in range(4):
                if lv < len(LEVELS) - 1:
                    v.wait_ge(S["df_ready"], 4 * lv + g + 1)
                    v.tensor_tensor(eight(Di, g), bank8(4 + g % 2), eight(Di, g), ALU.add).then_inc(S["d_added"], 1)
                v.wait_ge(S["dft_ready"], 4 * lv + g + 1)
                v.tensor_tensor(eight(DTi, g), bank8(g), eight(DTi, g), ALU.add).then_inc(S["dt_added"], 1)
        v.memset(SD[0], 0.0)
        for e in range(2):
            v.memset(UV(0)[HALF[e], :, e, :], 0.0).then_inc(S[f"s_placed{e}"], 1)
        for e in range(2):
            h = HALF[e]
            v.tensor_copy(G[h, :, e, :, 0:C], AR[h, :, :, 0:C]).then_inc(S["at_placed"], 1)
        for c in range(NCH):
            v.wait_ge(S["zc_ready"], c + 1)
            v.tensor_copy(ZSB.rearrange("p m i -> p (m i)"), PS[:, 0, :]).then_inc(S["zc_copied"], 1)
            v.wait_ge(S["u_ready"], c + 1)
            v.tensor_copy(UV(c)[HI, :, 1, :], PS[HI, 1, :].rearrange("p (m i) -> p m i", m=HM)).then_inc(S["u_placed1"], 1)
            if c < NCH - 1:
                v.wait_ge(S["s_ready"], c + 1)
                now, then = SD[c % 2], SD[(c + 1) % 2]
                link(v.tensor_tensor(then, PS[:, 2, :].rearrange("p (m i) -> p m i", m=HM), now, ALU.add))
                v.tensor_tensor(then, then, along(PEND[:, :, c], C), ALU.mult).then_inc(S["sd_ready"], 1)
                v.wait_ge(S["sd_ready"], c + 1)
                v.tensor_copy(UV(c + 1)[HI, :, 1, :], then[HI]).then_inc(S["s_placed1"], 1)
        gsq = area(B, 16, C)
        for t in range(TT):
            v.wait_ge(S["y_copied"], t + 1)
            if t == 0:
                v.wait_ge(S["y_ready"], NCH)
            y = Ytok[:, t, :].rearrange("p (h i) -> p h i", h=16)
            link(v.tensor_reduce(gnm, y, AX, ALU.add))
            link(v.tensor_scalar(gnm, gnm, 1.0 / C, None, ALU.mult))
            link(v.tensor_tensor(y, y, along(gnm, C), ALU.subtract))
            link(v.tensor_tensor(gsq, y, y, ALU.mult))
            link(v.tensor_reduce(gnv, gsq, AX, ALU.add))
            v.tensor_scalar(gnv, gnv, 1.0 / C, GN_EPS, ALU.mult, ALU.add).then_inc(S["gn_var"], 1)
            v.wait_ge(S["gn_root"], t + 1)
            link(v.reciprocal(gns, gns))
            v.tensor_tensor(y, y, along(gns, C), ALU.mult).then_inc(S["yn_ready"], 1)
        def mixer_low(h):
            v.wait_ge(S["mixed_high"], h + 1)
            x = actT[:, 8 * h:8 * h + 8, :]
            v.tensor_tensor(r32(x), x, high_of(XH[:, 8 * h:8 * h + 8, :]), ALU.subtract).then_inc(S["sum_step"], 1)

        low(N_OUT, (0,))
        mixer_low(0)
        low(N_OUT, (1,))
        v.wait_ge(S["yn_turned"], 1)
        for m in range(HM):
            ins = v.scalar_tensor_tensor(actT[:, 8 + m, :], PS[:, 4 + m // 2, m % 2 * T:(m % 2 + 1) * T], col("gn_g", m),
                                         bonus[:, m, :], ALU.mult, ALU.add)
        link(ins)
        v.wait_ge(S["gate_copied"], 1)
        v.tensor_tensor(actT[:, 8:16, :], actT[:, 8:16, :], GT, ALU.mult).then_inc(S["mixed"], 1)

        low(N_OUT, (2,))
        mixer_low(1)
        v.wait_ge(S["x_loaded"], 16)
        with v.Fori(0, 2) as i:
            for j in range(2):
                low(N_OUT + j, (3,), i)
                low(N_OUT + j + 1, (0, 1, 2), i)
                add_out(used(N_OUT + j, i), j, i * (2 * CW) + j * CW)
        v.wait_ge(S["sum_step"], SUM["ffn1"])
        norm("n2", "mlp_norm")
        with v.Fori(0, F1_PARTS) as i:
            for c in range(8):
                n = N_F1 + c
                low(n, (3,), i, 8)
                if 1 <= c <= 4:
                    v.wait_ge(S["ffn1_high"], i * 4 + c)
                    tiles = slice(4 * (c - 1), 4 * c)
                    v.tensor_tensor(r32(HTL[:, tiles]), RQ[(c - 1) % 2], high_of(HTH[:, tiles]), ALU.subtract).then_inc(S["ffn1_low"], 1)
                low(n + 1, (0, 1, 2), i, 8)
                if c >= 4:
                    add_out(used(n, i, 8), c % 2, slice(CW * (c - 4), CW * (c - 3)))
        v.wait_ge(S["sum_step"], SUM["gate"])
        norm("n3", "ple_norm")
        for c in range(4):
            n, g, r = N_GATE + c, gate_sb[c % 2], xs[:, :, CW * c:CW * (c + 1)]
            low(n, (3,))
            low(n + 1, (0, 1, 2))
            v.wait_ge(S["groups_read"], c + 1)
            v.wait_ge(S["proj_ready"], c + 1)
            link(v.tensor_tensor(g, PS[:, 4 + c % 2 * 2:6 + c % 2 * 2, :], g, ALU.mult))
            v.tensor_tensor(r, r, g, ALU.add).then_inc(S["sum_step"], 1)
        v.wait_ge(S["sum_step"], SUM["out2"])
        rms("fin")
        v.wait_ge(S["fing_loaded"], 16)
        for t in range(TT):
            v.scalar_tensor_tensor(xs[:, t, :], xs[:, t, :], rs[:, t:t + 1], fing, ALU.mult, ALU.mult).then_inc(S["fin_done"], 1)

        v.wait_ge(S["fin_done"], 2)
        norm("n4", "attn_norm_g_2", XL_IN2)
        for c in range(4):
            n = N_GLA + c
            low(n, (3,))
            if c < 3:
                low(n + 1, (0, 1, 2))

        def low2(n, *js):
            for j in js:
                v.wait_ge(S["w_high"], split_count(n, j))
                u = unit_at(n % 2, j)
                v.tensor_tensor(r32(u), u, high_of(HIW[j % 2]), ALU.subtract).then_inc(S["w_low"], 1)

        def conv(m0):
            for w in range(4):
                for m in range(m0, m0 + 4):
                    tap, x = col("gla_conv_w_2", 16 * w + m), ZG[:, m, w:w + T]
                    if w == 0:
                        ins = v.tensor_scalar(CV[:, m, :], x, tap, None, ALU.mult)
                    else:
                        ins = v.scalar_tensor_tensor(CV[:, m, :], x, tap, CV[:, m, :], ALU.mult, ALU.add)
                if w < 3:
                    link(ins)
            return ins

        low2(N_KCVC, 0, 1)
        v.wait_ge(S["zeroed"], 4)
        v.wait_ge(S["groups_read"], 6)
        conv(0)
        low2(N_KCVC, 2)
        low2(N_KCVC, 3)
        conv(4).then_inc(S["conv_done"], 1)
        low2(N_KSVS, 0, 1)
        v.wait_ge(S["groups_read"], 8)
        conv(8)
        low2(N_KSVS, 2, 3)
        conv(12).then_inc(S["conv_done"], 1)
        low2(N_KWVW, 0, 1, 2, 3)
        v.wait_ge(S["low_rank"], 3)
        for h in range(GH):
            ins = v.tensor_scalar(LB[:, h, :], PS[:, 6 + h // 2, h % 2 * T:(h % 2 + 1) * T], col("gla_gate_b_2", h), None, ALU.add)
        ins.then_inc(S["lb_in"], 1)
        v.wait_ge(S["la_soft"], 1)
        link(v.scalar_tensor_tensor(LB, LB, 0.0, Q1, ALU.min, ALU.subtract))
        for h in range(GH):
            ins = v.tensor_tensor_scan(LB[:, h, :], con("keep"), LB[:, h, :], 0.0, ALU.mult, ALU.add)
        link(ins)
        v.wait_ge(S["conv_done"], 2)
        lbf = LB.rearrange("p h (c j) -> p (h c) j", c=NCH)
        v.tensor_tensor(GE[1].rearrange("p h (c j) -> p (h c) j", c=NCH), along(lbf[:, :, C - 1], C), lbf, ALU.subtract)\
            .then_inc(S["gd_ready"], 1)

        def halves(a, w, e):
            return a.rearrange("p h (n e w) -> p (h n) e w", e=2, w=w)[:, :, e, :]

        def level_diff(n):
            w = GLA_HALF[n]
            first = halves(LB, w, 0)
            ref = along(first[:, :, w - 1], w)
            v.tensor_tensor(halves(WD[n % 2], w, 0), ref, first, ALU.subtract)
            v.tensor_tensor(halves(WD[n % 2], w, 1), halves(LB, w, 1), ref, ALU.subtract).then_inc(S["level_diff"], 1)

        def level_product(n):
            w, d = GLA_HALF[n], WD[n % 2]
            v.wait_ge(S["level_exp"], n + 1)
            v.tensor_tensor(halves(d, w, 0), halves(d, w, 0), halves(CV[:, 4:8, :], w, 0), ALU.mult)
            v.tensor_tensor(halves(d, w, 1), halves(d, w, 1), halves(CV[:, 0:4, :], w, 1), ALU.mult)\
                .then_inc(S["level_ready"], 1)

        def add_scores(n):
            v.wait_ge(S["gsc_ready"], n + 1)
            sc = SCT.rearrange("p h t j -> p (h t) j")
            tmp = SCTMP.rearrange("p (q j) -> p q j", q=8)
            mask = over(glamask[:, (n - 1) % (len(GLA_HALF) + 1), :], 8)
            v.tensor_tensor(tmp if n else sc, bank8(4 + n % 4), mask, ALU.mult).then_inc(S["gsc_masked"], 1)
            v.wait_ge(S["gsc_masked"], n + 1)
            if n:
                v.tensor_tensor(sc, sc, tmp, ALU.add).then_inc(S["gsc_summed"], 1)
                v.wait_ge(S["gsc_summed"], n)

        level_diff(0)
        level_diff(1)
        v.wait_ge(S["silu_qk"], 1)
        level_product(0)
        level_product(1)
        v.wait_ge(S["gexp_ready"], 1)
        v.scalar_tensor_tensor(Q1, CV[:, 0:4, :], GDK ** -0.5, GE[0], ALU.mult, ALU.mult)
        v.tensor_tensor(K4, CV[:, 4:8, :], GE[1], ALU.mult).then_inc(S["gqk_ready"], 1)
        v.wait_ge(S["glamask_loaded"], 16)
        add_scores(0)
        for n in range(0, len(GLA_HALF), 2):
            add_scores(n + 1)
            add_scores(n + 2)
            if n + 2 < len(GLA_HALF):
                for q in (n + 2, n + 3):
                    level_diff(q)
                for q in (n + 2, n + 3):
                    level_product(q)
        for c in range(NCH - 1):
            v.wait_ge(S["go_ready"], c + 1)
            v.wait_ge(S["gs_ready"], c + 1)
            for h in range(GH):
                src = PS[:, 6 + h // 2, h % 2 * GDV:(h % 2 + 1) * GDV]
                if c == 0:
                    v.tensor_copy(GS[:, h, :], src).then_inc(S["gs_step"], 1)
                else:
                    v.scalar_tensor_tensor(GS[:, h, :], GS[:, h, :], GDEC[:, h, c:c + 1], src, ALU.mult, ALU.add)\
                        .then_inc(S["gs_step"], 1)
            v.wait_ge(S["gs_step"], GH * (c + 1))
        om, ov, osq = small[:, 24:28], small[:, 28:32], small[:, 32:36]
        oj = area(GC + 2048, GH, GDV)
        for t in range(TT):
            v.wait_ge(S["o_copied"], t + 1)
            o = OT[:, t, :].rearrange("p (h e) -> p h e", h=GH)
            link(v.tensor_tensor(oj, o, o, ALU.mult))
            link(v.tensor_reduce(om, oj, AX, ALU.add))
            v.tensor_scalar(ov, om, 1.0 / GDV, EPS, ALU.mult, ALU.add).then_inc(S["gn_var"], 1)
            v.wait_ge(S["gn_root"], TT + t + 1)
            link(v.reciprocal(osq, osq))
            v.tensor_tensor(o, o, along(osq, GDV), ALU.mult).then_inc(S["on_ready"], 1)
        v.wait_ge(S["on_turned"], 1)
        v.wait_ge(S["gout_ready"], 1)
        for m in range(8):
            ins = v.scalar_tensor_tensor(actT[:, m, :], PS[:, 4 + m // 2, m % 2 * T:(m % 2 + 1) * T], col("gla_norm_g_2", m % 2),
                                         GOQ[:, m, :], ALU.mult, ALU.mult)
        ins.then_inc(S["on_read"], 1)
        qg = COL["nsa_q_norm_g_2"]
        link(v.tensor_scalar(QKG, pcol[:, qg + 1:qg + 4], pcol[:, qg:qg + 1], None, ALU.mult))
        v.wait_ge(S["k_sums"], 1)
        for i in range(2):
            ins = v.tensor_scalar(RK[:, i], PS[:, i, :], 1.0 / DH, EPS, ALU.mult, ALU.add)
        ins.then_inc(S["k_var"], 1)
        v.wait_ge(S["k_root"], 1)
        v.reciprocal(RK, RK)
        v.wait_ge(S["k_sums"], 2)
        v.tensor_scalar(QRS.rearrange("p t h -> p (t h)"), PS[:, 2, 0:TT * NH], 1.0 / DH, EPS, ALU.mult, ALU.add)\
            .then_inc(S["k_var"], 1)
        v.wait_ge(S["k_root"], 2)
        link(v.reciprocal(QRS, QRS))
        link(v.tensor_scalar(QRS, QRS, DH ** -0.5, None, ALU.mult))
        for s in range(2):
            k = NK[:, 4 + 2 * s:6 + 2 * s, :].rearrange("p a t -> p (a t)")
            v.scalar_tensor_tensor(k, k, QKG[:, 1 + s:2 + s], RK[:, s], ALU.mult, ALU.mult).then_inc(S["nk_ready"], 1)
        v.wait_ge(S["side_copied"], 6)
        link(v.tensor_copy(KCMP, PS[:, 3, 0:2 * NB]))
        v.tensor_tensor(KCSQ, KCMP, KCMP, ALU.mult).then_inc(S["kc_squared"], 1)

        def probs(t, s):
            a = PCM[:, t] if s == 2 else PSW[t][:, s]
            v.wait_ge(S["exp_done"], t * 3 + s + 1)
            link(v.reciprocal(WT[:, t, s, :], SM[:, t, s, :]))
            gate = gates[:, t, :].rearrange("p (h j) -> p j h", j=3)[:, (s + 1) % 3, :]
            link(v.tensor_tensor(WT[:, t, s, :], WT[:, t, s, :], gate, ALU.mult))
            if s == 2:
                link(v.tensor_tensor(a, a, over(con("cmpseen")[:, t * NB:(t + 1) * NB], NH), ALU.mult))
            v.tensor_tensor(a, a, along(WT[:, t, s, :], a.shape[2]), ALU.mult).then_inc(S["prob_ready"], 1)

        for t in range(TT):
            nk = (t + 1) * P
            for s in range(2):
                for h in range(NH):
                    u = (t * 2 + s) * NH + h
                    v.wait_ge(S["sc_ready"], u + 1)
                    v.scalar_tensor_tensor(PSW[t][:, s, h, :], PS[:, 4 + u % 4, 0:nk], QRS[:, t, h:h + 1],
                                           con("causal")[:, 2 * P - nk:2 * P] if t else con("causal")[:, P:2 * P],
                                           ALU.mult, ALU.add).then_inc(S["sc_read"], 1)
            if t == 0:
                v.wait_ge(S["k_sums"], 3)
                v.tensor_scalar(KCSQ, PS[:, 2, 0:2 * NB], 1.0 / DH, EPS, ALU.mult, ALU.add).then_inc(S["k_var"], 1)
                v.wait_ge(S["k_root"], 3)
                link(v.reciprocal(KCSQ, KCSQ))
                v.scalar_tensor_tensor(KCMP, KCMP, QKG[:, 0:1], KCSQ, ALU.mult, ALU.mult).then_inc(S["nk_ready"], 1)
            v.wait_ge(S["cs_ready"], t + 1)
            v.tensor_tensor(PCM[:, t], PS[:, 2, 0:NH * NB].rearrange("p (h n) -> p h n", h=NH), along(QRS[:, t, :], NB), ALU.mult)\
                .then_inc(S["cs_read"], 1)
            v.wait_ge(S["cs_read"], t + 1)
            link(v.tensor_tensor(PCM[:, t], PCM[:, t], over(con("cmpbias")[:, t * NB:(t + 1) * NB], NH), ALU.add))
            v.wait_ge(S["sc_read"], (t + 1) * 2 * NH)
            for s in range(3):
                link(v.tensor_reduce(MX[:, t, s, :], PCM[:, t] if s == 2 else PSW[t][:, s], AX, ALU.max))
                v.tensor_scalar(MX[:, t, s, :], MX[:, t, s, :], -1.0, None, ALU.mult).then_inc(S["max_ready"], 1)
                if t:
                    probs(0, s)
        for g in range(3 * KVH):
            v.wait_ge(S["pt_ready"], g + 1)
            if g >= 4:
                v.wait_ge(S["pt_used"], g - 3)
            if g % 3 == 2:
                ins = v.tensor_copy(PTC[g % 4], PS[0:NB, 4 + g % 4, :])
            else:
                ins = v.tensor_copy(PTR[g % 4], PS[:, 4 + g % 4, :])
            ins.then_inc(S["pt_copied"], 1)

        def attention_low(t, kv):
            v.wait_ge(S["att_high"], t * KVH + kv + 1)
            k = 8 + kv * GRP
            v.tensor_tensor(r32(actT[:, k:k + GRP, t * P:(t + 1) * P]), PS[:, kv, :].rearrange("p (h t) -> p h t", h=GRP),
                            high_of(XH2[:, k:k + GRP, t * P:(t + 1) * P]), ALU.subtract).then_inc(S["att_out"], 1)

        for s in range(3):
            probs(1, s)
            if s < KVH:
                attention_low(0, s)
        low(N_OUT2, (0, 1, 2))
        v.wait_ge(S["gla_high"], 1)
        v.tensor_tensor(r32(actT[:, 0:8, :]), actT[:, 0:8, :], high_of(XH2[:, 0:8, :]), ALU.subtract).then_inc(S["gla_low"], 1)
        for kv in range(KVH):
            attention_low(1, kv)
        with v.Fori(0, 2) as i:
            for j in range(2):
                low(N_OUT2 + j, (3,), i)
                low(N_OUT2 + j + 1, (0, 1, 2), i)
                add_out(used(N_OUT2 + j, i), j, i * (2 * CW) + j * CW)
        v.wait_ge(S["sum_step"], SUM["ffn2"])
        norm("n5", "ffn_norm_g_2")

        def ffn2_part(n0, groups, muls, i=None, last=False):
            def at(x):
                return x if i is None else i * F2_GROUPS + x

            plan = [UNITS[4]] * (2 * groups) + [UNITS[groups]] * 4 + [UNITS[4]]
            for c, (units, after) in enumerate(zip(plan, plan[1:])):
                n = n0 + c
                low(n, units[-1:], i, F2_N, units)
                if c % 2 == 0 and 2 <= c <= 2 * groups:
                    m = c // 2 - 1
                    v.wait_ge(S["ffn2_high"], at(muls + m + 1))
                    tiles = slice(4 * m, 4 * m + 4)
                    v.tensor_tensor(r32(HTL[:, tiles]), RQ[1], high_of(HTH[:, tiles]), ALU.subtract).then_inc(S["ffn2_low"], 1)
                if not (last and c == len(plan) - 2):
                    low(n + 1, after[:-1], i, F2_N, after)
                if c < 2 * groups and c % 2:
                    v.wait_ge(S["w_used"], used(n, i, F2_N))
                    v.wait_ge(S["ffn2_silu"], at(muls + c // 2 + 1))
                    v.tensor_tensor(by_half(RQ[1]), out_rows(1), by_half(RQ[0]), ALU.mult).then_inc(S["ffn2_mul"], 1)
                elif c >= 2 * groups:
                    g = c - 2 * groups
                    add_out(used(n, i, F2_N), g % 2, slice(CW * g, CW * (g + 1)))

        with v.Fori(0, F2_PARTS) as i:
            ffn2_part(N_F2, F2_GROUPS, 0, i)
        ffn2_part(N_F2 + F2_PARTS * F2_N, F2_LAST, F2_PARTS * F2_GROUPS, last=True)

    @block.gpsimd
    def _(pool):
        steps = [0]

        def link(ins):
            steps[0] += 1
            ins.then_inc(S["pool_step"], 1)
            pool.wait_ge(S["pool_step"], steps[0])

        pool.memset(prow, 0.0).then_inc(S["zeroed"], 1)
        pool.memset(Z[:, 24:27, 0:1], 0.0)
        pool.memset(Z[:, 0:16, 0:1], 0.0).then_inc(S["zeroed"], 1)
        pool.wait_ge(S["w_used"], used(N_KRV + 3))
        pool.memset(Z[:, 16:24, 0:1], 0.0).then_inc(S["zeroed"], 1)
        for b in PB:
            pool.memset(b[:, 0:16], 0.0)
        link(pool.memset(ZP[:, :, 0:16], 0.0))
        pool.wait_ge(S["const_loaded"], 16)
        pool.wait_ge(S["v_ready"], 1)
        pool.wait_ge(S["head_acts"], 5)
        link(pool.tensor_tensor(bonus, kk, zv, ALU.mult))
        for m in range(HM):
            ins = pool.tensor_scalar(bonus[:, m, :], bonus[:, m, :], col("gn_b", m), None, ALU.add)
        ins.then_inc(S["bonus_done"], 1)
        for m in range(HM):
            pool.wait_ge(S["z_copied"], 9 + m)
            g = m // 2
            src = ZP[:, m, :]
            for k in range(g + 1):
                dst = PB[k % 2]
                link(pool.tensor_tensor(dst[:, 16:PW], src[:, 16:PW], src[:, 16 - 2 ** k:PW - 2 ** k], ALU.add))
                src = dst
            pool.tensor_tensor(src[:, 16:32], src[:, 16:32], con("invcnt")[:, 16 * g:16 * g + 16], ALU.mult)
            link(pool.tensor_scalar(src[:, 32:PW], src[:, 32:PW], 0.5 ** (g + 1), None, ALU.mult))
            link(pool.tensor_tensor(ZP[:, m, 16:PW], src[:, 16:PW], ZP[:, m, 16:PW], ALU.subtract))
        pool.tensor_copy(PB[0][:, 0:1], PB[1][:, 0:1]).then_inc(S["pool_ready"], 1)
        pool.wait_ge(S["sum_step"], 2)
        pool.dma_start(ptok, inp["p"][0, 0].rearrange("(t p) d -> p t d", p=P)).then_inc(S["ptok_loaded"], 16)
        pool.dma_start(GW2, W["gla_gate_w2_2"]).then_inc(S["gw2_loaded"], 16)
        with pool.Fori(0, F1_PARTS) as i:
            for c in range(4):
                pool.wait_ge(S["ffn1_relu"], i * 4 + (c + 1))
                r = RQ[c % 2]
                pool.tensor_tensor(r32(HTH[:, 4 * c:4 * c + 4]), r, r, ALU.mult)
                pool.tensor_tensor(r, r, r, ALU.mult).then_inc(S["ffn1_high"], 1)
        pool.wait_ge(S["w_used"], used(N_GATE - 1))
        pool.dma_start(pproj, W["w_ple_proj"].rearrange("(k p) n -> p k n", p=P)).then_inc(S["pproj_loaded"], 16)
        pool.dma_start(fing, inp["final_norm"].unsqueeze(0).broadcast_to([P, D])).then_inc(S["fing_loaded"], 16)
        pool.wait_ge(S["proj_ready"], 4)
        pool.dma_start(SW[:, :, 0:16], wcols("w_in_2", 2048, 16)).then_inc(S["sw_loaded"], 16)
        pool.dma_start(SW[:, :, 16:40], wcols("w_in_2", 5648, 24)).then_inc(S["sw_loaded"], 16)
        pool.wait_ge(S["fin_done"], 2)
        pool.memset(ZG[:, :, 0:3], 0.0).then_inc(S["zeroed"], 1)
        pool.wait_ge(S["x_low"], XSPLIT["n4"] + 8)
        pool.tensor_tensor(actT[:], high_of(XH), high_of(XL_IN2), ALU.add).then_inc(S["x_whole"], 1)
        pool.wait_ge(S["conv_done"], 2)
        pool.dma_start(glamask.rearrange("p n j -> p (n j)"), consts[:, GLAMASK_AT:]).then_inc(S["glamask_loaded"], 16)
        pool.wait_ge(S["gqk_ready"], 1)
        pool.wait_ge(S["gsc_summed"], len(GLA_HALF))
        for i, n in enumerate(("k", "v")):
            pool.dma_start(PTAB[i], W[f"cmp_{n}_pos_2"]).then_inc(S["pos_loaded"], 16)
            pool.dma_start(CW2[i], W[f"cmp_{n}_w2_2"]).then_inc(S["pos_loaded"], 16)
        pool.wait_ge(S["groups_read"], 9)
        for i in range(2):
            for kv in range(KVH):
                for l in range(2):
                    ins = pool.tensor_copy(XC[i][:, CST * l:CST * (l + 1), kv * NB:(kv + 1) * NB],
                                           NK[:, 2 * i + kv, CST * l:CST * (l + NB)].rearrange("p (n l) -> p l n", l=CST))
        ins.then_inc(S["xc_ready"], 1)
        pool.wait_ge(S["xc_ready"], 1)
        pool.wait_ge(S["groups_read"], 15)
        pool.wait_ge(S["go_ready"], NCH)
        pool.tensor_tensor(SQ[:, 0:8, :], GOQ[:, 8:16, :], GOQ[:, 8:16, :], ALU.mult)
        pool.tensor_tensor(SQ[:, 8:12, :], NK[:, 4:8, :], NK[:, 4:8, :], ALU.mult).then_inc(S["nsq_ready"], 1)
        one = con("ones")[:, 0:1].unsqueeze(2).broadcast_to([P, 4, T])
        with pool.Fori(0, F2_PARTS) as i:
            for m in range(F2_GROUPS):
                pool.wait_ge(S["ffn2_mul"], i * F2_GROUPS + (m + 1))
                pool.tensor_tensor(r32(HTH[:, 4 * m:4 * m + 4]), RQ[1], one, ALU.mult).then_inc(S["ffn2_high"], 1)
        for m in range(F2_LAST):
            pool.wait_ge(S["ffn2_mul"], F2_PARTS * F2_GROUPS + m + 1)
            pool.tensor_tensor(r32(HTH[:, 4 * m:4 * m + 4]), RQ[1], one, ALU.mult).then_inc(S["ffn2_high"], 1)

    ctx.close()

INPUTS = ["x", "p", "attn_norm", "w_in", "mu_shift", "pool_w", "pool_scale", "w0", "w_up", "a0", "a_up", "g_up",
          "k_k", "k_a", "r_k", "gn_g", "gn_b", "w_out", "mlp_norm", "w_ffn_up", "w_ffn_down", "ple_norm",
          "w_ple_gate", "w_ple_proj", "final_norm", "attn_norm_g_2", "w_in_2", "gla_conv_w_2", "gla_gate_w2_2",
          "gla_gate_b_2", "gla_norm_g_2", "nsa_q_norm_g_2", "nsa_kc_norm_g_2", "nsa_ks_norm_g_2",
          "nsa_kw_norm_g_2", "cmp_k_pos_2", "cmp_k_w1_2", "cmp_k_w2_2", "cmp_v_pos_2", "cmp_v_w1_2",
          "cmp_v_w2_2", "w_out_2", "ffn_norm_g_2", "w_gate_2", "w_up_2", "w_down_2"]


def kernel(**inputs):
    import concourse.bacc as bacc
    from concourse.bass_utils import run_bass_kernel_spmd

    nc = bacc.Bacc("TRN2", target_bir_lowering=False, num_devices=1)
    arrays, aps = {}, {}
    for name in INPUTS:
        a = np.ascontiguousarray(inputs[name])
        arrays[f"in_{name}"] = a
        aps[name] = nc.dram_tensor(f"in_{name}", a.shape, mybir.dt.from_np(a.dtype), kind="ExternalInput").ap()
    arrays["in_constants"] = pack_constants()
    consts = nc.dram_tensor("in_constants", arrays["in_constants"].shape, F32, kind="ExternalInput").ap()
    out = nc.dram_tensor("out_y", (1, T, D), F32, kind="ExternalOutput").ap()
    build(nc, aps, consts, out)
    r = run_bass_kernel_spmd(nc, [arrays], core_ids=[0])
    return r.results[0]["out_y"]
```
